# Optimizing a Trainium2 kernel written in Bass

```python
import math
import jax, jax.numpy as jnp
from jax import lax
import numpy as np

D_MODEL = 1024
BATCH = 1
SEQ = 512
DEPTH = 1
DEC_BATCH = 1
DEC_SEQ = 64
PAST_LEN = 512

CHUNK = 64
Q_BLOCK = 128
EPS = 1e-6
GLA_HEADS = 4
GLA_DK = 32
GLA_DV = 64
GLA_GATE_RANK = 16
GLA_TAU = 16.0
POOL_WINDOWS = (2, 4, 8, 16)
POOL_GROUP = 64
POOL_WIDTH = 256
POOL_HIST = 15
DIFF_HEADS = 4
DIFF_DH = 64
DIFF_DV = 128
MEM_LEN = 256
MEM_HEADS = 4
MEM_DH = 128
N_GROUPS = 4
EXPERTS_PER_GROUP = 4
N_EXPERTS = 16
TOP_K = 2
EXPERT_HIDDEN = 512

GLA_QK = GLA_HEADS * GLA_DK
GLA_V = GLA_HEADS * GLA_DV
DIFF_QK = DIFF_HEADS * 2 * DIFF_DH
DIFF_V = DIFF_HEADS * DIFF_DV
MIX_WIDTH = GLA_V + POOL_WIDTH + DIFF_V
IN_SIZES = (GLA_QK, GLA_QK, GLA_V, GLA_V, GLA_GATE_RANK, POOL_WIDTH, DIFF_QK, DIFF_QK, DIFF_V)
IN_WIDTH = 2 * GLA_QK + 2 * GLA_V + GLA_GATE_RANK + POOL_WIDTH + 2 * DIFF_QK + DIFF_V

kernel_name = 'hybrid_stream_encoder_step'

def rmsnorm(x, g):
    xf = x.astype(jnp.float32)
    y = xf * lax.rsqrt(jnp.mean(xf * xf, axis=-1, keepdims=True) + EPS)
    return (y * g.astype(jnp.float32)).astype(x.dtype)

def gla_recurrence(q, k, v, log_a, s0):
    B, L, H, DK = q.shape
    DV = v.shape[-1]
    C = min(CHUNK, L)
    n = L // C
    causal = jnp.tril(jnp.ones((C, C), dtype=bool))

    def to_chunks(t):
        return t.reshape(B, n, C, H, t.shape[-1]).swapaxes(0, 1)

    def step(s, inp):
        qc, kc, vc, ac = inp
        b = jnp.cumsum(ac, axis=1)
        rel = b[:, :, None] - b[:, None, :]
        decay = jnp.exp(jnp.where(causal[None, :, :, None, None], rel, -jnp.inf))
        att = jnp.einsum('bthk,btshk,bshk->bhts', qc, decay, kc)
        o = (jnp.einsum('bhts,bshv->bthv', att, vc)
             + jnp.einsum('bthk,bhkv->bthv', qc * jnp.exp(b), s))
        b_end = b[:, -1]
        s_new = (jnp.exp(b_end)[..., None] * s
                 + jnp.einsum('bshk,bshv->bhkv', kc * jnp.exp(b_end[:, None] - b), vc))
        return s_new, o

    s_fin, o = lax.scan(step, s0, (to_chunks(q), to_chunks(k), to_chunks(v), to_chunks(log_a)))
    return o.swapaxes(0, 1).reshape(B, L, H, DV), s_fin

def pool_mixer(u, hist, pos0, w_pool, scale):
    B, L, _ = u.shape
    ext = jnp.concatenate([hist.astype(u.dtype), u], axis=1)
    cs = jnp.cumsum(ext.astype(jnp.float32), axis=1)
    cs = jnp.concatenate([jnp.zeros((B, 1, POOL_WIDTH), jnp.float32), cs], axis=1)
    pos = pos0 + jnp.arange(L)
    outs = []
    for gi, w in enumerate(POOL_WINDOWS):
        lo, hi = gi * POOL_GROUP, (gi + 1) * POOL_GROUP
        win_sum = (cs[:, POOL_HIST + 1:POOL_HIST + 1 + L, lo:hi]
                   - cs[:, POOL_HIST + 1 - w:POOL_HIST + 1 - w + L, lo:hi])
        cnt = jnp.minimum(w, pos + 1).astype(jnp.float32)[None, :, None]
        m = win_sum / cnt - u[..., lo:hi].astype(jnp.float32)
        outs.append(m @ w_pool[gi].astype(jnp.float32))
    out = jnp.concatenate(outs, axis=-1) * scale.astype(jnp.float32)
    return out, ext[:, -POOL_HIST:]

def diff_attention(q, k, v, q_pos, k_pos, lam):
    B, Lq, H, _, DH = q.shape
    DV = v.shape[-1]
    scale = DH ** -0.5
    k_chunk = k_pos // CHUNK

    def attend(qb, qpb):
        s = jnp.einsum('bqhmd,bkhmd->bhmqk', qb, k).astype(jnp.float32) * scale
        mask = k_chunk[None, :] <= (qpb // CHUNK)[:, None]
        s = jnp.where(mask[None, None, None], s, -jnp.inf)
        p = jax.nn.softmax(s, axis=-1)
        pd = p[:, :, 0] - lam * p[:, :, 1]
        return jnp.einsum('bhqk,bkhv->bqhv', pd.astype(v.dtype), v)

    if Lq > Q_BLOCK:
        nb = Lq // Q_BLOCK
        qb = q.reshape(B, nb, Q_BLOCK, H, 2, DH).swapaxes(0, 1)
        ob = lax.map(lambda a: attend(a[0], a[1]), (qb, q_pos.reshape(nb, Q_BLOCK)))
        return ob.swapaxes(0, 1).reshape(B, Lq, H, DV)
    return attend(q, q_pos)

def memory_kv(mem, g, w_kv):
    B, M, _ = mem.shape
    kv = rmsnorm(mem, g) @ w_kv
    mk, mv = jnp.split(kv, 2, axis=-1)
    return mk.reshape(B, M, MEM_HEADS, MEM_DH), mv.reshape(B, M, MEM_HEADS, MEM_DH)

def memory_attend(h, mk, mv, w_q, w_o):
    B, L, _ = h.shape
    q = (h @ w_q).reshape(B, L, MEM_HEADS, MEM_DH)
    s = jnp.einsum('bqhd,bkhd->bhqk', q, mk.astype(q.dtype)).astype(jnp.float32) * MEM_DH ** -0.5
    p = jax.nn.softmax(s, axis=-1)
    o = jnp.einsum('bhqk,bkhd->bqhd', p.astype(mv.dtype), mv).reshape(B, L, MEM_HEADS * MEM_DH)
    return (o.astype(h.dtype) @ w_o).astype(h.dtype)

def hier_moe(h, w_rg, b_rg, w_re, b_re, w_g, w_u, w_d):
    B, L, D = h.shape
    t = h.reshape(B * L, D)
    T = t.shape[0]
    g_prob = jax.nn.softmax((t @ w_rg).astype(jnp.float32) + b_rg.astype(jnp.float32), axis=-1)
    g_top = jnp.argmax(g_prob, axis=-1)
    g_onehot = jax.nn.one_hot(g_top, N_GROUPS, dtype=jnp.float32)
    g_w = jnp.sum(g_prob * g_onehot, axis=-1, keepdims=True)
    e_logit = ((t @ w_re).astype(jnp.float32) + b_re.astype(jnp.float32)).reshape(T, N_GROUPS, EXPERTS_PER_GROUP)
    e_in = jnp.sum(e_logit * g_onehot[:, :, None], axis=1)
    top_v, top_i = lax.top_k(jax.nn.softmax(e_in, axis=-1), TOP_K)
    top_v = top_v / jnp.sum(top_v, axis=-1, keepdims=True)
    within = jnp.sum(jax.nn.one_hot(top_i, EXPERTS_PER_GROUP, dtype=jnp.float32) * top_v[..., None], axis=1)
    gate = (g_onehot[:, :, None] * (g_w * within)[:, None, :]).reshape(T, N_EXPERTS)
    out = jnp.zeros((T, D), jnp.float32)
    for e in range(N_EXPERTS):
        y = (jax.nn.silu(t @ w_g[e]) * (t @ w_u[e])) @ w_d[e]
        out = out + gate[:, e:e + 1] * y.astype(jnp.float32)
    return out.reshape(B, L, D).astype(h.dtype)

def layer(p, lam_init, x, gla_s0, pool_hist, k_past, v_past, mk, mv):
    B, L, _ = x.shape
    P = 0 if k_past is None else k_past.shape[1]
    h = rmsnorm(x, p['norm_mix_g'])
    z = h @ p['w_in']
    idx = np.cumsum(IN_SIZES)[:-1].tolist()
    gq, gk, gv, gr, ga, pu, dq, dk, dv = jnp.split(z, idx, axis=-1)

    q = gq.reshape(B, L, GLA_HEADS, GLA_DK).astype(jnp.float32) * GLA_DK ** -0.5
    k = gk.reshape(B, L, GLA_HEADS, GLA_DK).astype(jnp.float32)
    v = gv.reshape(B, L, GLA_HEADS, GLA_DV).astype(jnp.float32)
    log_a = jax.nn.log_sigmoid((ga @ p['w_gla_a2']).astype(jnp.float32)
                               + p['b_gla_a'].astype(jnp.float32)) / GLA_TAU
    o_gla, gla_s = gla_recurrence(q, k, v, log_a.reshape(B, L, GLA_HEADS, GLA_DK), gla_s0.astype(jnp.float32))
    o_gla = rmsnorm(o_gla, p['gla_norm_g']).reshape(B, L, GLA_V) * jax.nn.silu(gr.astype(jnp.float32))

    o_pool, pool_buf = pool_mixer(pu, pool_hist, P, p['pool_w'], p['pool_scale'])

    dq5 = dq.reshape(B, L, DIFF_HEADS, 2, DIFF_DH)
    k_new = dk.reshape(B, L, DIFF_HEADS, 2 * DIFF_DH)
    v_new = dv.reshape(B, L, DIFF_HEADS, DIFF_DV)
    if k_past is None:
        k_all, v_all = k_new, v_new
    else:
        k_all = jnp.concatenate([k_past.astype(k_new.dtype), k_new], axis=1)
        v_all = jnp.concatenate([v_past.astype(v_new.dtype), v_new], axis=1)
    lam = (jnp.exp(jnp.sum(p['lambda_q1'].astype(jnp.float32) * p['lambda_k1'].astype(jnp.float32)))
           - jnp.exp(jnp.sum(p['lambda_q2'].astype(jnp.float32) * p['lambda_k2'].astype(jnp.float32)))
           + lam_init)
    o_diff = diff_attention(dq5, k_all.reshape(B, P + L, DIFF_HEADS, 2, DIFF_DH), v_all,
                            P + jnp.arange(L), jnp.arange(P + L), lam)
    o_diff = rmsnorm(o_diff, p['diff_norm_g']) * (1.0 - lam_init)

    mix = jnp.concatenate([o_gla.astype(h.dtype), o_pool.astype(h.dtype),
                           o_diff.reshape(B, L, DIFF_V).astype(h.dtype)], axis=-1)
    x = x + (mix @ p['w_out']).astype(x.dtype)
    x = x + memory_attend(rmsnorm(x, p['norm_mem_g']), mk, mv, p['w_mem_q'], p['w_mem_o'])
    x = x + hier_moe(rmsnorm(x, p['norm_ffn_g']), p['w_router_group'], p['b_router_group'],
                     p['w_router_expert'], p['b_router_expert'],
                     p['w_exp_gate'], p['w_exp_up'], p['w_exp_down'])
    return x, gla_s, pool_buf, k_new, v_new

def setup_inputs(seed: int = 0) -> dict:
    key = jax.random.key(seed)
    ks = jax.random.split(key, 40)

    def nrm(i, shape, scale):
        return scale * jax.random.normal(ks[i], shape, jnp.float32)

    def gain(i, shape):
        return 1.0 + nrm(i, shape, 0.02)

    return {
        'x_prompt': nrm(0, (BATCH, SEQ, D_MODEL), 1.0),
        'x_sample': nrm(1, (DEC_BATCH, DEC_SEQ, D_MODEL), 1.0),
        'mem_prompt': nrm(2, (BATCH, MEM_LEN, D_MODEL), 1.0),
        'cache_diff_k': nrm(3, (DEPTH, DEC_BATCH, PAST_LEN, DIFF_HEADS, 2 * DIFF_DH), 1.0),
        'cache_diff_v': nrm(4, (DEPTH, DEC_BATCH, PAST_LEN, DIFF_HEADS, DIFF_DV), 1.0),
        'cache_mem_k': nrm(5, (DEPTH, DEC_BATCH, MEM_LEN, MEM_HEADS, MEM_DH), 1.0),
        'cache_mem_v': nrm(6, (DEPTH, DEC_BATCH, MEM_LEN, MEM_HEADS, MEM_DH), 1.0),
        'state_gla': nrm(7, (DEPTH, DEC_BATCH, GLA_HEADS, GLA_DK, GLA_DV), 0.5),
        'state_pool': nrm(8, (DEPTH, DEC_BATCH, POOL_HIST, POOL_WIDTH), 1.0),
        'norm_mix_g': gain(9, (DEPTH, D_MODEL)),
        'w_in': nrm(10, (DEPTH, D_MODEL, IN_WIDTH), D_MODEL ** -0.5),
        'w_gla_a2': nrm(11, (DEPTH, GLA_GATE_RANK, GLA_QK), GLA_GATE_RANK ** -0.5),
        'b_gla_a': nrm(12, (DEPTH, GLA_QK), 0.1),
        'gla_norm_g': gain(13, (DEPTH, GLA_DV)),
        'pool_w': nrm(14, (DEPTH, len(POOL_WINDOWS), POOL_GROUP, POOL_GROUP), POOL_GROUP ** -0.5),
        'pool_scale': gain(15, (DEPTH, POOL_WIDTH)),
        'lambda_q1': nrm(16, (DEPTH, DIFF_DH), 0.1),
        'lambda_k1': nrm(17, (DEPTH, DIFF_DH), 0.1),
        'lambda_q2': nrm(18, (DEPTH, DIFF_DH), 0.1),
        'lambda_k2': nrm(19, (DEPTH, DIFF_DH), 0.1),
        'diff_norm_g': gain(20, (DEPTH, DIFF_DV)),
        'w_out': nrm(21, (DEPTH, MIX_WIDTH, D_MODEL), MIX_WIDTH ** -0.5),
        'norm_mem_g': gain(22, (DEPTH, D_MODEL)),
        'mem_norm_g': gain(23, (DEPTH, D_MODEL)),
        'w_mem_q': nrm(24, (DEPTH, D_MODEL, MEM_HEADS * MEM_DH), D_MODEL ** -0.5),
        'w_mem_kv': nrm(25, (DEPTH, D_MODEL, 2 * MEM_HEADS * MEM_DH), D_MODEL ** -0.5),
        'w_mem_o': nrm(26, (DEPTH, MEM_HEADS * MEM_DH, D_MODEL), (MEM_HEADS * MEM_DH) ** -0.5),
        'norm_ffn_g': gain(27, (DEPTH, D_MODEL)),
        'w_router_group': nrm(28, (DEPTH, D_MODEL, N_GROUPS), D_MODEL ** -0.5),
        'b_router_group': nrm(29, (DEPTH, N_GROUPS), 0.01),
        'w_router_expert': nrm(30, (DEPTH, D_MODEL, N_EXPERTS), D_MODEL ** -0.5),
        'b_router_expert': nrm(31, (DEPTH, N_EXPERTS), 0.01),
        'w_exp_gate': nrm(32, (DEPTH, N_EXPERTS, D_MODEL, EXPERT_HIDDEN), D_MODEL ** -0.5),
        'w_exp_up': nrm(33, (DEPTH, N_EXPERTS, D_MODEL, EXPERT_HIDDEN), D_MODEL ** -0.5),
        'w_exp_down': nrm(34, (DEPTH, N_EXPERTS, EXPERT_HIDDEN, D_MODEL), EXPERT_HIDDEN ** -0.5),
        'final_norm_g': gain(35, (D_MODEL,)),
    }

def reference(x_prompt, x_sample, mem_prompt, cache_diff_k, cache_diff_v, cache_mem_k, cache_mem_v,
              state_gla, state_pool, norm_mix_g, w_in, w_gla_a2, b_gla_a, gla_norm_g, pool_w, pool_scale,
              lambda_q1, lambda_k1, lambda_q2, lambda_k2, diff_norm_g, w_out, norm_mem_g, mem_norm_g,
              w_mem_q, w_mem_kv, w_mem_o, norm_ffn_g, w_router_group, b_router_group,
              w_router_expert, b_router_expert, w_exp_gate, w_exp_up, w_exp_down, final_norm_g):
    xp, xs = x_prompt, x_sample
    bp = x_prompt.shape[0]
    dk_p, dv_p, mk_p, mv_p, gs_p, ps_p = [], [], [], [], [], []
    dk_s, dv_s, gs_s, ps_s = [], [], [], []
    for l in range(DEPTH):
        p = dict(norm_mix_g=norm_mix_g[l], w_in=w_in[l], w_gla_a2=w_gla_a2[l], b_gla_a=b_gla_a[l],
                 gla_norm_g=gla_norm_g[l], pool_w=pool_w[l], pool_scale=pool_scale[l],
                 lambda_q1=lambda_q1[l], lambda_k1=lambda_k1[l], lambda_q2=lambda_q2[l],
                 lambda_k2=lambda_k2[l], diff_norm_g=diff_norm_g[l], w_out=w_out[l],
                 norm_mem_g=norm_mem_g[l], w_mem_q=w_mem_q[l], w_mem_o=w_mem_o[l],
                 norm_ffn_g=norm_ffn_g[l], w_router_group=w_router_group[l],
                 b_router_group=b_router_group[l], w_router_expert=w_router_expert[l],
                 b_router_expert=b_router_expert[l], w_exp_gate=w_exp_gate[l],
                 w_exp_up=w_exp_up[l], w_exp_down=w_exp_down[l])
        lam_init = 0.8 - 0.6 * math.exp(-0.3 * l)
        mk, mv = memory_kv(mem_prompt, mem_norm_g[l], w_mem_kv[l])
        xp, g_new, pool_new, k_new, v_new = layer(
            p, lam_init, xp, jnp.zeros((bp, GLA_HEADS, GLA_DK, GLA_DV), jnp.float32),
            jnp.zeros((bp, POOL_HIST, POOL_WIDTH), xp.dtype), None, None, mk, mv)
        dk_p.append(k_new); dv_p.append(v_new); mk_p.append(mk); mv_p.append(mv)
        gs_p.append(g_new); ps_p.append(pool_new)
        xs, g_new, pool_new, k_new, v_new = layer(
            p, lam_init, xs, state_gla[l], state_pool[l], cache_diff_k[l], cache_diff_v[l],
            cache_mem_k[l], cache_mem_v[l])
        dk_s.append(k_new); dv_s.append(v_new); gs_s.append(g_new); ps_s.append(pool_new)
    y_prompt = rmsnorm(xp, final_norm_g)
    y_sample = rmsnorm(xs, final_norm_g)
    return (y_prompt, y_sample,
            jnp.stack(dk_p), jnp.stack(dv_p), jnp.stack(mk_p), jnp.stack(mv_p),
            jnp.stack(gs_p), jnp.stack(ps_p),
            jnp.stack(dk_s), jnp.stack(dv_s), jnp.stack(gs_s), jnp.stack(ps_s))


_drawn_inputs = setup_inputs


def setup_inputs(seed=0):
    import zlib

    import numpy as np

    out = dict(_drawn_inputs(seed))
    spreads = {}
    factors = {'gla_norm_g': 4.231,
     'pool_scale': 3.717,
     'diff_norm_g': 3.202,
     'norm_mem_g': 8.0,
     'mem_norm_g': 2.904,
     'b_router_expert': 28.766,
     'final_norm_g': 8.638,
     'norm_ffn_g': 5.368,
     'b_router_group': 4.838}
    for name, (base, spread) in spreads.items():
        noise = np.random.default_rng([zlib.crc32(name.encode()), seed]).standard_normal(out[name].shape)
        drawn = base * np.exp(spread * noise) if base else spread * noise
        out[name] = __import__('jax').numpy.asarray(drawn.astype(out[name].dtype))
    for name, factor in factors.items():
        out[name] = (out[name] * factor).astype(out[name].dtype)
    return out
```

```python
from contextlib import ExitStack

import concourse.bass as bass
from concourse import mybir

F32 = mybir.dt.float32
F32R = mybir.dt.float32r
BF16 = mybir.dt.bfloat16
I32 = mybir.dt.int32
ALU = mybir.AluOpType
ACT = mybir.ActivationFunctionType
AX = mybir.AxisListType

P = 128
D = 1024
KB = D // P
SEQ, DEC, PAST, MEM = 512, 64, 512, 256
TOK = SEQ + DEC
TILES = 5
ROWS = [P, P, P, P, DEC]
CH = 64
NCH = TOK // CH
GH, GK, GV = 4, 32, 64
DH, DV, HEADS = 64, 128, 4
MH = 4
POOL_WINDOWS = (2, 4, 8, 16)
HIST = 15
EPS = 1e-6
LAM_INIT = 0.2
GROUPS, PER, E = 4, 4, 16
HID = 512
EXP_CLAMP = 40.0
UNIT = 4 * 512
RING = 6
WR = 4
MAX_EXTRA = 8
SLOT_ROWS = P * (E + MAX_EXTRA)
C_G, C_R, C_U, C_Q, C_K, C_V = 0, 512, 784, 1040, 1552, 2064

IN_BLOCKS = [("G", C_G, 512), ("R", C_R, 272), ("U", C_U, 256), ("K", C_K, 512), ("V", C_V, 512), ("Q", C_Q, 512)]


def dense_units():
    units = [("w_mem_kv", r, c, 512) for c in (0, 512) for r in (0, 512)]
    units += [("w_in", r, c, w) for _, c, w in IN_BLOCKS for r in (0, 512)]
    units += [("w_out", r, c, 512) for c in (0, 512) for r in (0, 512)]
    units += [("w_mem_q", r, 0, 512) for r in (0, 512)]
    units += [("w_mem_o", 0, c, 512) for c in (0, 512)]
    return units


def numbered(plan):
    seen, out = {"A": 0, "V": 0}, {}
    for n, (key, who) in enumerate(plan):
        out[key] = (n, who, seen[who])
        seen[who] += 1
    return out


def projection_plan():
    plan = [((b, i), "A") for b in ("memk", "memv") for i in range(2)]
    plan += [((b, t), "A") for b, _, _ in IN_BLOCKS for t in range(TILES)]
    plan += [(("gla_o", t), "V") for t in range(TILES)]
    plan += [((b, k), "A") for k in range(2) for b in ("pool", "pool_s")]
    plan += [(("diff_o", t), "V") for t in range(TILES)]
    plan += [(("w_out", c, t), "V") for c in range(2) for t in range(TILES)]
    plan += [(("mem_q", 0), "A")]
    for t in range(TILES):
        plan += [(("mem_q", t + 1), "A")] if t + 1 < TILES else []
        plan += [(("mem_o", t), "A")]
    plan += [(("w_mem_o", c, t), "V") for c in range(2) for t in range(TILES)]
    plan += [(("router",), "V"), (("pos",), "V")]
    return plan


def key_blocks(t):
    return t + 1 if t < 4 else 5


def transpose_plan():
    plan = [(("mem", i, g), "V") for i in range(2) for g in range(2)]
    plan += [(("mk", i), "A") for i in range(2)]
    plan += [(("x", t, g), "V") for t in range(TILES) for g in range(2)]
    plan += [(("G", t), "V") for t in range(TILES)]
    plan += [(("R", g), "A") for g in range(2)]
    plan += [(("U", t), "A") for t in range(TILES)] + [(("hist",), "A")]
    plan += [(("K", t), "A") for t in range(TILES)]
    plan += [(("kend", g), "V") for g in range(2)]
    plan += [(("Q", t), "A") for t in range(TILES)]
    plan += [(("mix_g", t), "A") for t in range(TILES)] + [(("kp", b), "A") for b in range(4)]
    for t in range(TILES):
        for h in range(HEADS):
            plan += [(("pd", t, h, 0), "A" if h % 2 else "V")] + ([(("pd", t, h, 1), "A")] if t == 4 else [])
            plan += [(("mix_d", t - 1), "A")] if h == 0 and t else []
    plan += [(("mix_d", TILES - 1), "A")]
    plan += [(("x1", t, g), "V") for t in range(TILES) for g in range(2)]
    plan += [(("mq", 0), "V")]
    for t in range(TILES):
        plan += [(("mq", t + 1), "V")] if t + 1 < TILES else []
        plan += [(("cmk", b), "A") for b in range(2)] if t == 3 else []
        plan += [(("pm", t, 0), "A"), (("pm", t, 1), "V")]
    plan += [(("x2", t, g), "AV"[g]) for t in range(TILES) for g in range(2)]
    return plan


def score_plan():
    plan = [(("gate",), "V")] + [(("kv", g), "V") for g in range(3)]
    plan += [(("att", t), "V") for t in range(TILES)]
    plan += [(("diff", t, h), "A") for t in range(4) for h in range(HEADS)]
    plan += [(("diff", 4, h, m), "A") for h in range(HEADS) for m in (1, 0)]
    plan += [(("mem", t), "A") for t in range(TILES)]
    return plan


DENSE = dense_units()
NDENSE = len(DENSE)
assert NDENSE % RING == 0
PJ, TR, SC = numbered(projection_plan()), numbered(transpose_plan()), numbered(score_plan())
NMOE = 6 * E
STEPS = [(t, h) for t in range(TILES) for h in range(HEADS)]


def layer_program(nc, A, O):
    ctx = ExitStack()
    with ctx:
        def sem(name):
            return ctx.enter_context(nc.semaphore(name))

        def sb(stack, name, shape, dt=F32):
            return stack.enter_context(nc.sbuf_tensor(name, shape, dt))

        def pb(name, dt=F32):
            return ctx.enter_context(nc.psum_tensor(name, [P, 512], dt))

        slot_token = nc.dram_tensor("slot_token", (SLOT_ROWS, 1), I32).ap()
        h3_rows = nc.dram_tensor("h3_rows", (TOK, D), F32).ap()
        y_rows = nc.dram_tensor("y_rows", (SLOT_ROWS, D), F32).ap()

        raw = sb(ctx, "raw", [P, RING, UNIT])
        X = sb(ctx, "X", [P, TILES, D])
        hT = sb(ctx, "hT", [P, KB, TOK])
        ident = sb(ctx, "ident", [P, P])
        stat = sb(ctx, "stat", [P, 16, 8])
        rs = sb(ctx, "rs", [P, 16, 8])
        neghalf = sb(ctx, "neghalf", [P, 8])
        wr = sb(ctx, "wr", [P, KB, GROUPS + E])
        br = sb(ctx, "br", [P, GROUPS + E])
        before = sb(ctx, "before", [P, P], BF16)
        onesb = sb(ctx, "onesb", [P, P], BF16)
        eidx = sb(ctx, "eidx", [P, E])
        tokid = sb(ctx, "tokid", [P, TILES], I32)
        chosen = sb(ctx, "chosen", [P, TILES, E], BF16)
        zeros = sb(ctx, "zeros", [P, 256])
        gate = sb(ctx, "gate", [P, 2, TILES])
        slot_i = sb(ctx, "slot_i", [P, 2, TILES], I32)
        idx_sb = sb(ctx, "idx_sb", [P, E], I32)
        small = sb(ctx, "small", [P, 2])
        tiny = sb(ctx, "tiny", [P, 48])
        extra_i = sb(ctx, "extra_i", [1, MAX_EXTRA + 1], I32)

        qT = X[:, :, :].rearrange("p t n -> p (t n)")[:, 0:HEADS * TOK].rearrange("p (h n) -> p h n", h=HEADS)
        kpT = X[:, :, :].rearrange("p t n -> p (t n)")[:, HEADS * TOK:HEADS * (TOK + PAST)].rearrange(
            "p (h n) -> p h n", h=HEADS)
        kprow = hT[:, :, :].rearrange("p k n -> p (k n)")[:, 0:2048].rearrange("p (b n) -> p b n", b=4)
        vp = hT[:, :, :].rearrange("p k n -> p (k n)")[:, 2048:4096].rearrange("p (b n) -> p b n", b=4)

        pre = ExitStack()
        mixT = sb(pre, "mixT", [P, KB, TOK])
        memT = mixT[:, :, 0:MEM]
        junk = mixT[:, :, 384:512]
        mkT = sb(pre, "mkT", [P, MH, MEM])
        mv = sb(pre, "mv", [P, 2, 512])
        kT = sb(pre, "kT", [P, HEADS, TOK])
        vrow = sb(pre, "vrow", [P, TILES, 512])
        rowbuf = sb(pre, "rowbuf", [P, 2, 512])
        gains = sb(pre, "gains", [P, 4, KB])
        gdiff = sb(pre, "gdiff", [P, P])
        ggla = sb(pre, "ggla", [P, GV])
        lamv = sb(pre, "lamv", [P, 4, 64])
        lams = sb(pre, "lams", [P, 8])
        wa2 = sb(pre, "wa2", [16, P])
        ba = sb(pre, "ba", [P, 1])
        pscale = sb(pre, "pscale", [P, 2])
        poolw = sb(pre, "poolw", [P, 2, P])
        causal = sb(pre, "causal", [P, P])
        hide_q = sb(pre, "hide_q", [CH + 1, P], BF16)
        hide_k = sb(pre, "hide_k", [CH + 1, CH], BF16)

        glas = ExitStack()
        gv = sb(glas, "gv", [P, TILES, GH * GV])
        zR = sb(glas, "zR", [P, TILES, 272])
        gq = sb(glas, "gq", [P, TOK])
        gk = sb(glas, "gk", [P, TOK])
        cum = sb(glas, "cum", [P, TOK])
        t1 = sb(glas, "t1", [P, TOK])
        t2 = sb(glas, "t2", [P, TOK])
        t3 = sb(glas, "t3", [P, TOK])
        t4 = sb(glas, "t4", [P, TOK])
        gaT = t4[0:16, :]
        dec_end = sb(glas, "dec_end", [P, NCH])
        kend = sb(glas, "kend", [P, TILES, P])
        S = sb(glas, "S", [P, 9, GH * GV])
        Ss = sb(glas, "Ss", [P, 2, GH * GV])
        own = sb(glas, "own", [P, GH * GV])
        attm = sb(glas, "attm", [P, 2, 512])
        EXT = 16 + SEQ + 16 + DEC
        S0 = 16 + SEQ + 16
        ext = sb(glas, "ext", [P, 2, EXT])
        win_a = sb(glas, "win_a", [P, 2, EXT])
        win_b = sb(glas, "win_b", [P, 2, EXT])
        ramp = sb(glas, "ramp", [P, 2, 16])
        keep = S[:, 5:8, :].rearrange("p a b -> p (a b)")[:, 0:TOK]
        mixg = cum[:, 0:512].rearrange("p (b n) -> p b n", b=2)
        hist = kend[0:HIST, 0:2, :].rearrange("p a b -> p (a b)")
        glas.close()

        dif = ExitStack()
        prob = sb(dif, "prob", [P, 2, 2, TOK])
        pdT = sb(dif, "pdT", [P, 2, 5, P])
        mixd = sb(dif, "mixd", [P, 2, 512])
        diff_sq = sb(dif, "diff_sq", [P, 512])
        dif.close()

        mem = ExitStack()
        cmkrow = sb(mem, "cmkrow", [P, 2, 512])
        cmkT = sb(mem, "cmkT", [P, MH, MEM])
        cmv = sb(mem, "cmv", [P, 2, 512])
        qmT = sb(mem, "qmT", [P, 2, MH, P])
        probm = sb(mem, "probm", [P, 2, MH, MEM])
        pmT = sb(mem, "pmT", [P, 2, 2 * MH, P])
        gffn = sb(mem, "gffn", [P, D])
        omT = sb(mem, "omT", [P, MH, TOK])
        h3 = sb(mem, "h3", [P, 2, D])
        mem.close()
        pre.close()

        moe = ExitStack()
        wh = sb(moe, "wh", [P, WR, UNIT], F32R)
        wl = sb(moe, "wl", [P, WR, UNIT], F32R)
        hTh = sb(moe, "hTh", [P, 2, 4, P], F32R)
        hTl = sb(moe, "hTl", [P, 2, 4, P], F32R)
        xgh = sb(moe, "xgh", [P, 2, KB, P], F32R)
        xgl = sb(moe, "xgl", [P, 2, KB, P], F32R)
        xg = sb(moe, "xg", [P, 2, D])
        act_g = sb(moe, "act_g", [P, 512])
        hid = sb(moe, "hid", [P, 512])
        y = sb(moe, "y", [P, 2, D])
        idx_extra = sb(moe, "idx_extra", [P, 1], I32)
        pool_mark = sb(moe, "pool_mark", [1, 2])
        moe.close()

        end = ExitStack()
        yg = sb(end, "yg", [P, 2, 2, D])
        gfin = sb(end, "gfin", [P, D])
        outb = sb(end, "outb", [P, 2, D])
        junk_end = sb(end, "junk_end", [P, D])
        end.close()
        pj = [pb("pj0"), pb("pj1")]
        tr = [pb("tr_v"), pb("tr_a")]
        sc = ctx.enter_context(nc.psum_tensor("scores", [P, 4 * 512], F32))

        def flat(ap):
            return ap.rearrange("p a b -> p (a b)")

        memsrc = flat(vrow[:, :, :])[:, 0:2048].rearrange("p (t n) -> p t n", t=2)
        q_heads = [gq[:, 0:512], gk[:, 0:512]]
        gla_sq = t4[:, 0:256]
        sq_scr = probm[:, 0, :, :].rearrange("p h k -> p (h k)")
        nmax, psum_, recip = (tiny[:, 4 * i:4 * i + 4].rearrange("p (b m) -> p b m", b=2) for i in range(3))
        nmaxm, psumm, nrec = (tiny[:, 16 + 8 * i:24 + 8 * i].rearrange("p (b h) -> p b h", b=2) for i in range(3))
        scratch = flat(hT[:, :, :])
        lg = scratch[:, 0:100].rearrange("p (t n) -> p t n", t=TILES)
        r20 = [scratch[:, 100 + 20 * i:120 + 20 * i].rearrange("p (t n) -> p t n", t=TILES) for i in range(6)]
        r5 = [scratch[:, 220 + 5 * i:225 + 5 * i] for i in range(7)]
        r80 = [scratch[:, 260 + 80 * i:340 + 80 * i].rearrange("p (t n) -> p t n", t=TILES) for i in range(4)]
        rank4 = scratch[:, 590:594]
        more, upto, base, ones16 = (scratch[:, 600 + 16 * i:616 + 16 * i] for i in range(4))
        r8x16 = scratch[0:1, 680:680 + MAX_EXTRA * E].rearrange("p (i e) -> p i e", e=E)
        extra_f = scratch[0:1, 820:820 + MAX_EXTRA]
        pg, pu, ph = pj, tr[0], tr[1]
        px = [sc[:, 0:512], sc[:, 512:1024]]
        py = [sc[:, 1024:1536], sc[:, 1536:2048]]

        ROW_USES = [(True, ("mk", 0)), (True, ("mk", 1))] + [(False, ("G", t)) for t in range(TILES)]
        ROW_USES += [(t >= 3, ("U", t)) for t in range(TILES)] + [(True, ("K", t)) for t in range(TILES)]
        ROW_USES += [(False, ("Q", t)) for t in range(TILES)]
        ROW_AT = {key: n for n, (_, key) in enumerate(ROW_USES)}
        ROW_STORES = [sum(s for s, _ in ROW_USES[n % 2:n:2]) for n in range(len(ROW_USES))]
        ROW_TOTAL = [sum(s for s, _ in ROW_USES[b::2]) for b in range(2)]
        NPARAMS = 16

        unit_in = [sem(f"unit_in{i}") for i in range(RING)]
        x_in = [sem(f"x_in{t}") for t in range(TILES)]
        x_again = sem("x_again")
        mem_in, params_in, hist_in, state_in = sem("mem_in"), sem("params_in"), sem("hist_in"), sem("state_in")
        kp_in, vp_in, cmk_in, cmv_in = sem("kp_in"), sem("vp_in"), sem("cmk_in"), sem("cmv_in")
        gffn_in, gfin_in = sem("gffn_in"), sem("gfin_in")
        stored = sem("stored")
        row_out = [sem("row_out0"), sem("row_out1")]
        state_out = sem("state_out")
        table_zero, table_out, idx_in = sem("table_zero"), sem("table_out"), sem("idx_in")
        h3_out = [sem("h3_out0"), sem("h3_out1")]
        consts = sem("consts")
        pj_full, pj_act, pj_dve = sem("pj_full"), sem("pj_act"), sem("pj_dve")
        tr_full, tr_act, tr_dve = sem("tr_full"), sem("tr_act"), sem("tr_dve")
        sc_full, sc_act, sc_dve = sem("sc_full"), sem("sc_act"), sem("sc_dve")
        ms_act, ms_dve, rs_ready = sem("ms_act"), sem("ms_dve"), sem("rs_ready")
        dve_step, act_step, pool_step = sem("dve_step"), sem("act_step"), sem("pool_step")
        lam_sum, lam_exp, lam_ready = sem("lam_sum"), sem("lam_exp"), sem("lam_ready")
        gate_arg, gate_log, cum_ready, decay_arg, decay_exp, gla_in = (sem(n) for n in (
            "gate_arg", "gate_log", "cum_ready", "decay_arg", "decay_exp", "gla_in"))
        silu_ready, glu_ready, states_ready, att_ready, mixg_ready = (sem(n) for n in (
            "silu_ready", "glu_ready", "states_ready", "att_ready", "mixg_ready"))
        sq_act = sem("sq_act")
        ramp_ready, pool_ready = sem("ramp_ready"), sem("pool_ready")
        max_ready, exp_ready, pd_ready, mixd_ready = (sem(n) for n in (
            "max_ready", "exp_ready", "pd_ready", "mixd_ready"))
        maxm_ready, expm_ready, pm_ready = sem("maxm_ready"), sem("expm_ready"), sem("pm_ready")
        h3_ready, chosen_ready, route_exp, slots_ready, list_ready = (sem(n) for n in (
            "h3_ready", "chosen_ready", "route_exp", "slots_ready", "list_ready"))
        route_arg, qb_ready, pool_mark_set = sem("route_arg"), sem("qb_ready"), sem("pool_mark_set")
        hi_done, lo_done, pe_unit = sem("hi_done"), sem("lo_done"), sem("pe_unit")
        xt_done, xh_done, xl_done = sem("xt_done"), sem("xh_done"), sem("xl_done")
        sg_done, h_done, ht_done, hh_done, hl_done = (sem(n) for n in ("sg_done", "h_done", "ht_done", "hh_done", "hl_done"))
        y_done, sum_done, out_ready = sem("y_done"), sem("sum_done"), sem("out_ready")
        xg_in, y_out, yg_in, out_stored = ([sem(n + "0"), sem(n + "1")] for n in ("xg_in", "y_out", "yg_in", "out_stored"))

        RS = {k: n for n, k in enumerate(
            ["mem", "x"] + [("gla", t) for t in range(TILES)] + [("diff", t) for t in range(TILES)]
            + [(b, t) for b in ("x1", "x2", "end") for t in range(TILES)])}
        STAT = {"mem": 0, "x": 1, "x1": 2, "x2": 3, "end": 4}
        MS_ACT = {k: n for n, k in enumerate(
            [("mem", 0), ("mem", 1)] + [(b, t) for b in ("x", "x1", "x2", "end") for t in range(TILES)])}
        PJ_KEYS, TR_KEYS, SC_KEYS = list(PJ), list(TR), list(SC)
        UNIT_USER = [("memk", 1)] * 2 + [("memv", 1)] * 2 + [(b, 4) for b, _, _ in IN_BLOCKS for _ in range(2)]
        UNIT_USER += [("w_out", c, 4) for c in range(2) for _ in range(2)] + [("mem_q", 4)] * 2
        UNIT_USER += [("w_mem_o", c, 4) for c in range(2)]
        BLOCK_UNITS = {b: (4 + 2 * n, 5 + 2 * n) for n, (b, _, _) in enumerate(IN_BLOCKS)}
        WIDTH = {b: w for b, _, w in IN_BLOCKS}
        WO_UNIT, MQ_UNIT, MO_UNIT = 16, 20, 22

        def stat_of(key):
            if key == "mem":
                return slice(0, P), 0, slice(0, 2)
            if key == "x":
                return slice(0, P), 1, slice(0, TILES)
            name, t = key
            if name in ("gla", "diff"):
                return slice(0, ROWS[t]), (5 if name == "gla" else 10) + t, slice(0, 4)
            return slice(0, ROWS[t]), STAT[name], slice(t, t + 1)

        def read_out(eng, numbers, act_sem, dve_sem, key):
            _, who, rank = numbers[key]
            eng.wait_ge(act_sem if who == "A" else dve_sem, rank + 1)

        def pj_read(eng, key):
            read_out(eng, PJ, pj_act, pj_dve, key)

        def tr_read(eng, key):
            read_out(eng, TR, tr_act, tr_dve, key)

        def sc_read(eng, key):
            read_out(eng, SC, sc_act, sc_dve, key)

        def cols(t):
            return slice(P * t, P * t + ROWS[t])

        def x_tile(t):
            return X[0:ROWS[t], t, :]

        def half(key):
            return sc[:, (SC[key][0] % 2) * 1024:(SC[key][0] % 2) * 1024 + 1024]

        def maps(t, h, nk):
            n, R = SC[last_score(t, h)][0], ROWS[t]
            if t < 4:
                return sc[0:R, (n % 2) * 1024:(n % 2) * 1024 + 1024].rearrange("p (m k) -> p m k", m=2)[:, :, 0:nk]
            assert n % 2 == 0
            return sc[0:R, :].rearrange("p (m k) -> p m k", m=2)[:, :, 0:nk]

        def keys_of(t):
            return P * (t + 1) if t < 4 else PAST + DEC

        def last_score(t, h):
            return ("diff", t, h) if t < 4 else ("diff", t, h, 0)

        def step_unit(j, last):
            names = [("w_exp_up", 0), ("w_exp_down", 0)] if last else [("w_exp_up", 0), ("w_exp_gate", 1), ("w_exp_down", 0)]
            return (*names[j // 2], j % 2)

        def fixed(e, n):
            return isinstance(e, int) and e < n

        block = ctx.enter_context(nc.Block())
        dram = {n: A[n] for n in ("w_mem_kv", "w_in", "w_out", "w_mem_q", "w_mem_o")}

        @block.sync
        def _(sp):
            for n, (name, r, c, w) in enumerate(DENSE):
                if n >= RING:
                    sp.wait_ge(pj_full, PJ[UNIT_USER[n - RING]][0] + 1)
                dst = raw[:, n % RING, 0:4 * w].rearrange("p (k w) -> p k w", k=4)
                src = dram[name][0, r:r + 512, c:c + w].rearrange("(k p) w -> p k w", p=P)
                sp.dma_start(dst, src).then_inc(unit_in[n % RING], 16)
            def load(n_slot, free, name, e, part):
                free()
                src = A[name][0, e if isinstance(e, int) else bass.ds(e, 1)]
                if not isinstance(e, int):
                    src = src.rearrange("a r c -> (a r) c")
                src = src[:, 512 * part:512 * part + 512] if name == "w_exp_down" else src[512 * part:512 * part + 512, :]
                sp.dma_start(raw[:, n_slot, :].rearrange("p (k w) -> p k w", k=4),
                             src.rearrange("(k p) w -> p k w", p=P)).then_inc(unit_in[n_slot], 16)

            def step_load(e, j, last=False):
                name, who, part = step_unit(j, last)

                def free():
                    if fixed(e, 1) and j < 4:
                        sp.wait_ge(pj_full, PJ[UNIT_USER[NDENSE - RING + 2 + j]][0] + 1)
                    else:
                        sp.wait_ge(lo_done, 6 * e + (j - 3))

                load((2 + j) % RING, free, name, e + who, part)

            for n in range(2):
                load(n, lambda: sp.wait_ge(pj_full, PJ[UNIT_USER[NDENSE - RING + n]][0] + 1), "w_exp_gate", 0, n)
            for e in range(2):
                for j in range(6):
                    step_load(e, j)
            with sp.Fori(1, E // 2 - 1) as i:
                for b in range(2):
                    for j in range(6):
                        step_load(2 * i + b, j)
            for j in range(6):
                step_load(E - 2, j)
            for j in range(4):
                step_load(E - 1, j, last=True)
            sp.wait_ge(list_ready, 1)
            rounds = sp.value_load(extra_i[0:1, MAX_EXTRA:MAX_EXTRA + 1], min_val=0, max_val=MAX_EXTRA)
            with sp.If(rounds > 0):
                with sp.Fori(0, rounds) as i:
                    e = sp.value_load(extra_i[0:1, bass.ds(i, 1)], min_val=0, max_val=E - 1)
                    for k in range(6):
                        name, part = ("w_exp_gate", "w_exp_up", "w_exp_down")[k // 2], k % 2
                        load(k, lambda: sp.wait_ge(lo_done, NMOE + 6 * i + (k - 5)), name, e, part)

        @block.gpsimd
        def _(pool):
            steps = [0]

            def link(ins):
                steps[0] += 1
                ins.then_inc(pool_step, 1)
                pool.wait_ge(pool_step, steps[0])

            def ready(ins):
                const_count[0] += 1
                ins.then_inc(consts, 1)
                pool.wait_ge(consts, const_count[0])

            const_count = [0]
            link(pool.memset(stat[:, :, :], 1.0))
            link(pool.memset(ident[:, :], 0.0))
            ready(pool.affine_select(out=ident[:, :], in_=ident[:, :], compare_op=ALU.not_equal, fill=1.0, base=0,
                                     pattern=[[-1, P]], channel_multiplier=1))
            link(pool.memset(causal[:, :], 1.0))
            link(pool.affine_select(out=causal[:, :], in_=causal[:, :], compare_op=ALU.is_ge, fill=0.0, base=0,
                                    pattern=[[1, P]], channel_multiplier=-1))
            ready(pool.memset(causal[0:CH, CH:P], 0.0))
            link(pool.memset(before[:, :], 1.0))
            ready(pool.affine_select(out=before[:, :], in_=before[:, :], compare_op=ALU.is_ge, fill=0.0, base=-1,
                                     pattern=[[1, P]], channel_multiplier=-1))
            ready(pool.memset(onesb[:, :], 1.0))
            ready(pool.memset(neghalf[:, :], -0.5))
            link(pool.memset(own[:, :], 0.0))
            for h in range(GH - 1):
                link(pool.memset(own[GK * h:GK * (h + 1), GV * h:GV * (h + 1)], 1.0))
            ready(pool.memset(own[GK * 3:P, GV * 3:], 1.0))
            ready(pool.memset(poolw[:, :, :], 0.0))
            ready(pool.iota(eidx[:, :], [[1, E]], base=0, channel_multiplier=0, allow_small_or_imprecise_dtypes=True))
            ready(pool.iota(tokid[:, :], [[P, TILES]], base=0, channel_multiplier=1))
            ready(pool.memset(zeros[:, :], 0.0))
            link(pool.memset(hide_q[:, :], 0.0))
            link(pool.memset(hide_q[:, 0:CH], 1.0))
            ready(pool.memset(hide_k[:, :], -1e30))
            link(pool.memset(S[:, 0, :], 0.0))
            link(pool.memset(keep, 1.0))
            ready(pool.memset(keep.rearrange("p (c n) -> p c n", n=CH)[:, :, 0], 0.0))
            ready(pool.memset(Ss[:, 0, :], 0.0))
            link(pool.memset(ext[:, :, 0:16], 0.0))
            ready(pool.memset(ext[:, :, S0 - 16:S0 - 15], 0.0))
            for g in range(4):
                pool.dma_start(poolw[64 * (g % 2):64 * (g % 2) + 64, g // 2, 64 * (g % 2):64 * (g % 2) + 64],
                               A["pool_w"][0, g]).then_inc(state_in, 16)
                pool.dma_start(Ss[GK * g:GK * g + GK, 0, GV * g:GV * g + GV], A["state_gla"][0, 0, g])\
                    .then_inc(state_in, 16)
            pool.dma_start(slot_token.rearrange("(p n) o -> p (n o)", p=P), zeros[:, 0:SLOT_ROWS // P].bitcast(I32))\
                .then_inc(table_zero, 16)
            pool.dma_start(y_rows[P * E:SLOT_ROWS, :].rearrange("(p r) (b n) -> p (r b) n", p=P, n=256),
                           zeros[:, :].unsqueeze(1).to_broadcast([P, 4 * MAX_EXTRA, 256])).then_inc(table_zero, 16)

            def root(key):
                rows, n, cs = stat_of(key)
                if key == "mem":
                    pool.wait_ge(ms_act, MS_ACT[("mem", 1)] + 1)
                elif key == "x":
                    pool.wait_ge(ms_act, MS_ACT[("x", TILES - 1)] + 1)
                elif key[0] in ("gla", "diff"):
                    pool.wait_ge(ms_dve, RS[key] - 1)
                else:
                    pool.wait_ge(ms_act, MS_ACT[key] + 1)
                link(pool.tensor_scalar(rs[rows, n, cs], stat[rows, n, cs], EPS, None, ALU.add))
                width = cs.stop - cs.start
                pool.tensor_tensor(rs[rows, n, cs], rs[rows, n, cs], neghalf[rows, 0:width], ALU.pow)\
                    .then_inc(rs_ready, 1)
                pool.wait_ge(rs_ready, RS[key] + 1)

            root("mem")
            root("x")
            pool.wait_ge(silu_ready, 2)
            for t in range(TILES):
                v = zR[0:ROWS[t], t, 0:256].rearrange("p (h v) -> p h v", h=GH)
                pool.tensor_tensor(v, v, ggla[0:ROWS[t], :].unsqueeze(1).to_broadcast([ROWS[t], GH, GV]), ALU.mult)\
                    .then_inc(glu_ready, 1)
                pool.wait_ge(glu_ready, t + 1)
            tr_read(pool, ("hist",))
            tr_read(pool, ("U", TILES - 1))
            W = EXT
            link(pool.tensor_tensor(win_a[:, :, 1:W], ext[:, :, 1:W], ext[:, :, 0:W - 1], ALU.add))
            link(pool.tensor_tensor(win_b[:, :, 3:W], win_a[:, :, 3:W], win_a[:, :, 1:W - 2], ALU.add))
            link(pool.tensor_tensor(win_a[:, 1, 7:W], win_b[:, 1, 7:W], win_b[:, 1, 3:W - 4], ALU.add))
            link(pool.tensor_tensor(win_b[64:P, 1, 15:W], win_a[64:P, 1, 15:W], win_a[64:P, 1, 7:W - 8], ALU.add))
            pool.wait_ge(ramp_ready, 1)
            for g, win in enumerate((win_a, win_b, win_a, win_b)):
                rows, b = slice(64 * (g % 2), 64 * (g % 2) + 64), g // 2
                link(pool.tensor_tensor(win[rows, b, 16:32], win[rows, b, 16:32], ramp[rows, b, :], ALU.mult))
                link(pool.tensor_scalar(win[rows, b, 16:W], win[rows, b, 16:W], 1.0 / POOL_WINDOWS[g], None, ALU.mult))
                pool.tensor_tensor(ext[rows, b, 16:W], win[rows, b, 16:W], ext[rows, b, 16:W], ALU.subtract)\
                    .then_inc(pool_ready, 1)
                pool.wait_ge(pool_ready, g + 1)
            for b in ("gla", "diff", "x1", "x2"):
                for t in range(TILES):
                    root((b, t))
            pool.wait_ge(table_zero, 32)
            pool.wait_ge(slots_ready, 1)
            for i in range(2):
                for t in range(TILES):
                    r = ROWS[t]
                    pool.indirect_dma_start(slot_token, bass.IndirectOffsetOnAxis(ap=slot_i[0:r, i, t:t + 1], axis=0),
                                            tokid[0:r, t:t + 1], None).then_inc(table_out, 16)
            pool.wait_ge(table_out, 16 * 2 * TILES)
            pool.dma_start(idx_sb[:, :], slot_token[0:P * E, :].rearrange("(p e) o -> p (e o)", e=E)).then_inc(idx_in, 16)
            pool.wait_ge(idx_in, 16)
            pool.wait_ge(h3_out[0], 16 * 3)
            pool.wait_ge(h3_out[1], 16 * 2)

            def gather(e):
                if e >= 2:
                    pool.wait_ge(xt_done, 2 * (e - 2) + 2)
                pool.indirect_dma_start(xg[:, e % 2, :], None, h3_rows,
                                        bass.IndirectOffsetOnAxis(ap=idx_sb[:, e:e + 1], axis=0)).then_inc(xg_in[e % 2], 16)

            gather(0)
            gather(1)
            for e in range(E):
                if e + 2 < E:
                    gather(e + 2)
                pool.wait_ge(y_done, 2 * e + 2)
                pool.dma_start(y_rows[0:P * E, :].rearrange("(p e) n -> p e n", e=E)[:, e, :], y[:, e % 2, :])\
                    .then_inc(y_out[e % 2], 16)
            pool.wait_ge(list_ready, 1)
            rounds = pool.value_load(extra_i[0:1, MAX_EXTRA:MAX_EXTRA + 1], min_val=0, max_val=MAX_EXTRA)
            with pool.If(rounds > 0):
                with pool.Fori(0, rounds) as i:
                    pool.wait_ge(xt_done, 2 * E + 2 * i)
                    pool.tensor_tensor(pool_mark[:, 0:1], zeros[0:1, 0:1], zeros[0:1, 1:2], ALU.add).then_inc(pool_mark_set, 1)
                    table = slot_token.rearrange("(r p) o -> r p o", p=P)[bass.ds(E + i, 1)]
                    pool.dma_start(idx_extra[:, :], table.rearrange("a p o -> (a p) o"), allow_slow_non_contiguous=True)\
                        .then_inc(idx_in, 16)
                    pool.wait_ge(pool_mark_set, 3 * i + 1)
                    pool.wait_ge(idx_in, 16 * i + 32)
                    pool.tensor_tensor(pool_mark[:, 0:1], zeros[0:1, 0:1], zeros[0:1, 1:2], ALU.add).then_inc(pool_mark_set, 1)
                    pool.indirect_dma_start(xg[:, 0, :], None, h3_rows,
                                            bass.IndirectOffsetOnAxis(ap=idx_extra[:, 0:1], axis=0)).then_inc(xg_in[0], 16)
                    pool.wait_ge(pool_mark_set, 3 * i + 2)
                    pool.wait_ge(y_done, 2 * E + 2 * i + 2)
                    pool.tensor_tensor(pool_mark[:, 0:1], zeros[0:1, 0:1], zeros[0:1, 1:2], ALU.add).then_inc(pool_mark_set, 1)
                    rows = y_rows.rearrange("(r p) n -> r p n", p=P)[bass.ds(E + i, 1)]
                    pool.dma_start(rows.rearrange("a p n -> (a p) n"), y[:, 0, :]).then_inc(y_out[0], 16)
            pool.wait_ge(y_out[0], 8 * E + 16 * rounds)
            pool.wait_ge(y_out[1], 8 * E)
            pool.tensor_tensor(pool_mark[:, 1:2], zeros[0:1, 0:1], zeros[0:1, 1:2], ALU.add)

            def gather_y(t):
                if t >= 2:
                    pool.wait_ge(sum_done, t - 1)
                for i in range(2):
                    r = ROWS[t]
                    pool.indirect_dma_start(yg[0:r, t % 2, i, :], None, y_rows,
                                            bass.IndirectOffsetOnAxis(ap=slot_i[0:r, i, t:t + 1], axis=0))\
                        .then_inc(yg_in[t % 2], 16)

            gather_y(0)
            pool.dma_start(gfin[:, :], A["final_norm_g"].unsqueeze(0).to_broadcast([P, D])).then_inc(gfin_in, 16)
            gather_y(1)
            for t in range(TILES):
                if t + 2 < TILES:
                    gather_y(t + 2)
                root(("end", t))

        @block.scalar
        def _(act):
            steps = [0]

            def link(ins):
                steps[0] += 1
                ins.then_inc(act_step, 1)
                act.wait_ge(act_step, steps[0])

            def split_hi(e, b, j):
                s4, s6 = (2 + 6 * b + j) % WR, (2 + j) % RING
                act.wait_ge(unit_in[s6], 16 * (e + (NDENSE // RING + 1 + (2 + j) // RING)))
                if not fixed(6 * e + j + 2 if isinstance(e, int) else e, WR):
                    act.wait_ge(pe_unit, 6 * e + (j - 1))
                act.activation(wh[:, s4, :], raw[:, s6, :], ACT.Copy).then_inc(hi_done, 1)

            act.dma_start(memsrc[:, :, :], A["mem_prompt"][0].rearrange("(t p) n -> p t n", p=P)).then_inc(mem_in, 16)
            for t in range(4):
                act.dma_start(X[:, t, :], A["x_prompt"][0, P * t:P * t + P, :]).then_inc(x_in[t], 16)
            act.dma_start(X[0:DEC, 4, :], A["x_sample"][0]).then_inc(x_in[4], 16)
            params = [(gains[:, i, :], A[n].rearrange("a (k p) -> p (a k)", p=P)) for i, n in enumerate(
                ("norm_mix_g", "mem_norm_g", "norm_mem_g"))]
            params += [(ggla[:, :], A["gla_norm_g"].to_broadcast([P, GV])),
                       (gdiff[:, :], A["diff_norm_g"].to_broadcast([P, P])),
                       (wa2[:, :], A["w_gla_a2"][0]), (ba[:, :], A["b_gla_a"].rearrange("a p -> p a")),
                       (pscale[:, :], A["pool_scale"].rearrange("a (k p) -> p (a k)", p=P)),
                       (wr[:, :, 0:GROUPS], A["w_router_group"][0].rearrange("(k p) n -> p k n", p=P)),
                       (wr[:, :, GROUPS:], A["w_router_expert"][0].rearrange("(k p) n -> p k n", p=P)),
                       (br[:, 0:GROUPS], A["b_router_group"].to_broadcast([P, GROUPS])),
                       (br[:, GROUPS:], A["b_router_expert"].to_broadcast([P, E]))]
            params += [(lamv[:, i, :], A[n].to_broadcast([P, 64])) for i, n in enumerate(
                ("lambda_q1", "lambda_k1", "lambda_q2", "lambda_k2"))]
            for dst, src in params:
                act.dma_start(dst, src, allow_slow_non_contiguous=True).then_inc(params_in, 16)
            assert len(params) == NPARAMS
            act.dma_start(hist, A["state_pool"][0, 0]).then_inc(hist_in, 16)

            def mean_square(key, src, j, folded=False):
                rows, n, cs = stat_of(key if key[0] not in ("mem", "x") else key[0])
                i = key[1]
                r = src.shape[0]
                if MS_ACT[key]:
                    act.wait_ge(ms_act, MS_ACT[key])
                src = src.rearrange("p (a b) -> p a b", a=KB) if folded else src
                act.activation(j[0:r], src, ACT.Square, scale=1.0 / 32, accum_out=stat[0:r, n, i:i + 1])\
                    .then_inc(ms_act, 1)

            act.wait_ge(consts, 1)
            act.wait_ge(mem_in, 16)
            for i in range(2):
                mean_square(("mem", i), memsrc[:, i, :], junk, True)
            for t in range(TILES):
                act.wait_ge(x_in[t], 16)
                mean_square(("x", t), x_tile(t), junk, True)

            def pj_out(key, dst, scale=None, at=None):
                j = PJ[key][0]
                act.wait_ge(pj_full, j + 1)
                src = pj[j % 2][0:dst.shape[0], 0:dst.shape[-1]] if at is None else at
                if scale is None:
                    return act.activation(dst, src, ACT.Copy)
                return act.activation(dst, src, ACT.Copy, scale=scale)

            def tr_out(key, dst, src):
                act.wait_ge(tr_full, TR[key][0] + 1)
                act.activation(dst, src, ACT.Copy).then_inc(tr_act, 1)

            def heads_view(bank, n, r=P):
                return bank[:, 0:n * P].rearrange("p (h q) -> p h q", h=n)[:, :, 0:r]

            act.wait_ge(rs_ready, RS["mem"] + 1)
            for b in ("memk", "memv"):
                for i in range(2):
                    dst = rowbuf[:, i, :] if b == "memk" else mv[:, i, :]
                    pj_out((b, i), dst, rs[:, 0, i:i + 1]).then_inc(pj_act, 1)
                    act.wait_ge(pj_act, PJ[(b, i)][2] + 1)
                    out = O[4 if b == "memk" else 5][0, 0, P * i:P * i + P].rearrange("m h d -> m (h d)")
                    act.dma_start(out, dst).then_inc(row_out[i] if b == "memk" else stored, 16)
            for i in range(2):
                tr_out(("mk", i), mkT[:, :, P * i:P * i + P], heads_view(tr[1], MH))

            act.wait_ge(rs_ready, RS["x"] + 1)

            def rowbuf_free(n):
                if ROW_STORES[n]:
                    act.wait_ge(row_out[n % 2], 16 * ROW_STORES[n])
                if ROW_USES[n - 2][1] is not None:
                    act.wait_ge(tr_full, TR[ROW_USES[n - 2][1]][0] + 1)

            for t in range(TILES):
                n = 2 + t
                rowbuf_free(n)
                r = ROWS[t]
                pj_out(("G", t), rowbuf[0:r, n % 2, 0:256], rs[0:r, 1, t:t + 1],
                       pj[PJ[("G", t)][0] % 2][0:r, 0:256]).then_inc(act_step, 1)
                steps[0] += 1
                pj_out(("G", t), gv[0:r, t, :], rs[0:r, 1, t:t + 1],
                       pj[PJ[("G", t)][0] % 2][0:r, 256:512]).then_inc(pj_act, 1)
            for t in range(TILES):
                pj_out(("R", t), zR[0:ROWS[t], t, :], rs[0:ROWS[t], 1, t:t + 1]).then_inc(pj_act, 1)
            tr_out(("R", 0), gaT[:, 0:512], tr[1][0:16, :])
            tr_out(("R", 1), gaT[:, 512:TOK], tr[1][0:16, 0:DEC])
            for r, ts in ((P, slice(0, 4)), (DEC, slice(4, 5))):
                act.activation(zR[0:r, ts, 0:256], zR[0:r, ts, 0:256], ACT.Silu).then_inc(silu_ready, 1)

            def rows_block(b, t, n):
                rowbuf_free(n)
                r, w = ROWS[t], WIDTH[b]
                pj_out((b, t), rowbuf[0:r, n % 2, 0:w], rs[0:r, 1, t:t + 1]).then_inc(pj_act, 1)
                act.wait_ge(pj_act, PJ[(b, t)][2] + 1)
                if b == "K":
                    out = O[2][0, 0, P * t:P * t + P] if t < 4 else O[8][0, 0]
                    act.dma_start(out.rearrange("m h d -> m (h d)"), rowbuf[0:r, n % 2, :]).then_inc(row_out[n % 2], 16)
                if b == "U" and t >= 3:
                    out = O[7] if t == 3 else O[11]
                    act.dma_start(out[0, 0], rowbuf[r - HIST:r, n % 2, 0:256]).then_inc(row_out[n % 2], 16)

            def u_out(t):
                c0 = 16 + P * t if t < 4 else S0
                tr_out(("U", t), ext[:, :, c0:c0 + ROWS[t]], heads_view(tr[1], 2, ROWS[t]))

            for t in range(TILES):
                rows_block("U", t, ROW_AT[("U", t)])
                if t:
                    u_out(t - 1)
            u_out(TILES - 1)
            tr_out(("hist",), ext[:, :, S0 - HIST:S0], heads_view(tr[1], 2, HIST))

            act.wait_ge(gate_arg, 1)
            link(act.activation(t2[:, :], t2[:, :], ACT.Exp))
            act.activation(t3[:, :], t2[:, :], ACT.Ln, bias=1.0).then_inc(gate_log, 1)

            def kq_out(b, t):
                tr_out((b, t), (kT if b == "K" else qT)[:, :, cols(t)], heads_view(tr[1], HEADS, ROWS[t]))

            for t in range(TILES):
                rows_block("K", t, ROW_AT[("K", t)])
                if t:
                    kq_out("K", t - 1)
            kq_out("K", TILES - 1)
            act.wait_ge(cum_ready, 1)
            act.activation(dec_end[:, :], cum[:, :].rearrange("p (c n) -> p c n", n=CH)[:, :, CH - 1], ACT.Exp)\
                .then_inc(decay_exp, 1)
            act.activation(t3[:, :], cum[:, :], ACT.Exp).then_inc(decay_exp, 1)
            for i, buf in enumerate((t1, t2, t4)):
                act.wait_ge(decay_arg, i + 1)
                act.activation(buf[:, :], buf[:, :], ACT.Exp).then_inc(decay_exp, 1)
            act.wait_ge(lam_sum, 1)
            act.activation(lams[:, 2:4], lams[:, 0:2], ACT.Exp).then_inc(lam_exp, 1)

            for t in range(TILES):
                pj_out(("V", t), vrow[0:ROWS[t], t, :], rs[0:ROWS[t], 1, t:t + 1]).then_inc(pj_act, 1)
                act.wait_ge(pj_act, PJ[("V", t)][2] + 1)
                out = O[3][0, 0, P * t:P * t + P] if t < 4 else O[9][0, 0]
                act.dma_start(out.rearrange("m h d -> m (h d)"), vrow[0:ROWS[t], t, :]).then_inc(stored, 16)
            for t in range(TILES):
                rows_block("Q", t, ROW_AT[("Q", t)])
                if t:
                    kq_out("Q", t - 1)
            kq_out("Q", TILES - 1)
            act.dma_start(kprow, A["cache_diff_k"][0, 0].rearrange("(b p) h d -> p b (h d)", p=P)).then_inc(kp_in, 16)
            act.dma_start(vp, A["cache_diff_v"][0, 0].rearrange("(b p) h d -> p b (h d)", p=P)).then_inc(vp_in, 16)

            def mixg_out(t):
                tr_out(("mix_g", t), mixT[:, 0:2, cols(t)], heads_view(tr[1], 2, ROWS[t]))

            act.wait_ge(states_ready, 1)
            for i, src in ((6, S[:, 8, :]), (10, Ss[:, 1, :])):
                for h in range(GH):
                    act.dma_start(O[i][0, 0, h], src[GK * h:GK * h + GK, GV * h:GV * h + GV]).then_inc(state_out, 16)
            for t in range(TILES):
                j, r = PJ[("gla_o", t)][0], ROWS[t]
                act.wait_ge(pj_full, j + 1)
                if t:
                    act.wait_ge(ms_dve, t)
                act.activation(gla_sq[0:r, :], pj[j % 2][0:r, 0:256], ACT.Square, scale=0.125).then_inc(sq_act, 1)
                if t:
                    mixg_out(t - 1)
            mixg_out(TILES - 1)
            for b in range(4):
                tr_out(("kp", b), kpT[:, :, P * b:P * b + P], heads_view(tr[1], HEADS))
            for b in range(2):
                for name, w, c0 in (("pool", 512, 0), ("pool_s", DEC, 512)):
                    pj_out((name, b), mixT[:, 2 + b, c0:c0 + w], pscale[:, b:b + 1]).then_inc(pj_act, 1)

            act.wait_ge(state_out, 16 * 8)

            def exps(s):
                t, h = STEPS[s]
                r, nk = ROWS[t], keys_of(t)
                act.wait_ge(max_ready, s + 1)
                if s >= 2:
                    act.wait_ge(tr_full, TR[("pd", *STEPS[s - 2], 1 if STEPS[s - 2][0] == 4 else 0)][0] + 1)
                for m in range(2):
                    done = (m == 1) if t < 4 else True
                    ins = act.activation(prob[0:r, s % 2, m, 0:nk], maps(t, h, nk)[:, m, :], ACT.Exp,
                                         bias=nmax[0:r, s % 2, m:m + 1], scale=DH ** -0.5,
                                         accum_out=psum_[0:r, s % 2, m:m + 1])
                    ins.then_inc(sc_act, 1) if done else ins.then_inc(act_step, 1)
                    steps[0] += not done

            def mixd_out(t):
                tr_out(("mix_d", t), mixT[:, 4:8, cols(t)], heads_view(tr[1], 4, ROWS[t]))

            exps(0)
            for s, (t, h) in enumerate(STEPS):
                if s + 1 < len(STEPS):
                    exps(s + 1)
                r, nb = ROWS[t], min(key_blocks(t), 4)
                if TR[("pd", t, h, 0)][1] == "A":
                    tr_out(("pd", t, h, 0), pdT[:, s % 2, 0:nb, 0:r], heads_view(tr[1], nb, r))
                if t == 4:
                    tr_out(("pd", t, h, 1), pdT[0:CH, s % 2, 4, 0:r], tr[1][0:CH, 0:r])
                if h == 0 and t:
                    mixd_out(t - 1)
                if h == HEADS - 1:
                    j = PJ[("diff_o", t)][0]
                    act.wait_ge(pj_full, j + 1)
                    act.wait_ge(ms_dve, TILES + t)
                    act.activation(diff_sq[0:r, :], pj[j % 2][0:r, :], ACT.Square, scale=P ** -0.5).then_inc(sq_act, 1)
            mixd_out(TILES - 1)
            act.wait_ge(sc_full, SC[last_score(4, HEADS - 1)][0] + 1)
            act.dma_start(X[:, 0:4, :], A["x_prompt"][0].rearrange("(t p) n -> p t n", p=P)).then_inc(x_again, 16)
            act.dma_start(X[0:DEC, 4, :], A["x_sample"][0]).then_inc(x_again, 16)
            act.wait_ge(pj_full, PJ[("diff_o", 4)][0] + 1)
            act.wait_ge(mixd_ready, TILES)
            act.wait_ge(tr_full, TR[("mix_d", 4)][0] + 1)
            act.dma_start(cmkrow[:, :, :], A["cache_mem_k"][0, 0].rearrange("(b p) h d -> p b (h d)", p=P)).then_inc(cmk_in, 16)
            act.dma_start(cmv[:, :, :], A["cache_mem_v"][0, 0].rearrange("(b p) h d -> p b (h d)", p=P)).then_inc(cmv_in, 16)
            act.dma_start(gffn[:, :], A["norm_ffn_g"].to_broadcast([P, D])).then_inc(gffn_in, 16)
            act.wait_ge(row_out[0], 16 * ROW_TOTAL[0])
            act.wait_ge(row_out[1], 16 * ROW_TOTAL[1])

            for t in range(TILES):
                pj_read(act, ("w_out", 1, t))
                mean_square(("x1", t), x_tile(t), sq_scr)

            def mq_out(t):
                if t >= 2:
                    act.wait_ge(tr_full, TR[("mq", t - 2)][0] + 1)
                act.wait_ge(rs_ready, RS[("x1", t)] + 1)
                pj_out(("mem_q", t), rowbuf[0:ROWS[t], t % 2, :], rs[0:ROWS[t], 2, t:t + 1]).then_inc(pj_act, 1)

            def exps_m(t):
                act.wait_ge(maxm_ready, t + 1)
                if t >= 2:
                    act.wait_ge(tr_full, TR[("pm", t - 2, 1)][0] + 1)
                r = ROWS[t]
                for h in range(MH):
                    ins = act.activation(probm[0:r, t % 2, h, :], half(("mem", t))[0:r, MEM * h:MEM * h + MEM], ACT.Exp,
                                         bias=nmaxm[0:r, t % 2, h:h + 1], scale=P ** -0.5,
                                         accum_out=psumm[0:r, t % 2, h:h + 1])
                    if h == MH - 1:
                        ins.then_inc(sc_act, 1)
                    else:
                        steps[0] += 1
                        ins.then_inc(act_step, 1)

            mq_out(0)
            exps_m(0)
            for t in range(TILES):
                if t + 1 < TILES:
                    mq_out(t + 1)
                    if t == 3:
                        for b in range(2):
                            tr_out(("cmk", b), cmkT[:, :, P * b:P * b + P], heads_view(tr[1], MH))
                    exps_m(t + 1)
                if t >= 2:
                    act.wait_ge(pj_full, PJ[("mem_o", t - 2)][0] + 1)
                tr_out(("pm", t, 0), pmT[:, t % 2, 0:4, 0:ROWS[t]], heads_view(tr[1], 4, ROWS[t]))
                j = PJ[("mem_o", t)][0]
                act.wait_ge(pj_full, j + 1)
                act.activation(omT[:, :, cols(t)], heads_view(pj[j % 2], 4, ROWS[t]), ACT.Copy).then_inc(pj_act, 1)
            for j in range(-2, 2):
                split_hi(0, 0, j)
            for t in range(TILES):
                pj_read(act, ("w_mem_o", 1, t))
                mean_square(("x2", t), x_tile(t), sq_scr)
            for t in range(TILES):
                act.wait_ge(h3_ready, t + 1)
                act.dma_start(h3_rows[P * t:P * t + ROWS[t], :], h3[0:ROWS[t], t % 2, :]).then_inc(h3_out[t % 2], 16)
                tr_out(("x2", t, 0), hT[:, 0:4, cols(t)], heads_view(tr[1], 4, ROWS[t]))
            for i, v in enumerate((r20[1], r5[3])):
                act.wait_ge(route_arg, i + 1)
                act.activation(v, v, ACT.Exp).then_inc(route_exp, 1)
            def x_hi(e, b):
                for g in range(2):
                    act.wait_ge(xt_done, 2 * e + (g + 1))
                    if not fixed(e, 2):
                        act.wait_ge(pe_unit, 6 * e - 8)
                    act.activation(xgh[:, b, 4 * g:4 * g + 4, :], px[g].rearrange("p (k q) -> p k q", k=4),
                                   ACT.Copy).then_inc(xh_done, 1)

            def silu(e, bank, units):
                act.wait_ge(pe_unit, units)
                if not fixed(e, 1):
                    act.wait_ge(h_done, e)
                act.activation(act_g[:, :], bank[:, :], ACT.Silu).then_inc(sg_done, 1)

            def hid_hi(e, b, units=None):
                act.wait_ge(ht_done, e + 1)
                if not fixed(e, 2):
                    act.wait_ge(pe_unit, 6 * e - 4)
                act.activation(hTh[:, b, :, :], ph[:, :].rearrange("p (k q) -> p k q", k=4), ACT.Copy)\
                    .then_inc(hh_done, 1)

            def y_evac(b, c, units, stores):
                act.wait_ge(pe_unit, units)
                if c == 0 and not fixed(stores, 1):
                    act.wait_ge(y_out[b], stores)
                act.activation(y[:, b, 512 * c:512 * c + 512], py[c], ACT.Copy).then_inc(y_done, 1)

            def step(e, b, last=False):
                first = fixed(e, 1)
                silu(e, pg[b], 2 if first else 6 * e)
                if not last:
                    x_hi(e + 1, 1 - b)
                if not first:
                    y_evac(1 - b, 1, 6 * e + 2, None)
                if last:
                    split_hi(e, b, 3)
                    hid_hi(e, b)
                    y_evac(b, 0, 6 * e + 5, 8 * e - 8 * b)
                    y_evac(b, 1, 6 * e + 6, None)
                    return
                for j in range(3, 9):
                    if j == 6:
                        hid_hi(e, b)
                    split_hi(e, b, j)
                y_evac(b, 0, 6 * e + 7, 8 * e - 8 * b)

            x_hi(0, 0)
            split_hi(0, 0, 2)
            for e in range(2):
                step(e, e)
            with act.Fori(1, E // 2 - 1) as i:
                for b in range(2):
                    step(2 * i + b, b)
            step(E - 2, 0)
            step(E - 1, 1, last=True)
            act.wait_ge(list_ready, 1)
            rounds = act.value_load(extra_i[0:1, MAX_EXTRA:MAX_EXTRA + 1], min_val=0, max_val=MAX_EXTRA)
            with act.If(rounds > 0):
                with act.Fori(0, rounds) as i:
                    r, units = i + E, 6 * i + NMOE
                    act.wait_ge(pe_unit, units)
                    x_hi(r, 0)
                    for k in range(6):
                        if k == 4:
                            silu(r, pg[0], units + 2)
                        act.wait_ge(unit_in[k], 16 * i + 16 * ((NDENSE + NMOE) // RING + 1))
                        if k >= WR:
                            act.wait_ge(pe_unit, units + (k - 3))
                        act.activation(wh[:, k % WR, :], raw[:, k, :], ACT.Copy).then_inc(hi_done, 1)
                    hid_hi(r, 0)
                    y_evac(0, 0, units + 5, 16 * i + 8 * E)
                    y_evac(0, 1, units + 6, None)
            def store_end(t):
                act.wait_ge(out_ready, t + 1)
                out = O[0][0, P * t:P * t + P, :] if t < 4 else O[1][0]
                act.dma_start(out, outb[0:ROWS[t], t % 2, :]).then_inc(out_stored[t % 2], 16)

            for t in range(TILES):
                act.wait_ge(sum_done, t + 1)
                mean_square(("end", t), x_tile(t), junk_end)
                if t:
                    store_end(t - 1)
            store_end(TILES - 1)
            act.wait_ge(stored, 16 * (2 + TILES))
            act.wait_ge(out_stored[0], 16 * 3)
            act.wait_ge(out_stored[1], 16 * 2)

        @block.vector
        def _(dve):
            steps = [0]

            def link(ins):
                steps[0] += 1
                ins.then_inc(dve_step, 1)
                dve.wait_ge(dve_step, steps[0])

            def tt(out, a, b, op):
                return dve.tensor_tensor(out, a, b, op)

            def tr_wait(key):
                dve.wait_ge(tr_full, TR[key][0] + 1)

            def split_lo(e, b, j):
                s4, s6 = (2 + 6 * b + j) % WR, (2 + j) % RING
                dve.wait_ge(hi_done, 6 * e + (3 + j))
                tt(wl[:, s4, :], raw[:, s6, :], wh[:, s4, :].bitcast(F32), ALU.subtract).then_inc(lo_done, 1)

            def gained(key, dst, gain):
                tr_wait(key)
                src = tr[0][:, :].rearrange("p (k q) -> p k q", k=4)[:, :, 0:dst.shape[2]]
                tt(dst, src, gain.unsqueeze(2).to_broadcast([P, 4, dst.shape[2]]), ALU.mult).then_inc(tr_dve, 1)

            dve.wait_ge(params_in, 16 * NPARAMS)
            for i in range(2):
                dve.wait_ge(ms_act, MS_ACT[("x", 4)] + 1)
                for g in range(2):
                    gained(("mem", i, g), memT[:, 4 * g:4 * g + 4, P * i:P * i + P], gains[:, 1, 4 * g:4 * g + 4])
            for t in range(TILES):
                for g in range(2):
                    gained(("x", t, g), hT[:, 4 * g:4 * g + 4, cols(t)], gains[:, 0, 4 * g:4 * g + 4])

            link(tt(lamv[:, 0, :], lamv[:, 0, :], lamv[:, 1, :], ALU.mult))
            link(tt(lamv[:, 2, :], lamv[:, 2, :], lamv[:, 3, :], ALU.mult))
            link(dve.tensor_reduce(lams[:, 0:1], lamv[:, 0, :], AX.X, ALU.add))
            dve.tensor_reduce(lams[:, 1:2], lamv[:, 2, :], AX.X, ALU.add).then_inc(lam_sum, 1)
            link(dve.tensor_scalar(gdiff[:, :], gdiff[:, :], 1.0 - LAM_INIT, None, ALU.mult))
            dve.wait_ge(consts, 14)
            for g in range(4):
                rows, b, w = slice(64 * (g % 2), 64 * (g % 2) + 64), g // 2, float(POOL_WINDOWS[g])
                link(dve.tensor_scalar(ramp[rows, b, :], eidx[rows, :], 1.0, w, ALU.add, ALU.min))
                link(dve.reciprocal(ramp[rows, b, :], ramp[rows, b, :]))
                ins = dve.tensor_scalar(ramp[rows, b, :], ramp[rows, b, :], w, None, ALU.mult)
                if g < 3:
                    link(ins)
                else:
                    ins.then_inc(ramp_ready, 1)

            for t in range(TILES):
                tr_wait(("G", t))
                link(dve.tensor_scalar(gq[:, cols(t)], tr[0][:, 0:ROWS[t]], GK ** -0.5, None, ALU.mult))
                dve.tensor_copy(gk[:, cols(t)], tr[0][:, P:P + ROWS[t]]).then_inc(tr_dve, 1)

            dve.wait_ge(sc_full, SC[("gate",)][0] + 1)
            ins = dve.tensor_scalar(t1[:, :], half(("gate",))[:, 0:TOK], ba[:, 0:1], None, ALU.add)
            ins.then_inc(sc_dve, 1)
            dve.wait_ge(sc_dve, 1)
            dve.scalar_tensor_tensor(out=t2[:, :], in0=t1[:, :], scalar=-1.0, in1=t1[:, :], op0=ALU.mult,
                                     op1=ALU.min).then_inc(gate_arg, 1)
            dve.wait_ge(gate_arg, 1)
            link(dve.tensor_scalar(t1[:, :], t1[:, :], 0.0, None, ALU.min))
            dve.wait_ge(gate_log, 1)
            link(tt(t1[:, :], t1[:, :], t3[:, :], ALU.subtract))
            link(dve.tensor_scalar(t1[:, :], t1[:, :], 1.0 / 16, None, ALU.mult))
            dve.tensor_tensor_scan(cum[:, :], keep, t1[:, :], 0.0, ALU.mult, ALU.add).then_inc(cum_ready, 1)
            dve.wait_ge(cum_ready, 1)
            c3 = cum[:, :].rearrange("p (c n) -> p c n", n=CH)

            def chunks(ap):
                return ap.rearrange("p (c n) -> p c n", n=CH)

            mid = c3[:, :, CH // 2 - 1:CH // 2].to_broadcast([P, NCH, CH])
            last = c3[:, :, CH - 1:CH].to_broadcast([P, NCH, CH])
            link(tt(chunks(t1[:, :]), c3, mid, ALU.subtract))
            link(dve.tensor_scalar(t2[:, :], t1[:, :], -1.0, EXP_CLAMP, ALU.mult, ALU.min))
            dve.tensor_scalar(t1[:, :], t1[:, :], EXP_CLAMP, None, ALU.min).then_inc(decay_arg, 1)
            link(tt(chunks(t4[:, :]), last, c3, ALU.subtract))
            dve.tensor_copy(small[:, 0:1], t4[:, 0:1]).then_inc(decay_arg, 2)
            for i, (buf, by, n) in enumerate(((t3, gq, 2), (t1, gq, 3), (t2, gk, 4), (t4, gk, 5))):
                dve.wait_ge(decay_exp, n)
                tt(buf[:, :], buf[:, :], by[:, :], ALU.mult).then_inc(gla_in, 1)
            dve.wait_ge(lam_exp, 1)
            link(tt(lams[:, 4:5], lams[:, 3:4], lams[:, 2:3], ALU.subtract))
            link(dve.tensor_scalar(lams[:, 5:6], lams[:, 4:5], LAM_INIT, None, ALU.subtract))

            for g, ts in enumerate((slice(0, 4), slice(4, 5))):
                r = P if g == 0 else DEC
                tr_wait(("kend", g))
                dve.tensor_copy(kend[0:r, ts, :], tr[0][0:r, 0:P * (ts.stop - ts.start)].rearrange(
                    "p (t n) -> p t n", n=P)).then_inc(tr_dve, 1)
            dve.wait_ge(state_in, 16 * 8)
            for g in range(3):
                dve.wait_ge(sc_full, SC[("kv", g)][0] + 1)
                cs = range(4 * g, min(4 * g + 4, NCH))
                if g < 2:
                    src = half(("kv", g))[:, :].rearrange("p (o c n) -> p c o n", o=2, n=256)
                    dst = S[:, 1 + cs[0]:1 + cs[-1] + 1, :].rearrange("p (c o) n -> p c o n", o=2)
                    mask = own[:, :].unsqueeze(1).unsqueeze(1).to_broadcast([P, 2, 2, 256])
                else:
                    src, dst, mask = half(("kv", g))[:, 0:256], Ss[:, 1, :], own[:, :]
                tt(dst, src, mask, ALU.mult).then_inc(sc_dve, 1)
                dve.wait_ge(sc_dve, SC[("kv", g)][2] + 1)
            for c in range(NCH):
                old, new = (S[:, c, :], S[:, c + 1, :]) if c < NCH - 1 else (Ss[:, 0, :], Ss[:, 1, :])
                ins = dve.scalar_tensor_tensor(out=new, in0=old, scalar=dec_end[:, c:c + 1], in1=new, op0=ALU.mult,
                                               op1=ALU.add)
                if c < NCH - 1:
                    link(ins)
                else:
                    ins.then_inc(states_ready, 1)

            def mask_scores(t):
                r = ROWS[t]
                dve.wait_ge(sc_full, SC[("att", t)][0] + 1)
                if t >= 2:
                    dve.wait_ge(pj_full, PJ[("gla_o", t - 2)][0] + 1)
                src = half(("att", t))[0:r, 0:GH * r].rearrange("p (h q) -> p h q", h=GH)
                dst = attm[0:r, t % 2, :].rearrange("p (h q) -> p h q", h=GH)[:, :, 0:r]
                tt(dst, src, causal[0:r, 0:r].unsqueeze(1).to_broadcast([r, GH, r]), ALU.mult).then_inc(sc_dve, 1)

            def head_norm(key, n, sq, width, dst, gain_bc, ready, free_key):
                t, r, j = key[1], ROWS[key[1]], PJ[free_key][0]
                rows, i, cs = stat_of(key)
                hv = lambda ap: ap.rearrange("p (h v) -> p h v", h=4)
                dve.wait_ge(sq_act, n + 1)
                dve.tensor_reduce(stat[rows, i, cs], hv(sq[0:r, 0:width]), AX.X, ALU.add).then_inc(ms_dve, 1)
                dve.wait_ge(rs_ready, RS[key] + 1)
                if t >= 2:
                    dve.wait_ge(tr_full, TR[({"gla": "mix_g", "diff": "mix_d"}[key[0]], t - 2)][0] + 1)
                w = width // 4
                tt(hv(dst), hv(pj[j % 2][0:r, 0:width]), rs[rows, i, cs].unsqueeze(2).to_broadcast([r, 4, w]),
                   ALU.mult).then_inc(pj_dve, 1)
                dve.wait_ge(pj_dve, PJ[free_key][2] + 1)
                tt(hv(dst), hv(dst), gain_bc, ALU.mult).then_inc(ready, 1)

            def q_by_head(t):
                r = ROWS[t]
                if t >= 2:
                    dve.wait_ge(sc_full, SC[("att", t - 2)][0] + 1)
                tt(q_heads[t % 2][:, 0:GH * r].rearrange("p (h q) -> p h q", h=GH),
                   t1[:, cols(t)].unsqueeze(1).to_broadcast([P, GH, r]),
                   own[:, :].rearrange("p (h v) -> p h v", h=GH)[:, :, 0:1].to_broadcast([P, GH, r]), ALU.mult)\
                    .then_inc(qb_ready, 1)

            dve.wait_ge(gla_in, 4)
            q_by_head(0)
            q_by_head(1)
            mask_scores(0)
            dve.wait_ge(glu_ready, TILES)
            for t in range(TILES):
                if t + 2 < TILES:
                    q_by_head(t + 2)
                if t + 1 < TILES:
                    mask_scores(t + 1)
                r = ROWS[t]
                head_norm(("gla", t), t, gla_sq, 256, mixg[0:r, t % 2, :],
                          zR[0:r, t, 0:256].rearrange("p (h v) -> p h v", h=GH), mixg_ready, ("gla_o", t))

            def row_max(s):
                t, h = STEPS[s]
                r = ROWS[t]
                dve.wait_ge(sc_full, SC[last_score(t, h)][0] + 1)
                link(dve.tensor_reduce(nmax[0:r, s % 2, :], maps(t, h, keys_of(t)), AX.X, ALU.max))
                dve.tensor_scalar(nmax[0:r, s % 2, :], nmax[0:r, s % 2, :], -DH ** -0.5, None, ALU.mult)\
                    .then_inc(max_ready, 1)

            def diff_norm(t):
                r = ROWS[t]
                head_norm(("diff", t), TILES + t, diff_sq, 512, mixd[0:r, t % 2, :],
                          gdiff[0:r, :].unsqueeze(1).to_broadcast([r, 4, P]), mixd_ready, ("diff_o", t))

            row_max(0)
            for s, (t, h) in enumerate(STEPS):
                r, nk, b = ROWS[t], keys_of(t), s % 2
                if s + 1 < len(STEPS):
                    row_max(s + 1)
                sc_read(dve, last_score(t, h))
                link(dve.reciprocal(recip[0:r, b, :], psum_[0:r, b, :]))
                link(tt(recip[0:r, b, 1:2], recip[0:r, b, 1:2], lams[0:r, 5:6], ALU.mult))
                link(dve.tensor_scalar(prob[0:r, b, 1, 0:nk], prob[0:r, b, 1, 0:nk], recip[0:r, b, 1:2], None, ALU.mult))
                dve.scalar_tensor_tensor(out=prob[0:r, b, 0, 0:nk], in0=prob[0:r, b, 0, 0:nk], scalar=recip[0:r, b, 0:1],
                                         in1=prob[0:r, b, 1, 0:nk], op0=ALU.mult, op1=ALU.add).then_inc(pd_ready, 1)
                if TR[("pd", t, h, 0)][1] == "V":
                    tr_wait(("pd", t, h, 0))
                    nb = min(key_blocks(t), 4)
                    dve.tensor_copy(pdT[:, b, 0:nb, 0:r], tr[0][:, 0:P * nb].rearrange("p (b q) -> p b q", q=P)[:, :, 0:r])\
                        .then_inc(tr_dve, 1)
                if h == HEADS - 1:
                    diff_norm(t)

            dve.wait_ge(x_again, 32)

            def add_rows(name, after=lambda c, t: None):
                for c in range(2):
                    for t in range(TILES):
                        j, r = PJ[(name, c, t)][0], ROWS[t]
                        dve.wait_ge(pj_full, j + 1)
                        dst = X[0:r, t, 512 * c:512 * c + 512]
                        tt(dst, pj[j % 2][0:r, :], dst, ALU.add).then_inc(pj_dve, 1)
                        after(c, t)

            add_rows("w_out")
            for t in range(TILES):
                for g in range(2):
                    gained(("x1", t, g), hT[:, 4 * g:4 * g + 4, cols(t)], gains[:, 2, 4 * g:4 * g + 4])

            def q_and_max(t):
                r = ROWS[t]
                tr_wait(("mq", t))
                dve.tensor_copy(qmT[:, t % 2, :, 0:r], tr[0][:, :].rearrange("p (h q) -> p h q", h=MH)[:, :, 0:r])\
                    .then_inc(tr_dve, 1)
                dve.wait_ge(sc_full, SC[("mem", t)][0] + 1)
                link(dve.tensor_reduce(nmaxm[0:r, t % 2, :], half(("mem", t))[0:r, :].rearrange("p (h k) -> p h k", h=MH),
                                       AX.X, ALU.max))
                dve.tensor_scalar(nmaxm[0:r, t % 2, :], nmaxm[0:r, t % 2, :], -P ** -0.5, None, ALU.mult)\
                    .then_inc(maxm_ready, 1)

            q_and_max(0)
            for t in range(TILES):
                r = ROWS[t]
                if t + 1 < TILES:
                    q_and_max(t + 1)
                sc_read(dve, ("mem", t))
                link(dve.reciprocal(nrec[0:r, t % 2, :], psumm[0:r, t % 2, :]))
                tt(probm[0:r, t % 2, :, :], probm[0:r, t % 2, :, :],
                   nrec[0:r, t % 2, :].unsqueeze(2).to_broadcast([r, MH, MEM]), ALU.mult).then_inc(pm_ready, 1)
                if t >= 2:
                    dve.wait_ge(pj_full, PJ[("mem_o", t - 2)][0] + 1)
                tr_wait(("pm", t, 1))
                dve.tensor_copy(pmT[:, t % 2, 4:8, 0:r], tr[0][:, :].rearrange("p (h q) -> p h q", h=4)[:, :, 0:r])\
                    .then_inc(tr_dve, 1)
            add_rows("w_mem_o", lambda c, t: split_lo(0, 0, t - 2) if c == 0 and t < 4 else None)
            dve.wait_ge(gffn_in, 16)
            for t in range(TILES):
                r = ROWS[t]
                if t >= 2:
                    dve.wait_ge(h3_out[t % 2], 16 * (t // 2))
                    dve.wait_ge(tr_full, TR[("x2", t - 2, 1)][0] + 1)
                dve.wait_ge(rs_ready, RS[("x2", t)] + 1)
                dve.scalar_tensor_tensor(out=h3[0:r, t % 2, :], in0=x_tile(t), scalar=rs[0:r, 3, t:t + 1],
                                         in1=gffn[0:r, :], op0=ALU.mult, op1=ALU.mult).then_inc(h3_ready, 1)
                tr_wait(("x2", t, 1))
                dve.tensor_copy(hT[:, 4:8, cols(t)], tr[0][:, :].rearrange("p (k q) -> p k q", k=4)[:, :, 0:r])\
                    .then_inc(tr_dve, 1)

            T5 = [P, TILES]
            dve.wait_ge(pj_full, PJ[("router",)][0] + 1)
            link(dve.memset(lg, 0.0))
            jb = pj[PJ[("router",)][0] % 2]
            link(tt(lg[:, 0:4, :], jb[:, 0:80].rearrange("p (t n) -> p t n", t=4),
                    br[:, :].unsqueeze(1).to_broadcast([P, 4, 20]), ALU.add))
            tt(lg[0:DEC, 4, :], jb[0:DEC, 80:100], br[0:DEC, :], ALU.add).then_inc(pj_dve, 1)
            dve.wait_ge(pj_dve, PJ[("router",)][2] + 1)

            def bc(ap, n):
                return ap.unsqueeze(len(ap.shape)).to_broadcast(list(ap.shape) + [n])

            first = eidx[:, 0:4]

            def first_max(v, m, hot):
                link(dve.tensor_reduce(m, v, AX.X, ALU.max))
                link(tt(hot, v, bc(m, 4), ALU.is_equal))
                link(tt(hot, hot, rank4[:, :].unsqueeze(1).to_broadcast([P, TILES, 4]), ALU.mult))
                link(dve.tensor_reduce(r5[4], hot, AX.X, ALU.max))
                link(tt(hot, hot, bc(r5[4], 4), ALU.is_equal))

            link(dve.tensor_scalar(rank4, first, -1.0, 4.0, ALU.mult, ALU.add))
            first_max(lg[:, :, 0:4], r5[0], r20[0])
            tt(r20[1], lg[:, :, 0:4], bc(r5[0], 4), ALU.subtract).then_inc(route_arg, 1)
            link(tt(r80[0].rearrange("p t (g i) -> p t g i", g=4), lg[:, :, 4:20].rearrange("p t (g i) -> p t g i", g=4),
                    bc(r20[0], 4), ALU.mult))
            link(dve.tensor_reduce(r20[2], r80[0].rearrange("p t (g i) -> p t i g", g=4), AX.X, ALU.add))
            first_max(r20[2], r5[1], r20[3])
            link(dve.scalar_tensor_tensor(out=r20[4], in0=r20[3], scalar=-1e30, in1=r20[2], op0=ALU.mult, op1=ALU.add))
            first_max(r20[4], r5[2], r20[5])
            tt(r5[3], r5[2], r5[1], ALU.subtract).then_inc(route_arg, 1)
            for i, hot in ((1, r20[3]), (2, r20[5])):
                for g in range(4):
                    ins = tt(r80[i][:, :, 4 * g:4 * g + 4], hot, bc(r20[0][:, :, g], 4), ALU.mult)
                link(ins)
            link(tt(chosen[:, :, :], r80[1], r80[2], ALU.add))
            dve.memset(chosen[DEC:P, 4, :], 0.0).then_inc(chosen_ready, 1)
            dve.wait_ge(route_exp, 1)
            link(dve.tensor_reduce(r5[4], r20[1], AX.X, ALU.add))
            link(dve.reciprocal(r5[4], r5[4]))
            dve.wait_ge(route_exp, 2)
            link(dve.tensor_scalar(r5[5], r5[3], 1.0, None, ALU.add))
            link(dve.reciprocal(r5[5], r5[5]))
            link(tt(gate[:, 0, :], r5[4], r5[5], ALU.mult))
            link(tt(gate[:, 1, :], gate[:, 0, :], r5[3], ALU.mult))
            jb = pj[PJ[("pos",)][0] % 2]
            pos, cnt = jb[:, 0:80].rearrange("p (t e) -> p t e", e=E), jb[:, 80:96]
            dve.wait_ge(pj_full, PJ[("pos",)][0] + 1)
            link(dve.tensor_scalar(more, cnt, float(P), None, ALU.is_gt))
            for q in range(2, 5):
                link(dve.scalar_tensor_tensor(out=more, in0=cnt, scalar=float(P * q), in1=more, op0=ALU.is_gt, op1=ALU.add))
            link(dve.memset(ones16, 1.0))
            link(dve.tensor_tensor_scan(upto, ones16, more, 0.0, ALU.mult, ALU.add))
            link(tt(base, upto, more, ALU.subtract))
            link(dve.tensor_scalar(base, base, float(P), float(P * E - P), ALU.mult, ALU.add))
            link(tt(r80[3], pos, base.unsqueeze(1).to_broadcast([P, TILES, E]), ALU.add))
            link(dve.scalar_tensor_tensor(out=r80[0], in0=pos, scalar=float(E),
                                          in1=eidx[:, :].unsqueeze(1).to_broadcast([P, TILES, E]), op0=ALU.mult,
                                          op1=ALU.add))
            link(tt(r80[3], r80[3], r80[0], ALU.subtract))
            dve.scalar_tensor_tensor(out=r80[3], in0=pos, scalar=P - 0.5, in1=r80[3], op0=ALU.is_gt, op1=ALU.mult)\
                .then_inc(pj_dve, 1)
            dve.wait_ge(pj_dve, PJ[("pos",)][2] + 1)
            link(tt(r80[0], r80[0], r80[3], ALU.add))
            for i in (1, 2):
                link(tt(r80[i], r80[i], r80[0], ALU.mult))
                link(dve.tensor_reduce(r5[6], r80[i], AX.X, ALU.add))
                ins = dve.tensor_copy(slot_i[:, i - 1, :], r5[6])
                if i == 1:
                    link(ins)
            ins.then_inc(slots_ready, 1)
            link(tt(r8x16, upto[0:1, :].unsqueeze(1).to_broadcast([1, MAX_EXTRA, E]),
                    eidx[0:1, 0:MAX_EXTRA].unsqueeze(2).to_broadcast([1, MAX_EXTRA, E]), ALU.is_le))
            link(dve.tensor_reduce(extra_f, r8x16, AX.X, ALU.add))
            link(dve.tensor_copy(extra_i[:, 0:MAX_EXTRA], extra_f))
            dve.tensor_copy(extra_i[:, MAX_EXTRA:MAX_EXTRA + 1], upto[0:1, E - 1:E]).then_inc(list_ready, 1)
            def x_lo(e, b):
                for g in range(2):
                    dve.wait_ge(xh_done, 2 * e + (g + 1))
                    tt(xgl[:, b, 4 * g:4 * g + 4, :], px[g].rearrange("p (k q) -> p k q", k=4),
                       xgh[:, b, 4 * g:4 * g + 4, :].bitcast(F32), ALU.subtract).then_inc(xl_done, 1)

            def hidden(e, units):
                dve.wait_ge(sg_done, e + 1)
                dve.wait_ge(pe_unit, units)
                if not fixed(e, 1):
                    dve.wait_ge(ht_done, e)
                tt(hid[:, :], act_g[:, :], pu[:, :], ALU.mult).then_inc(h_done, 1)

            def hid_lo(e, b):
                dve.wait_ge(hh_done, e + 1)
                tt(hTl[:, b, :, :], ph[:, :].rearrange("p (k q) -> p k q", k=4),
                   hTh[:, b, :, :].bitcast(F32), ALU.subtract).then_inc(hl_done, 1)

            def step(e, b, last=False):
                if not last:
                    x_lo(e + 1, 1 - b)
                if last:
                    split_lo(e, b, 3)
                    hidden(e, 6 * e + 4)
                    hid_lo(e, b)
                    return
                for j in range(3, 9):
                    if j == 5:
                        hidden(e, 6 * e + 4)
                    if j == 6:
                        hid_lo(e, b)
                    split_lo(e, b, j)

            x_lo(0, 0)
            split_lo(0, 0, 2)
            for e in range(2):
                step(e, e)
            with dve.Fori(1, E // 2 - 1) as i:
                for b in range(2):
                    step(2 * i + b, b)
            step(E - 2, 0)
            step(E - 1, 1, last=True)
            dve.wait_ge(list_ready, 1)
            rounds = dve.value_load(extra_i[0:1, MAX_EXTRA:MAX_EXTRA + 1], min_val=0, max_val=MAX_EXTRA)
            with dve.If(rounds > 0):
                with dve.Fori(0, rounds) as i:
                    r, units = i + E, 6 * i + NMOE
                    x_lo(r, 0)
                    for k in range(6):
                        if k == 4:
                            hidden(r, units + 4)
                        dve.wait_ge(hi_done, units + (k + 1))
                        tt(wl[:, k % WR, :], raw[:, k, :], wh[:, k % WR, :].bitcast(F32), ALU.subtract).then_inc(lo_done, 1)
                    hid_lo(r, 0)
            for t in range(TILES + 1):
                if t < TILES:
                    r = ROWS[t]
                    dve.wait_ge(yg_in[t % 2], 32 * (t // 2 + 1))
                    link(dve.scalar_tensor_tensor(out=x_tile(t), in0=yg[0:r, t % 2, 0, :], scalar=gate[0:r, 0, t:t + 1],
                                                  in1=x_tile(t), op0=ALU.mult, op1=ALU.add))
                    dve.scalar_tensor_tensor(out=x_tile(t), in0=yg[0:r, t % 2, 1, :], scalar=gate[0:r, 1, t:t + 1],
                                             in1=x_tile(t), op0=ALU.mult, op1=ALU.add).then_inc(sum_done, 1)
                if t:
                    u, r = t - 1, ROWS[t - 1]
                    dve.wait_ge(rs_ready, RS[("end", u)] + 1)
                    dve.wait_ge(gfin_in, 16)
                    if u >= 2:
                        dve.wait_ge(out_stored[u % 2], 16 * (u // 2))
                    dve.scalar_tensor_tensor(out=outb[0:r, u % 2, :], in0=x_tile(u), scalar=rs[0:r, 4, u:u + 1],
                                             in1=gfin[0:r, :], op0=ALU.mult, op1=ALU.mult).then_inc(out_ready, 1)

        @block.tensor
        def _(pe):
            placed = {"pj": 0, "tr": 0, "sc": 0}

            def claim(kind, numbers, keys, key, act_sem, dve_sem):
                n = numbers[key][0]
                assert n == placed[kind], (key, n, placed[kind])
                placed[kind] += 1
                if kind == "tr":
                    prev = [k for k in keys[:n] if numbers[k][1] == numbers[key][1]][-1:]
                else:
                    prev = keys[n - 2:n - 1] if n >= 2 else []
                for k in prev:
                    read_out(pe, numbers, act_sem, dve_sem, k)
                return n

            def mm(out, lhsT, rhs, start, stop):
                return pe.matmul(out, lhsT, rhs, start=start, stop=stop, skip_group_check=True)

            def transposes(key, blocks):
                claim("tr", TR, TR_KEYS, key, tr_act, tr_dve)
                bank = tr[0] if TR[key][1] == "V" else tr[1]
                for c0, src in blocks:
                    r, n = src.shape
                    ins = pe.transpose(bank[0:n, c0:c0 + r], src, ident[0:r, 0:r])
                ins.then_inc(tr_full, 1)

            def unit_ready(n):
                pe.wait_ge(unit_in[n % RING], 16 * (n // RING + 1))

            def unit(n, w):
                return raw[:, n % RING, 0:4 * w].rearrange("p (k w) -> p k w", k=4)

            def project(key, lhs, units, w, r):
                j = claim("pj", PJ, PJ_KEYS, key, pj_act, pj_dve)
                for n in units:
                    unit_ready(n)
                nk = 4 * len(units)
                for k in range(nk):
                    ins = mm(pj[j % 2][0:r, 0:w], lhs(k), unit(units[k // 4], w)[:, k % 4, :], k == 0, k == nk - 1)
                ins.then_inc(pj_full, 1)

            def h_block(t):
                return lambda k: hT[:, k, cols(t)]

            pe.wait_ge(consts, 1)
            pe.wait_ge(mem_in, 16)
            for i in range(2):
                for g in range(2):
                    transposes(("mem", i, g), [(P * k, memsrc[:, i, P * (4 * g + k):P * (4 * g + k) + P]) for k in range(4)])
            for n, b in enumerate(("memk", "memv")):
                for i in range(2):
                    tr_read(pe, ("mem", i, 1))
                    project((b, i), lambda k: memT[:, k, P * i:P * i + P], (2 * n, 2 * n + 1), 512, P)
            for i in range(2):
                pj_read(pe, ("memk", i))
                transposes(("mk", i), [(P * h, rowbuf[:, i, P * h:P * h + P]) for h in range(MH)])
            for t in range(TILES):
                pe.wait_ge(x_in[t], 16)
                for g in range(2):
                    transposes(("x", t, g), [(P * k, x_tile(t)[:, P * (4 * g + k):P * (4 * g + k) + P]) for k in range(4)])

            def rows_T(b, t, nb):
                pj_read(pe, (b, t))
                n = ROW_AT[(b, t)]
                transposes((b, t), [(P * k, rowbuf[0:ROWS[t], n % 2, P * k:P * k + P]) for k in range(nb)])

            def in_block(b, nb):
                for t in range(TILES):
                    tr_read(pe, ("x", t, 1))
                    project((b, t), h_block(t), BLOCK_UNITS[b], WIDTH[b], ROWS[t])
                    if t and nb:
                        rows_T(b, t - 1, nb)
                if nb:
                    rows_T(b, TILES - 1, nb)

            in_block("G", 2)
            in_block("R", 0)
            pj_read(pe, ("R", 4))
            transposes(("R", 0), [(P * t, zR[:, t, 256:272]) for t in range(4)])
            transposes(("R", 1), [(0, zR[0:DEC, 4, 256:272])])
            tr_read(pe, ("R", 1))
            claim("sc", SC, SC_KEYS, ("gate",), sc_act, sc_dve)
            mm(half(("gate",))[:, 0:512], wa2[:, :], gaT[:, 0:512], True, True)
            mm(half(("gate",))[:, 512:TOK], wa2[:, :], gaT[:, 512:TOK], True, True).then_inc(sc_full, 1)
            in_block("U", 2)
            pe.wait_ge(hist_in, 16)
            transposes(("hist",), [(P * b, hist[:, P * b:P * b + P]) for b in range(2)])
            in_block("K", 4)
            in_block("V", 0)
            pe.wait_ge(gla_in, 4)
            for g, ts in enumerate((range(4), range(4, 5))):
                transposes(("kend", g), [(P * (t - ts[0]), t4[:, cols(t)]) for t in ts])
            for g in range(3):
                claim("sc", SC, SC_KEYS, ("kv", g), sc_act, sc_dve)
                if g == 0:
                    tr_read(pe, ("kend", 1))
                for c in range(4 * g, min(4 * g + 4, NCH)):
                    rows = slice(CH * (c % 2), CH * (c % 2) + CH)
                    place = 512 * (c % 2) + 256 * (c % 4 // 2)
                    ins = mm(half(("kv", g))[:, place:place + 256], kend[rows, c // 2, :],
                             gv[rows, c // 2, :], True, True)
                ins.then_inc(sc_full, 1)
            in_block("Q", 4)

            def gla_scores(t):
                r = ROWS[t]
                claim("sc", SC, SC_KEYS, ("att", t), sc_act, sc_dve)
                pe.wait_ge(qb_ready, t + 1)
                mm(half(("att", t))[0:r, 0:GH * r], t2[:, cols(t)], q_heads[t % 2][:, 0:GH * r], True, True)\
                    .then_inc(sc_full, 1)

            def gla_out(t):
                r, j = ROWS[t], claim("pj", PJ, PJ_KEYS, ("gla_o", t), pj_act, pj_dve)
                for u in range(r // CH):
                    c = 2 * t + u
                    state = S[:, c, :] if t < 4 else Ss[:, 0, :]
                    mm(pj[j % 2][CH * u:CH * u + CH, 0:256], t3[:, CH * c:CH * c + CH], state, True, False)
                read_out(pe, SC, sc_act, sc_dve, ("att", t))
                for h in range(GH):
                    ins = mm(pj[j % 2][0:r, GV * h:GV * h + GV], attm[0:r, t % 2, P * h:P * h + r],
                             gv[0:r, t, GV * h:GV * h + GV], False, h == GH - 1)
                ins.then_inc(pj_full, 1)

            def mixg_T(t):
                pe.wait_ge(mixg_ready, t + 1)
                transposes(("mix_g", t), [(P * b, mixg[0:ROWS[t], t % 2, P * b:P * b + P]) for b in range(2)])

            gla_scores(0)
            pe.wait_ge(states_ready, 1)
            for t in range(TILES):
                if t + 1 < TILES:
                    gla_scores(t + 1)
                gla_out(t)
                if t:
                    mixg_T(t - 1)
            mixg_T(TILES - 1)
            pe.wait_ge(kp_in, 16)
            for b in range(4):
                transposes(("kp", b), [(P * h, kprow[:, b, P * h:P * h + P]) for h in range(HEADS)])
            pe.wait_ge(pool_ready, 4)
            pe.wait_ge(state_in, 16 * 8)
            for b in range(2):
                for name, w, c0 in (("pool", 512, 16), ("pool_s", DEC, S0)):
                    j = claim("pj", PJ, PJ_KEYS, (name, b), pj_act, pj_dve)
                    mm(pj[j % 2][:, 0:w], poolw[:, b, :], ext[:, b, c0:c0 + w], True, True).then_inc(pj_full, 1)

            tr_read(pe, ("K", 4))
            tr_read(pe, ("Q", 4))
            tr_read(pe, ("kp", 3))
            pj_read(pe, ("V", 4))
            pe.wait_ge(vp_in, 16)

            def diff_scores(s):
                t, h = STEPS[s]
                r, nk = ROWS[t], keys_of(t)
                for m in (0, 1) if t < 4 else (1, 0):
                    ms, q = slice(DH * m, DH * m + DH), qT[DH * m:DH * m + DH, h, cols(t)]
                    if t < 4:
                        key = ("diff", t, h)
                        if m == 0:
                            claim("sc", SC, SC_KEYS, key, sc_act, sc_dve)
                        out = half(key)[:, 512 * m:512 * m + 512]
                        mm(out[:, 0:nk], q, kT[ms, h, 0:nk], True, False)
                        ins = mm(out[:, nk - CH:nk], hide_q[DH * m:DH * m + 1, :], hide_k[DH * m:DH * m + 1, :], False, True)
                        if m == 1:
                            ins.then_inc(sc_full, 1)
                    else:
                        claim("sc", SC, SC_KEYS, ("diff", t, h, m), sc_act, sc_dve)
                        mm(sc[0:r, 1024 * m:1024 * m + PAST], q, kpT[ms, h, :], True, True)
                        mm(sc[0:r, 1024 * m + PAST:1024 * m + nk], q, kT[ms, h, SEQ:TOK], True, True).then_inc(sc_full, 1)

            def mixd_T(t):
                pe.wait_ge(mixd_ready, t + 1)
                transposes(("mix_d", t), [(P * b, mixd[0:ROWS[t], t % 2, P * b:P * b + P]) for b in range(4)])

            pe.wait_ge(consts, 11)
            diff_scores(0)
            for s, (t, h) in enumerate(STEPS):
                r, nb, b = ROWS[t], key_blocks(t), s % 2
                if s + 1 < len(STEPS):
                    diff_scores(s + 1)
                pe.wait_ge(pd_ready, s + 1)
                transposes(("pd", t, h, 0), [(P * k, prob[0:r, b, 0, P * k:P * k + P]) for k in range(min(nb, 4))])
                if t == 4:
                    transposes(("pd", t, h, 1), [(0, prob[0:r, b, 0, PAST:PAST + DEC])])
                if h == 0:
                    j = claim("pj", PJ, PJ_KEYS, ("diff_o", t), pj_act, pj_dve)
                tr_read(pe, ("pd", t, h, 0))
                if t == 4:
                    tr_read(pe, ("pd", t, h, 1))
                hs = slice(DV * h, DV * h + DV)
                for k in range(nb):
                    if t < 4:
                        ins = mm(pj[j % 2][0:r, hs], pdT[:, b, k, 0:r], vrow[:, k, hs], k == 0, k == nb - 1)
                    elif k < 4:
                        ins = mm(pj[j % 2][0:r, hs], pdT[:, b, k, 0:r], vp[:, k, hs], k == 0, False)
                    else:
                        ins = mm(pj[j % 2][0:r, hs], pdT[0:DEC, b, 4, 0:r], vrow[0:DEC, 4, hs], False, True)
                if h == HEADS - 1:
                    ins.then_inc(pj_full, 1)
                if h == 0 and t:
                    mixd_T(t - 1)
            mixd_T(TILES - 1)

            tr_read(pe, ("mix_g", 4))
            pj_read(pe, ("pool_s", 1))
            for c in range(2):
                for t in range(TILES):
                    tr_read(pe, ("mix_d", t))
                    project(("w_out", c, t), lambda k: mixT[:, k, cols(t)], (WO_UNIT + 2 * c, WO_UNIT + 2 * c + 1), 512, ROWS[t])
            for t in range(TILES):
                pj_read(pe, ("w_out", 1, t))
                for g in range(2):
                    transposes(("x1", t, g), [(P * k, x_tile(t)[:, P * (4 * g + k):P * (4 * g + k) + P]) for k in range(4)])

            def mem_scores(t):
                r = ROWS[t]
                tr_read(pe, ("x1", t, 1))
                project(("mem_q", t), h_block(t), (MQ_UNIT, MQ_UNIT + 1), 512, r)
                pj_read(pe, ("mem_q", t))
                transposes(("mq", t), [(P * h, rowbuf[0:r, t % 2, P * h:P * h + P]) for h in range(MH)])
                if t == 4:
                    pe.wait_ge(cmk_in, 16)
                    for b in range(2):
                        transposes(("cmk", b), [(P * h, cmkrow[:, b, P * h:P * h + P]) for h in range(MH)])
                    tr_read(pe, ("cmk", 1))
                    pe.wait_ge(cmv_in, 16)
                tr_read(pe, ("mq", t))
                claim("sc", SC, SC_KEYS, ("mem", t), sc_act, sc_dve)
                for h in range(MH):
                    ins = mm(half(("mem", t))[0:r, MEM * h:MEM * h + MEM], qmT[:, t % 2, h, 0:r],
                             (mkT if t < 4 else cmkT)[:, h, :], True, True)
                ins.then_inc(sc_full, 1)

            mem_scores(0)
            for t in range(TILES):
                r = ROWS[t]
                if t + 1 < TILES:
                    mem_scores(t + 1)
                pe.wait_ge(pm_ready, t + 1)
                for g in range(2):
                    transposes(("pm", t, g), [(P * (2 * hh + k), probm[0:r, t % 2, 2 * g + hh, P * k:P * k + P])
                                              for hh in range(2) for k in range(2)])
                j = claim("pj", PJ, PJ_KEYS, ("mem_o", t), pj_act, pj_dve)
                for g in range(2):
                    tr_read(pe, ("pm", t, g))
                for h in range(MH):
                    for k in range(2):
                        ins = mm(pj[j % 2][:, P * h:P * h + r], (mv if t < 4 else cmv)[:, k, P * h:P * h + P],
                                 pmT[:, t % 2, 2 * h + k, 0:r], k == 0, k == 1)
                ins.then_inc(pj_full, 1)
            for c in range(2):
                for t in range(TILES):
                    pj_read(pe, ("mem_o", t))
                    project(("w_mem_o", c, t), lambda k: omT[:, k, cols(t)], (MO_UNIT + c,), 512, ROWS[t])
            for t in range(TILES):
                pe.wait_ge(h3_ready, t + 1)
                for g in range(2):
                    transposes(("x2", t, g), [(P * k, h3[0:ROWS[t], t % 2, P * (4 * g + k):P * (4 * g + k) + P]) for k in range(4)])
            j = claim("pj", PJ, PJ_KEYS, ("router",), pj_act, pj_dve)
            for t in range(TILES):
                for g in range(2):
                    tr_read(pe, ("x2", t, g))
                for k in range(KB):
                    ins = mm(pj[j % 2][0:ROWS[t], 20 * t:20 * t + 20], hT[:, k, cols(t)], wr[:, k, :], k == 0, k == KB - 1)
            ins.then_inc(pj_full, 1)
            pe.wait_ge(chosen_ready, 1)
            j = claim("pj", PJ, PJ_KEYS, ("pos",), pj_act, pj_dve)
            for t in range(TILES + 1):
                for i in range(min(t + 1, TILES)):
                    ins = mm(pj[j % 2][:, E * t:E * t + E], (before if i == t else onesb)[:, :], chosen[:, i, :],
                             i == 0, i == min(t, TILES - 1))
            ins.then_inc(pj_full, 1)
            def x_turn(e, buf, landed):
                pe.wait_ge(xg_in[buf], landed)
                for g in range(2):
                    if not fixed(e, 1):
                        pe.wait_ge(xl_done, 2 * e + (g - 1))
                    for k in range(4):
                        ins = pe.transpose(px[g][:, P * k:P * k + P], xg[:, buf, P * (4 * g + k):P * (4 * g + k) + P],
                                           ident[:, :])
                    ins.then_inc(xt_done, 1)

            def split_mm(out, hi, lo, slot, start, stop):
                for k in range(4):
                    w = slice(512 * k, 512 * k + 512)
                    mm(out, hi[:, k, :], wh[:, slot, w], start and k == 0, False)
                    mm(out, hi[:, k, :], wl[:, slot, w], False, False)
                    ins = mm(out, lo[:, k, :], wh[:, slot, w], False, stop and k == 3)
                ins.then_inc(pe_unit, 1)

            def gate_or_up(bank, buf, part, slot, split):
                pe.wait_ge(lo_done, split)
                split_mm(bank[:, :], xgh[:, buf, 4 * part:4 * part + 4, :], xgl[:, buf, 4 * part:4 * part + 4, :], slot,
                         part == 0, part == 1)

            def hid_turn(e):
                pe.wait_ge(h_done, e + 1)
                if not fixed(e, 1):
                    pe.wait_ge(hl_done, e)
                for k in range(4):
                    ins = pe.transpose(ph[:, P * k:P * k + P], hid[:, P * k:P * k + P], ident[:, :])
                ins.then_inc(ht_done, 1)

            def down(e, c, buf, slot, split):
                if c == 0:
                    pe.wait_ge(hl_done, e + 1)
                if not fixed(e, 1):
                    pe.wait_ge(y_done, 2 * e + (c - 1))
                pe.wait_ge(lo_done, split)
                split_mm(py[c], hTh[:, buf, :, :], hTl[:, buf, :, :], slot, True, True)

            def step(e, b, last=False):
                s4 = lambda j: (2 + 6 * b + j) % WR
                first = fixed(e, 1)
                if not last:
                    x_turn(e + 1, 1 - b, 8 * e + (16 if b == 0 else 24))
                if not first:
                    pe.wait_ge(h_done, e)
                for part in range(2):
                    gate_or_up(pu, b, part, s4(part), 6 * e + (3 + part))
                if not last:
                    pe.wait_ge(xl_done, 2 * e + 4)
                    if not first:
                        pe.wait_ge(sg_done, e)
                    for part in range(2):
                        gate_or_up(pg[1 - b], 1 - b, part, s4(2 + part), 6 * e + (5 + part))
                        if part == 0:
                            hid_turn(e)
                else:
                    hid_turn(e)
                for c in range(2):
                    j = (2 if last else 4) + c
                    down(e, c, b, s4(j), 6 * e + (3 + j))

            x_turn(0, 0, 16)
            pe.wait_ge(xl_done, 2)
            pe.wait_ge(pj_dve, PJ[("pos",)][2] + 1)
            for part in range(2):
                gate_or_up(pg[0], 0, part, part, part + 1)
            for e in range(2):
                step(e, e)
            with pe.Fori(1, E // 2 - 1) as i:
                for b in range(2):
                    step(2 * i + b, b)
            step(E - 2, 0)
            step(E - 1, 1, last=True)
            pe.wait_ge(list_ready, 1)
            rounds = pe.value_load(extra_i[0:1, MAX_EXTRA:MAX_EXTRA + 1], min_val=0, max_val=MAX_EXTRA)
            with pe.If(rounds > 0):
                with pe.Fori(0, rounds) as i:
                    r, u = i + E, 6 * i + NMOE
                    x_turn(r, 0, 16 * i + (8 * E + 16))
                    pe.wait_ge(xl_done, 2 * i + (2 * E + 2))
                    for j, bank in ((0, pg[0]), (2, pu)):
                        for part in range(2):
                            gate_or_up(bank, 0, part, (j + part) % WR, u + (j + part + 1))
                    hid_turn(r)
                    for c in range(2):
                        down(r, c, 0, (4 + c) % WR, u + (5 + c))


_INS = ['x_prompt', 'x_sample', 'mem_prompt', 'cache_diff_k', 'cache_diff_v', 'cache_mem_k', 'cache_mem_v',
        'state_gla', 'state_pool', 'norm_mix_g', 'w_in', 'w_gla_a2', 'b_gla_a', 'gla_norm_g', 'pool_w', 'pool_scale',
        'lambda_q1', 'lambda_k1', 'lambda_q2', 'lambda_k2', 'diff_norm_g', 'w_out', 'norm_mem_g', 'mem_norm_g',
        'w_mem_q', 'w_mem_kv', 'w_mem_o', 'norm_ffn_g', 'w_router_group', 'b_router_group',
        'w_router_expert', 'b_router_expert', 'w_exp_gate', 'w_exp_up', 'w_exp_down', 'final_norm_g']
_OUTS = [(1, SEQ, D), (1, DEC, D), (1, 1, SEQ, HEADS, 2 * DH), (1, 1, SEQ, HEADS, DV), (1, 1, MEM, MH, P),
         (1, 1, MEM, MH, P), (1, 1, GH, GK, GV), (1, 1, HIST, 256), (1, 1, DEC, HEADS, 2 * DH),
         (1, 1, DEC, HEADS, DV), (1, 1, GH, GK, GV), (1, 1, HIST, 256)]


def kernel(**inputs):
    import numpy as _np
    import concourse.bacc as _bacc
    from concourse.bass_utils import run_bass_kernel_spmd as _run

    nc = _bacc.Bacc("TRN2", target_bir_lowering=False, num_devices=1)
    arrays, ins = {}, {}
    for name in _INS:
        a = _np.ascontiguousarray(inputs[name])
        arrays[f"in_{name}"] = a
        ins[name] = nc.dram_tensor(f"in_{name}", a.shape, mybir.dt.from_np(a.dtype), kind="ExternalInput").ap()
    outs = [nc.dram_tensor(f"out_{i}", shape, F32, kind="ExternalOutput").ap() for i, shape in enumerate(_OUTS)]
    layer_program(nc, ins, outs)
    r = _run(nc, [arrays], core_ids=[0])
    return tuple(r.results[0][f"out_{i}"] for i in range(len(_OUTS)))
```

```python
from contextlib import ExitStack

import concourse.bass as bass
from concourse import mybir

F32 = mybir.dt.float32
F32R = mybir.dt.float32r
BF16 = mybir.dt.bfloat16
I32 = mybir.dt.int32
ALU = mybir.AluOpType
ACT = mybir.ActivationFunctionType
AX = mybir.AxisListType

P = 128
D = 1024
KB = D // P
SEQ, DEC, PAST, MEM = 512, 64, 512, 256
TOK = SEQ + DEC
TILES = 5
ROWS = [P, P, P, P, DEC]
CH = 64
NCH = TOK // CH
GH, GK, GV = 4, 32, 64
DH, DV, HEADS = 64, 128, 4
MH = 4
POOL_WINDOWS = (2, 4, 8, 16)
HIST = 15
EPS = 1e-6
LAM_INIT = 0.2
GROUPS, PER, E = 4, 4, 16
HID = 512
EXP_CLAMP = 40.0
UNIT = 4 * 512
RING = 6
WR = 4
EMPTY = 2047
MAX_EXTRA = 8
SLOT_ROWS = P * MAX_EXTRA
C_G, C_R, C_U, C_Q, C_K, C_V = 0, 512, 784, 1040, 1552, 2064

IN_BLOCKS = [("G", C_G, 512), ("R", C_R, 272), ("U", C_U, 256), ("K", C_K, 512), ("V", C_V, 512), ("Q", C_Q, 512)]


POOL_USES = [("pool", 0), ("pool_s", 0), ("pool", 1), ("pool_s", 1)]


def dense_units():
    units = [("w_mem_kv", r, c, 512) for c in (0, 512) for r in (0, 512)]
    units += [("w_in", r, c, w) for _, c, w in IN_BLOCKS for r in (0, 512)]
    units += [("w_out", r, c, 512) for c in (0, 512) for r in (0, 512)]
    units += [("w_mem_q", r, 0, 512) for r in (0, 512)]
    units += [("w_mem_o", 0, c, 512) for c in (0, 512)]
    return units


def numbered(plan):
    seen, out, bank = {"A": 0, "V": 0}, {}, 1
    for n, (key, who, *named) in enumerate(plan):
        bank = named[0] if named else 1 - bank
        out[key] = (n, who, seen[who], bank)
        seen[who] += 1
    return out


def swap_reads(numbers, a, b):
    (i, who, ra, x), (j, _, rb, y) = numbers[a], numbers[b]
    numbers[a], numbers[b] = (i, who, rb, x), (j, who, ra, y)


def projection_plan():
    plan = [((b, i), "A") for b in ("memk", "memv") for i in range(2)]
    plan += [((b, t), "A") for b, _, _ in IN_BLOCKS[:-1] for t in range(TILES)] + [(("Q", t), "A") for t in range(2)]
    for t in range(TILES):
        plan += [(("gla_o", t), "V")] + ([(("Q", t + 2), "A")] if t + 2 < TILES else [])
    for t in range(TILES):
        plan += [(("w_out", 0, t - 1), "V", 1 - t % 2)] if t else [(key, "A", 1) for key in POOL_USES[0:3]]
        plan += [(("diff_o", t), "V", t % 2)]
        plan += [(("w_out", 1, t - 1), "V", 1 - t % 2)] if t else [(POOL_USES[3], "A", 1)]
    plan += [(("w_out", c, TILES - 1), "V") for c in range(2)]
    plan += [(("mem_q", 0), "A")]
    for t in range(TILES):
        plan += [(("mem_q", t + 1), "A")] if t + 1 < TILES else []
        plan += [(("mem_o", t), "A")]
        plan += [(("w_mem_o", c, t - 1), "V") for c in range(2)] if t else []
    plan += [(("w_mem_o", c, TILES - 1), "V") for c in range(2)]
    plan += [(("router",), "V"), (("pos",), "V"), (("entries",), "V")]
    return plan


def key_blocks(t):
    return t + 1 if t < 4 else 5


def transpose_plan():
    plan = [(("params",), "V")] + [(("mem", i, g), "V") for i in range(2) for g in range(2)]
    plan += [(("mk", i), "A") for i in range(2)]
    plan += [(("x", t, g), "V") for t in range(TILES) for g in range(2)]
    plan += [(("G", t), "V") for t in range(TILES)]
    plan += [(("R", g), "A") for g in range(2)]
    plan += [(("U", t), "A") for t in range(TILES)] + [(("hist",), "A")]
    plan += [(("K", t), "A") for t in range(TILES)]
    plan += [(("kend", g), "V") for g in range(2)]
    plan += [(("Q", 0), "A")]
    for t in range(TILES):
        plan += ([(("Q", t + 1), "A")] if t + 1 < TILES else []) + ([(("mix_g", t - 1), "A")] if t else [])
    plan += [(("mix_g", TILES - 1), "A")]
    for t in range(TILES):
        for h in range(HEADS):
            plan += [(("pd", t, h, g), "A") for g in range(2 if t == 4 else 1)]
            plan += [(("mix_d", t - 1), "A")] if h == 1 and t else []
            plan += [(("kp", h), "A")] if t == 0 else []
    plan += [(("mix_d", TILES - 1), "A")]
    plan += [(("x1", t, g), "V") for t in range(2) for g in range(2)] + [(("mq", 0), "V")]
    for t in range(TILES):
        plan += [(("pm", t, 0), "A"), (("pm", t, 1), "V")]
        plan += [(("mq", t + 1), "V")] if t + 1 < TILES else []
        plan += [(("x1", t + 2, g), "V") for g in range(2)] if t + 2 < TILES else []
        plan += [(("cmk", b), "A") for b in range(2)] if t == 3 else []
        plan += [(("x2", t - 2, g), "AV"[g]) for g in range(2)] if t >= 2 else []
    plan += [(("x2", t, g), "AV"[g]) for t in range(TILES - 2, TILES) for g in range(2)]
    return plan


def score_plan():
    plan = [(("gate",), "V")] + [(("kv", g), "V") for g in range(3)]
    plan += [(("att", t), "V") for t in range(TILES)]
    plan += [(("diff", t, h), "A") for t in range(4) for h in range(HEADS)]
    plan += [(("diff", 4, h, m), "A") for h in range(HEADS) for m in (1, 0)]
    plan += [(("mem", t), "A") for t in range(TILES)]
    return plan


DENSE = dense_units()
NDENSE = len(DENSE)
assert NDENSE % RING == 0
PJ, TR, SC = numbered(projection_plan()), numbered(transpose_plan()), numbered(score_plan())
for _t in range(1, TILES):
    swap_reads(PJ, ("diff_o", _t), ("w_out", 1, _t - 1))
NMOE = 6 * E
STEPS = [(t, h) for t in range(TILES) for h in range(HEADS)]


def layer_program(nc, A, O):
    ctx = ExitStack()
    with ctx:
        def sem(name):
            return ctx.enter_context(nc.semaphore(name))

        def sb(stack, name, shape, dt=F32):
            return stack.enter_context(nc.sbuf_tensor(name, shape, dt))

        def pb(name, dt=F32):
            return ctx.enter_context(nc.psum_tensor(name, [P, 512], dt))

        slots = nc.dram_tensor("slots", (SLOT_ROWS, 2), I32).ap()
        h3_rows = nc.dram_tensor("h3_rows", (TOK, D), F32).ap()
        y_rows = nc.dram_tensor("y_rows", (2 * TOK, D), F32).ap()

        raw = sb(ctx, "raw", [P, RING, UNIT])
        X = sb(ctx, "X", [P, TILES, D])
        hT = sb(ctx, "hT", [P, KB, TOK])
        ident = sb(ctx, "ident", [P, P])
        stat = sb(ctx, "stat", [P, 16, 8])
        rs = sb(ctx, "rs", [P, 16, 8])
        neghalf = sb(ctx, "neghalf", [P, 8])
        wr = sb(ctx, "wr", [P, KB, GROUPS + E])
        br = sb(ctx, "br", [P, GROUPS + E])
        before = sb(ctx, "before", [P, P], BF16)
        onesb = sb(ctx, "onesb", [P, P], BF16)
        eidx = sb(ctx, "eidx", [P, E])
        tokid = sb(ctx, "tokid", [P, 2, TILES, 2], I32)
        chosen = sb(ctx, "chosen", [P, TILES, E], BF16)
        empty = sb(ctx, "empty", [P, 2 * SLOT_ROWS // P], I32)
        gate = sb(ctx, "gate", [P, 2, TILES])
        slot_i = sb(ctx, "slot_i", [P, 2, TILES], I32)
        lane = sb(ctx, "lane", [P, P])
        entry = sb(ctx, "entry", [P, 2, TILES, 2])
        idx_sb = sb(ctx, "idx_sb", [P, E, 2], I32)
        tiny = sb(ctx, "tiny", [P, 48])
        extra_i = sb(ctx, "extra_i", [1, MAX_EXTRA + 1], I32)

        qT = X[:, :, :].rearrange("p t n -> p (t n)")[:, 0:HEADS * TOK].rearrange("p (h n) -> p h n", h=HEADS)
        kpT = X[:, :, :].rearrange("p t n -> p (t n)")[:, HEADS * TOK:HEADS * (TOK + PAST)].rearrange(
            "p (h n) -> p h n", h=HEADS)
        kprow = hT[:, :, :].rearrange("p k n -> p (k n)")[:, 0:2048].rearrange("p (b n) -> p b n", b=4)
        vp = hT[:, :, :].rearrange("p k n -> p (k n)")[:, 2048:4096].rearrange("p (b n) -> p b n", b=4)

        pre = ExitStack()
        mixT = sb(pre, "mixT", [P, KB, TOK])
        memT = mixT[:, :, 0:MEM]
        junk = mixT[:, :, 384:512]
        mkT = sb(pre, "mkT", [P, MH, MEM])
        mv = sb(pre, "mv", [P, 2, 512])
        kT = sb(pre, "kT", [P, HEADS, TOK])
        vrow = sb(pre, "vrow", [P, TILES, 512])
        rowbuf = sb(pre, "rowbuf", [P, 2, 512])
        grow = sb(pre, "grow", [27, P])
        gcol = sb(pre, "gcol", [P, 27])
        gains = gcol[:, 0:24].rearrange("p (i k) -> p i k", i=3)
        gdiff = sb(pre, "gdiff", [P, P])
        ggla = sb(pre, "ggla", [P, GV])
        lamv = sb(pre, "lamv", [P, 4, 64])
        lams = sb(pre, "lams", [P, 8])
        wa2 = sb(pre, "wa2", [16, P])
        ba, pscale = gcol[:, 26:27], gcol[:, 24:26]
        poolw = sb(pre, "poolw", [P, 2, P])
        causal = sb(pre, "causal", [P, P])
        hide_q = sb(pre, "hide_q", [CH + 1, P], BF16)
        hide_k = sb(pre, "hide_k", [CH + 1, CH], BF16)

        glas = ExitStack()
        gv = sb(glas, "gv", [P, TILES, GH * GV])
        zR = sb(glas, "zR", [P, TILES, 272])
        gq = sb(glas, "gq", [P, TOK])
        gk = sb(glas, "gk", [P, TOK])
        cum = sb(glas, "cum", [P, TOK])
        t1 = sb(glas, "t1", [P, TOK])
        t2 = sb(glas, "t2", [P, TOK])
        t3 = sb(glas, "t3", [P, TOK])
        t4 = sb(glas, "t4", [P, TOK])
        gaT = t4[0:16, :]
        dec_end = sb(glas, "dec_end", [P, NCH])
        kend = sb(glas, "kend", [P, TILES, P])
        S = sb(glas, "S", [P, 9, GH * GV])
        Ss = sb(glas, "Ss", [P, 2, GH * GV])
        own = sb(glas, "own", [P, GH * GV])
        attm = sb(glas, "attm", [P, 2, 512])
        EXT = 16 + SEQ + 16 + DEC
        S0 = 16 + SEQ + 16
        ext = sb(glas, "ext", [P, 2, EXT])
        win_a = sb(glas, "win_a", [P, 2, EXT])
        win_b = sb(glas, "win_b", [P, 2, EXT])
        ramp = sb(glas, "ramp", [P, 2, 16])
        keep = S[:, 5:8, :].rearrange("p a b -> p (a b)")[:, 0:TOK]
        mixg = cum[:, 0:512].rearrange("p (b n) -> p b n", b=2)
        hist = kend[0:HIST, 0:2, :].rearrange("p a b -> p (a b)")
        glas.close()

        dif = ExitStack()
        prob = sb(dif, "prob", [P, 2, 2, TOK])
        pdT = sb(dif, "pdT", [P, 2, 5, P])
        mixd = sb(dif, "mixd", [P, 2, 512])
        diff_sq = sb(dif, "diff_sq", [P, 512])
        dif.close()

        mem = ExitStack()
        probm = sb(mem, "probm", [P, 2, MH, MEM])
        pmT = sb(mem, "pmT", [P, 2, 2 * MH, P])
        gffn = sb(mem, "gffn", [P, D])
        mem.close()
        pad = ExitStack()
        sb(pad, "attention_or_memory", [P, 5 * D])
        xw = sb(pad, "xw", [P, TILES, D])
        omT = sb(pad, "omT", [P, MH, TOK])
        h3 = sb(pad, "h3", [P, 2, D])
        sq_scr = sb(pad, "sq_scr", [P, D])
        pad.close()
        pre.close()

        moe = ExitStack()
        wh = sb(moe, "wh", [P, WR, UNIT], F32R)
        wl = sb(moe, "wl", [P, WR, UNIT], F32R)
        hTh = sb(moe, "hTh", [P, 2, 4, P], F32R)
        hTl = sb(moe, "hTl", [P, 2, 4, P], F32R)
        xgh = sb(moe, "xgh", [P, 2, KB, P], F32R)
        xgl = sb(moe, "xgl", [P, 2, KB, P], F32R)
        xg = sb(moe, "xg", [P, 2, D])
        act_g = sb(moe, "act_g", [P, 512])
        hid = sb(moe, "hid", [P, 512])
        y = sb(moe, "y", [P, 2, D])
        idx_extra = sb(moe, "idx_extra", [P, 2], I32)
        pool_mark = sb(moe, "pool_mark", [1, 3])
        moe.close()

        end = ExitStack()
        yg = sb(end, "yg", [P, TILES, 2, D])
        gfin = sb(end, "gfin", [P, D])
        outb = sb(end, "outb", [P, 2, D])
        junk_end = sb(end, "junk_end", [P, D])
        end.close()
        pj = [pb("pj0"), pb("pj1")]
        tr = [pb("tr_v"), pb("tr_a")]
        sc = ctx.enter_context(nc.psum_tensor("scores", [P, 4 * 512], F32))

        def flat(ap):
            return ap.rearrange("p a b -> p (a b)")

        memsrc = flat(vrow[:, :, :])[:, 0:2048].rearrange("p (t n) -> p t n", t=2)
        q_heads = [gq[:, 0:512], gk[:, 0:512]]
        gla_sq = t4[:, 0:256]
        qmT = flat(kT[:, :, :])[:, 0:1024].rearrange("p (b h q) -> p b h q", b=2, h=MH)
        cmkT = flat(kT[:, :, :])[:, 1024:2048].rearrange("p (h k) -> p h k", h=MH)
        cmkrow, cmv = vrow[:, 0:2, :], vrow[:, 2:4, :]
        nmax, psum_, recip = (tiny[:, 4 * i:4 * i + 4].rearrange("p (b m) -> p b m", b=2) for i in range(3))
        nmaxm, psumm, nrec = (tiny[:, 16 + 8 * i:24 + 8 * i].rearrange("p (b h) -> p b h", b=2) for i in range(3))
        scratch = flat(hT[:, :, :])
        lg = scratch[:, 0:100].rearrange("p (t n) -> p t n", t=TILES)
        r20 = [scratch[:, 100 + 20 * i:120 + 20 * i].rearrange("p (t n) -> p t n", t=TILES) for i in range(6)]
        r5 = [scratch[:, 220 + 5 * i:225 + 5 * i] for i in range(7)]
        r80 = [scratch[:, 260 + 80 * i:340 + 80 * i].rearrange("p (t n) -> p t n", t=TILES) for i in range(4)]
        rank4 = scratch[:, 590:594]
        more, upto, base, ones16 = (scratch[:, 600 + 16 * i:616 + 16 * i] for i in range(4))
        r8x16 = scratch[0:1, 680:680 + MAX_EXTRA * E].rearrange("p (i e) -> p i e", e=E)
        placed = scratch[:, 1024:1024 + 10 * P].rearrange("p (i t n) -> p i t n", i=2, t=TILES)
        held = scratch[:, 2304:2304 + 320].rearrange("p (i t v e) -> p i t v e", i=2, t=TILES, v=2)
        posc, posi = scratch[:, 2640:2736], [scratch[:, 2740 + 5 * i:2745 + 5 * i] for i in range(2)]
        extra_f = scratch[0:1, 820:820 + MAX_EXTRA]
        pg, pu, ph = pj, tr[0], tr[1]
        px = [sc[:, 0:512], sc[:, 512:1024]]
        py = [sc[:, 1024:1536], sc[:, 1536:2048]]

        ROW_USES = [(True, ("mk", 0)), (True, ("mk", 1))] + [(False, ("G", t)) for t in range(TILES)]
        ROW_USES += [(t >= 3, ("U", t)) for t in range(TILES)] + [(True, ("K", t)) for t in range(TILES)]
        ROW_USES += [(False, ("Q", t)) for t in range(TILES)]
        ROW_AT = {key: n for n, (_, key) in enumerate(ROW_USES)}
        ROW_STORES = [sum(s for s, _ in ROW_USES[n % 2:n:2]) for n in range(len(ROW_USES))]
        ROW_TOTAL = [sum(s for s, _ in ROW_USES[b::2]) for b in range(2)]
        NPARAMS = 11

        unit_in = [sem(f"unit_in{i}") for i in range(RING)]
        x_in = [sem(f"x_in{t}") for t in range(TILES)]
        x_again = sem("x_again")
        mem_in, gains_in, params_in = sem("mem_in"), sem("gains_in"), sem("params_in")
        hist_in, state_in = sem("hist_in"), sem("state_in")
        kp_in, vp_in, cmk_in, cmv_in = sem("kp_in"), sem("vp_in"), sem("cmk_in"), sem("cmv_in")
        gffn_in, gfin_in = sem("gffn_in"), sem("gfin_in")
        idx_in = sem("idx_in")
        xg_in = [sem("xg_in0"), sem("xg_in1")]
        yg_in = [sem(f"yg_in{t}") for t in range(TILES)]
        stored = sem("stored")
        row_out = [sem("row_out0"), sem("row_out1")]
        state_out = sem("state_out")
        h3_out = [sem("h3_out0"), sem("h3_out1")]
        table_empty, table_out = sem("table_empty"), sem("table_out")
        y_out = [sem("y_out0"), sem("y_out1")]
        out_stored = [sem("out_stored0"), sem("out_stored1")]
        pj_full, pj_act, pj_dve = sem("pj_full"), sem("pj_act"), sem("pj_dve")
        tr_full, tr_act, tr_dve = sem("tr_full"), sem("tr_act"), sem("tr_dve")
        sc_full, sc_act, sc_dve = sem("sc_full"), sem("sc_act"), sem("sc_dve")
        ms_act, ms_dve, rs_ready, sq_act = sem("ms_act"), sem("ms_dve"), sem("rs_ready"), sem("sq_act")
        dve_step, act_step, pool_step = sem("dve_step"), sem("act_step"), sem("pool_step")
        consts = sem("consts")
        lam_sum, lam_exp = sem("lam_sum"), sem("lam_exp")
        gate_arg, gate_log, cum_ready = sem("gate_arg"), sem("gate_log"), sem("cum_ready")
        decay_arg, decay_exp, gla_in = sem("decay_arg"), sem("decay_exp"), sem("gla_in")
        silu_ready, glu_ready = sem("silu_ready"), sem("glu_ready")
        states_ready, qb_ready, mixg_ready = sem("states_ready"), sem("qb_ready"), sem("mixg_ready")
        ramp_ready, pool_ready = sem("ramp_ready"), sem("pool_ready")
        max_ready, pd_ready, mixd_ready = sem("max_ready"), sem("pd_ready"), sem("mixd_ready")
        maxm_ready, pm_ready = sem("maxm_ready"), sem("pm_ready")
        h3_ready, route_arg, route_exp = sem("h3_ready"), sem("route_arg"), sem("route_exp")
        chosen_ready, place_ready = sem("chosen_ready"), sem("place_ready")
        slots_ready, list_ready = sem("slots_ready"), sem("list_ready")
        hi_done, lo_done, pe_unit = sem("hi_done"), sem("lo_done"), sem("pe_unit")
        xt_done, xh_done, xl_done, xg_clear = sem("xt_done"), sem("xh_done"), sem("xl_done"), sem("xg_clear")
        sg_done, h_done, ht_done = sem("sg_done"), sem("h_done"), sem("ht_done")
        hh_done, hl_done, y_done = sem("hh_done"), sem("hl_done"), sem("y_done")
        pool_mark_set = sem("pool_mark_set")
        y_all, sum_done, out_ready = sem("y_all"), sem("sum_done"), sem("out_ready")

        RS = {k: n for n, k in enumerate(
            ["mem", "x"] + [("gla", t) for t in range(TILES)]
            + [k for t in range(TILES) for k in ([("x1", t - 2)] if t >= 2 else []) + [("diff", t)]]
            + [("x1", t) for t in range(TILES - 2, TILES)] + [(b, t) for b in ("x2", "end") for t in range(TILES)])}
        STAT = {"mem": 0, "x": 1, "x1": 2, "x2": 3, "end": 4}
        MS_ACT = {k: n for n, k in enumerate(
            [("mem", 0), ("mem", 1)] + [(b, t) for b in ("x", "x1", "x2", "end") for t in range(TILES)])}
        PJ_KEYS, TR_KEYS, SC_KEYS = list(PJ), list(TR), list(SC)
        UNIT_USER = [("memk", 1)] * 2 + [("memv", 1)] * 2 + [(b, 4) for b, _, _ in IN_BLOCKS for _ in range(2)]
        UNIT_USER += [("w_out", c, 4) for c in range(2) for _ in range(2)] + [("mem_q", 4)] * 2
        UNIT_USER += [("w_mem_o", c, 4) for c in range(2)]
        BLOCK_UNITS = {b: (4 + 2 * n, 5 + 2 * n) for n, (b, _, _) in enumerate(IN_BLOCKS)}
        WIDTH = {b: w for b, _, w in IN_BLOCKS}
        WO_UNIT, MQ_UNIT, MO_UNIT = 16, 20, 22

        def stat_of(key):
            if key == "mem":
                return slice(0, P), 0, slice(0, 2)
            if key == "x":
                return slice(0, P), 1, slice(0, TILES)
            name, t = key
            if name in ("gla", "diff"):
                return slice(0, ROWS[t]), (5 if name == "gla" else 10) + t, slice(0, 4)
            return slice(0, ROWS[t]), STAT[name], slice(t, t + 1)

        def read_out(eng, numbers, act_sem, dve_sem, key):
            _, who, rank, _ = numbers[key]
            eng.wait_ge(act_sem if who == "A" else dve_sem, rank + 1)

        def pj_read(eng, key):
            read_out(eng, PJ, pj_act, pj_dve, key)

        def tr_read(eng, key):
            read_out(eng, TR, tr_act, tr_dve, key)

        def sc_read(eng, key):
            read_out(eng, SC, sc_act, sc_dve, key)

        def cols(t):
            return slice(P * t, P * t + ROWS[t])

        def x_tile(t):
            return X[0:ROWS[t], t, :]

        def xw_tile(t):
            return xw[0:ROWS[t], t, :]

        def half(key):
            return sc[:, (SC[key][0] % 2) * 1024:(SC[key][0] % 2) * 1024 + 1024]

        def maps(t, h, nk):
            n, R = SC[last_score(t, h)][0], ROWS[t]
            if t < 4:
                return sc[0:R, (n % 2) * 1024:(n % 2) * 1024 + 1024].rearrange("p (m k) -> p m k", m=2)[:, :, 0:nk]
            assert n % 2 == 0
            return sc[0:R, :].rearrange("p (m k) -> p m k", m=2)[:, :, 0:nk]

        def keys_of(t):
            return P * (t + 1) if t < 4 else PAST + DEC

        def last_score(t, h):
            return ("diff", t, h) if t < 4 else ("diff", t, h, 0)

        def step_unit(j, last):
            names = [("w_exp_up", 0), ("w_exp_down", 0)] if last else [("w_exp_up", 0), ("w_exp_gate", 1), ("w_exp_down", 0)]
            return (*names[j // 2], j % 2)

        def fixed(e, n):
            return isinstance(e, int) and e < n

        block = ctx.enter_context(nc.Block())
        dram = {n: A[n] for n in ("w_mem_kv", "w_in", "w_out", "w_mem_q", "w_mem_o")}

        @block.sync
        def _(sp):
            row = 0
            for name, n in (("norm_mix_g", KB), ("mem_norm_g", KB), ("norm_mem_g", KB), ("pool_scale", 2), ("b_gla_a", 1)):
                sp.dma_start(grow[row:row + n, :], A[name].rearrange("a (k p) -> (a k) p", p=P)).then_inc(gains_in, 16)
                row += n
            sp.dma_start(memsrc[:, :, :], A["mem_prompt"][0].rearrange("(t p) n -> p t n", p=P)).then_inc(mem_in, 16)
            for n, (name, r, c, w) in enumerate(DENSE):
                if n >= RING:
                    sp.wait_ge(pj_full, PJ[UNIT_USER[n - RING]][0] + 1)
                dst = raw[:, n % RING, 0:4 * w].rearrange("p (k w) -> p k w", k=4)
                src = dram[name][0, r:r + 512, c:c + w].rearrange("(k p) w -> p k w", p=P)
                sp.dma_start(dst, src).then_inc(unit_in[n % RING], 16)
            def load(n_slot, free, name, e, part):
                free()
                src = A[name][0, e if isinstance(e, int) else bass.ds(e, 1)]
                if not isinstance(e, int):
                    src = src.rearrange("a r c -> (a r) c")
                src = src[:, 512 * part:512 * part + 512] if name == "w_exp_down" else src[512 * part:512 * part + 512, :]
                sp.dma_start(raw[:, n_slot, :].rearrange("p (k w) -> p k w", k=4),
                             src.rearrange("(k p) w -> p k w", p=P)).then_inc(unit_in[n_slot], 16)

            def step_load(e, j, last=False):
                name, who, part = step_unit(j, last)

                def free():
                    if fixed(e, 1) and j < 4:
                        sp.wait_ge(pj_full, PJ[UNIT_USER[NDENSE - RING + 2 + j]][0] + 1)
                    else:
                        sp.wait_ge(lo_done, 6 * e + (j - 3))

                load((2 + j) % RING, free, name, e + who, part)

            for n in range(2):
                load(n, lambda: sp.wait_ge(pj_full, PJ[UNIT_USER[NDENSE - RING + n]][0] + 1), "w_exp_gate", 0, n)
            for e in range(2):
                for j in range(6):
                    step_load(e, j)
            with sp.Fori(1, E // 2 - 1) as i:
                for b in range(2):
                    for j in range(6):
                        step_load(2 * i + b, j)
            for j in range(6):
                step_load(E - 2, j)
            for j in range(4):
                step_load(E - 1, j, last=True)
            sp.wait_ge(list_ready, 1)
            rounds = sp.value_load(extra_i[0:1, MAX_EXTRA:MAX_EXTRA + 1], min_val=0, max_val=MAX_EXTRA)
            with sp.If(rounds > 0):
                with sp.Fori(0, rounds) as i:
                    e = sp.value_load(extra_i[0:1, bass.ds(i, 1)], min_val=0, max_val=E - 1)
                    for k in range(6):
                        name, part = ("w_exp_gate", "w_exp_up", "w_exp_down")[k // 2], k % 2
                        load(k, lambda: sp.wait_ge(lo_done, NMOE + 6 * i + (k - 5)), name, e, part)
            sp.wait_ge(y_all, 1)
            for t in range(TILES):
                sp.dma_start(yg[0:ROWS[t], t, :, :], y_rows.rearrange("(i n) d -> n i d", i=2)[P * t:P * t + ROWS[t]])\
                    .then_inc(yg_in[t], 16)
                if t == 0:
                    sp.dma_start(gfin[:, :], A["final_norm_g"].unsqueeze(0).to_broadcast([P, D])).then_inc(gfin_in, 16)

        @block.gpsimd
        def _(pool):
            steps = [0]

            def link(ins):
                steps[0] += 1
                ins.then_inc(pool_step, 1)
                pool.wait_ge(pool_step, steps[0])

            def ready(ins):
                const_count[0] += 1
                ins.then_inc(consts, 1)
                pool.wait_ge(consts, const_count[0])

            const_count = [0]
            link(pool.memset(stat[:, :, :], 1.0))
            link(pool.memset(ident[:, :], 0.0))
            ready(pool.affine_select(out=ident[:, :], in_=ident[:, :], compare_op=ALU.not_equal, fill=1.0, base=0,
                                     pattern=[[-1, P]], channel_multiplier=1))
            link(pool.memset(causal[:, :], 1.0))
            link(pool.affine_select(out=causal[:, :], in_=causal[:, :], compare_op=ALU.is_ge, fill=0.0, base=0,
                                    pattern=[[1, P]], channel_multiplier=-1))
            ready(pool.memset(causal[0:CH, CH:P], 0.0))
            link(pool.memset(before[:, :], 1.0))
            ready(pool.affine_select(out=before[:, :], in_=before[:, :], compare_op=ALU.is_ge, fill=0.0, base=-1,
                                     pattern=[[1, P]], channel_multiplier=-1))
            ready(pool.memset(onesb[:, :], 1.0))
            ready(pool.memset(neghalf[:, :], -0.5))
            link(pool.memset(own[:, :], 0.0))
            for h in range(GH - 1):
                link(pool.memset(own[GK * h:GK * (h + 1), GV * h:GV * (h + 1)], 1.0))
            ready(pool.memset(own[GK * 3:P, GV * 3:], 1.0))
            ready(pool.memset(poolw[:, :, :], 0.0))
            ready(pool.iota(eidx[:, :], [[1, E]], base=0, channel_multiplier=0, allow_small_or_imprecise_dtypes=True))
            link(pool.iota(tokid[:, :, :, 0], [[0, 2], [P, TILES]], base=0, channel_multiplier=1))
            ready(pool.iota(tokid[:, :, :, 1], [[TOK, 2], [P, TILES]], base=0, channel_multiplier=1))
            link(pool.iota(lane[:, :], [[1, P]], base=0, channel_multiplier=0, allow_small_or_imprecise_dtypes=True))
            link(pool.tensor_copy(entry[:, :, :, :], tokid[:, :, :, :]))
            link(pool.tensor_scalar(entry[:, :, :, :], entry[:, :, :, :], -float(EMPTY), None, ALU.add))
            ready(pool.memset(empty[:, :], EMPTY))
            link(pool.memset(hide_q[:, :], 0.0))
            link(pool.memset(hide_q[:, 0:CH], 1.0))
            ready(pool.memset(hide_k[:, :], -1e30))
            link(pool.memset(S[:, 0, :], 0.0))
            link(pool.memset(keep, 1.0))
            ready(pool.memset(keep.rearrange("p (c n) -> p c n", n=CH)[:, :, 0], 0.0))
            ready(pool.memset(Ss[:, 0, :], 0.0))
            link(pool.memset(ext[:, :, 0:16], 0.0))
            ready(pool.memset(ext[:, :, S0 - 16:S0 - 15], 0.0))
            for g in range(4):
                pool.dma_start(poolw[64 * (g % 2):64 * (g % 2) + 64, g // 2, 64 * (g % 2):64 * (g % 2) + 64],
                               A["pool_w"][0, g]).then_inc(state_in, 16)
                pool.dma_start(Ss[GK * g:GK * g + GK, 0, GV * g:GV * g + GV], A["state_gla"][0, 0, g])\
                    .then_inc(state_in, 16)
            pool.dma_start(slots.rearrange("(p n) o -> p (n o)", p=P), empty[:, :]).then_inc(table_empty, 16)

            def root(key):
                rows, n, cs = stat_of(key)
                if key == "mem":
                    pool.wait_ge(ms_act, MS_ACT[("mem", 1)] + 1)
                elif key == "x":
                    pool.wait_ge(ms_act, MS_ACT[("x", TILES - 1)] + 1)
                elif key[0] in ("gla", "diff"):
                    pool.wait_ge(ms_dve, (TILES if key[0] == "diff" else 0) + key[1] + 1)
                else:
                    pool.wait_ge(ms_act, MS_ACT[key] + 1)
                link(pool.tensor_scalar(rs[rows, n, cs], stat[rows, n, cs], EPS, None, ALU.add))
                width = cs.stop - cs.start
                pool.tensor_tensor(rs[rows, n, cs], rs[rows, n, cs], neghalf[rows, 0:width], ALU.pow)\
                    .then_inc(rs_ready, 1)
                pool.wait_ge(rs_ready, RS[key] + 1)

            root("mem")
            root("x")
            pool.wait_ge(silu_ready, 2)
            for t in range(TILES):
                v = zR[0:ROWS[t], t, 0:256].rearrange("p (h v) -> p h v", h=GH)
                pool.tensor_tensor(v, v, ggla[0:ROWS[t], :].unsqueeze(1).to_broadcast([ROWS[t], GH, GV]), ALU.mult)\
                    .then_inc(glu_ready, 1)
                pool.wait_ge(glu_ready, t + 1)
            tr_read(pool, ("hist",))
            tr_read(pool, ("U", TILES - 1))
            W = EXT
            link(pool.tensor_tensor(win_a[:, :, 1:W], ext[:, :, 1:W], ext[:, :, 0:W - 1], ALU.add))
            link(pool.tensor_tensor(win_b[:, :, 3:W], win_a[:, :, 3:W], win_a[:, :, 1:W - 2], ALU.add))
            link(pool.tensor_tensor(win_a[:, 1, 7:W], win_b[:, 1, 7:W], win_b[:, 1, 3:W - 4], ALU.add))
            link(pool.tensor_tensor(win_b[64:P, 1, 15:W], win_a[64:P, 1, 15:W], win_a[64:P, 1, 7:W - 8], ALU.add))
            pool.wait_ge(ramp_ready, 1)
            for g, win in enumerate((win_a, win_b, win_a, win_b)):
                rows, b = slice(64 * (g % 2), 64 * (g % 2) + 64), g // 2
                link(pool.tensor_tensor(win[rows, b, 16:32], win[rows, b, 16:32], ramp[rows, b, :], ALU.mult))
                link(pool.tensor_scalar(win[rows, b, 16:W], win[rows, b, 16:W], 1.0 / POOL_WINDOWS[g], None, ALU.mult))
                pool.tensor_tensor(ext[rows, b, 16:W], win[rows, b, 16:W], ext[rows, b, 16:W], ALU.subtract)\
                    .then_inc(pool_ready, 1)
                pool.wait_ge(pool_ready, g + 1)
            for key in list(RS)[2:-TILES]:
                root(key)
            pool.wait_ge(chosen_ready, 1)
            pool.memset(xg[:, :, :], 0.0).then_inc(xg_clear, 1)
            pool.wait_ge(xg_clear, 1)
            pj_read(pool, ("entries",))
            pool.wait_ge(h3_out[0], 16 * 3)
            pool.wait_ge(h3_out[1], 16 * 2)

            def gather(b, idx):
                pool.indirect_dma_start(xg[:, b, :], None, h3_rows, bass.IndirectOffsetOnAxis(ap=idx, axis=0),
                                        bounds_check=TOK - 1, oob_is_err=False).then_inc(xg_in[b], 16)

            def scatter(b, idx):
                pool.indirect_dma_start(y_rows, bass.IndirectOffsetOnAxis(ap=idx, axis=0), y[:, b, :], None,
                                        bounds_check=2 * TOK - 1, oob_is_err=False).then_inc(y_out[b], 16)

            def mark(n):
                return pool.tensor_tensor(pool_mark[:, n:n + 1], neghalf[0:1, 0:1], neghalf[0:1, 1:2], ALU.add)

            gather(0, idx_sb[:, 0, 0:1])
            gather(1, idx_sb[:, 1, 0:1])
            for e in range(E):
                if e + 2 < E:
                    pool.wait_ge(xt_done, 2 * e + 2)
                    gather(e % 2, idx_sb[:, e + 2, 0:1])
                pool.wait_ge(y_done, 2 * e + 2)
                scatter(e % 2, idx_sb[:, e, 1:2])
            pool.wait_ge(list_ready, 1)
            rounds = pool.value_load(extra_i[0:1, MAX_EXTRA:MAX_EXTRA + 1], min_val=0, max_val=MAX_EXTRA)
            with pool.If(rounds > 0):
                pool.wait_ge(table_empty, 16)
                pool.wait_ge(slots_ready, 1)
                for i in range(2):
                    for t in range(TILES):
                        r = ROWS[t]
                        pool.indirect_dma_start(slots, bass.IndirectOffsetOnAxis(ap=slot_i[0:r, i, t:t + 1], axis=0),
                                                tokid[0:r, i, t, :], None, bounds_check=SLOT_ROWS - 1,
                                                oob_is_err=False).then_inc(table_out, 16)
                pool.wait_ge(table_out, 16 * 2 * TILES)
                with pool.Fori(0, rounds) as i:
                    pool.wait_ge(xt_done, 2 * E + 2 * i)
                    pool.wait_ge(y_out[0], 8 * E + 16 * i)
                    mark(0).then_inc(pool_mark_set, 1)
                    table = slots.rearrange("(r p) o -> r p o", p=P)[bass.ds(i, 1)]
                    pool.dma_start(idx_extra[:, :], table.rearrange("a p o -> (a p) o")).then_inc(idx_in, 16)
                    pool.wait_ge(pool_mark_set, 3 * i + 1)
                    pool.wait_ge(idx_in, 16 * i + 16)
                    mark(0).then_inc(pool_mark_set, 1)
                    gather(0, idx_extra[:, 0:1])
                    pool.wait_ge(pool_mark_set, 3 * i + 2)
                    pool.wait_ge(y_done, 2 * E + 2 * i + 2)
                    mark(1).then_inc(pool_mark_set, 1)
                    scatter(0, idx_extra[:, 1:2])
            pool.wait_ge(y_out[0], 8 * E + 16 * rounds)
            pool.wait_ge(y_out[1], 8 * E)
            mark(2).then_inc(y_all, 1)
            for t in range(TILES):
                root(("end", t))

        @block.scalar
        def _(act):
            steps = [0]

            def link(ins):
                steps[0] += 1
                ins.then_inc(act_step, 1)
                act.wait_ge(act_step, steps[0])

            def split_hi(e, b, j):
                s4, s6 = (2 + 6 * b + j) % WR, (2 + j) % RING
                act.wait_ge(unit_in[s6], 16 * (e + (NDENSE // RING + 1 + (2 + j) // RING)))
                if not fixed(6 * e + j + 2 if isinstance(e, int) else e, WR):
                    act.wait_ge(pe_unit, 6 * e + (j - 1))
                act.activation(wh[:, s4, :], raw[:, s6, :], ACT.Copy).then_inc(hi_done, 1)

            act.wait_ge(mem_in, 16)
            for t in range(4):
                act.dma_start(X[:, t, :], A["x_prompt"][0, P * t:P * t + P, :]).then_inc(x_in[t], 16)
            act.dma_start(X[0:DEC, 4, :], A["x_sample"][0]).then_inc(x_in[4], 16)
            params = [(ggla[:, :], A["gla_norm_g"].to_broadcast([P, GV])),
                       (gdiff[:, :], A["diff_norm_g"].to_broadcast([P, P])),
                       (wa2[:, :], A["w_gla_a2"][0]),
                       (wr[:, :, 0:GROUPS], A["w_router_group"][0].rearrange("(k p) n -> p k n", p=P)),
                       (wr[:, :, GROUPS:], A["w_router_expert"][0].rearrange("(k p) n -> p k n", p=P)),
                       (br[:, 0:GROUPS], A["b_router_group"].to_broadcast([P, GROUPS])),
                       (br[:, GROUPS:], A["b_router_expert"].to_broadcast([P, E]))]
            params += [(lamv[:, i, :], A[n].to_broadcast([P, 64])) for i, n in enumerate(
                ("lambda_q1", "lambda_k1", "lambda_q2", "lambda_k2"))]
            for dst, src in params:
                act.dma_start(dst, src).then_inc(params_in, 16)
            assert len(params) == NPARAMS
            act.dma_start(hist, A["state_pool"][0, 0]).then_inc(hist_in, 16)

            def mean_square(key, src, j, folded=False):
                rows, n, cs = stat_of(key if key[0] not in ("mem", "x") else key[0])
                i = key[1]
                r = src.shape[0]
                if MS_ACT[key]:
                    act.wait_ge(ms_act, MS_ACT[key])
                src = src.rearrange("p (a b) -> p a b", a=KB) if folded else src
                act.activation(j[0:r], src, ACT.Square, scale=1.0 / 32, accum_out=stat[0:r, n, i:i + 1])\
                    .then_inc(ms_act, 1)

            act.wait_ge(consts, 1)
            for i in range(2):
                mean_square(("mem", i), memsrc[:, i, :], junk, True)
            for t in range(TILES):
                act.wait_ge(x_in[t], 16)
                mean_square(("x", t), x_tile(t), junk, True)

            def pj_out(key, dst, scale=None, at=None):
                act.wait_ge(pj_full, PJ[key][0] + 1)
                src = pj[PJ[key][3]][0:dst.shape[0], 0:dst.shape[-1]] if at is None else at
                if scale is None:
                    return act.activation(dst, src, ACT.Copy)
                return act.activation(dst, src, ACT.Copy, scale=scale)

            def tr_out(key, dst, src):
                act.wait_ge(tr_full, TR[key][0] + 1)
                act.activation(dst, src, ACT.Copy).then_inc(tr_act, 1)

            def heads_view(bank, n, r=P):
                return bank[:, 0:n * P].rearrange("p (h q) -> p h q", h=n)[:, :, 0:r]

            act.wait_ge(rs_ready, RS["mem"] + 1)
            for b in ("memk", "memv"):
                for i in range(2):
                    dst = rowbuf[:, i, :] if b == "memk" else mv[:, i, :]
                    pj_out((b, i), dst, rs[:, 0, i:i + 1]).then_inc(pj_act, 1)
                    act.wait_ge(pj_act, PJ[(b, i)][2] + 1)
                    out = O[4 if b == "memk" else 5][0, 0, P * i:P * i + P].rearrange("m h d -> m (h d)")
                    act.dma_start(out, dst).then_inc(row_out[i] if b == "memk" else stored, 16)
            for i in range(2):
                tr_out(("mk", i), mkT[:, :, P * i:P * i + P], heads_view(tr[1], MH))

            act.wait_ge(rs_ready, RS["x"] + 1)

            def rowbuf_free(n):
                if ROW_STORES[n]:
                    act.wait_ge(row_out[n % 2], 16 * ROW_STORES[n])
                if ROW_USES[n - 2][1] is not None:
                    act.wait_ge(tr_full, TR[ROW_USES[n - 2][1]][0] + 1)

            for t in range(TILES):
                n = 2 + t
                rowbuf_free(n)
                r = ROWS[t]
                pj_out(("G", t), rowbuf[0:r, n % 2, 0:256], rs[0:r, 1, t:t + 1],
                       pj[PJ[("G", t)][3]][0:r, 0:256]).then_inc(act_step, 1)
                steps[0] += 1
                pj_out(("G", t), gv[0:r, t, :], rs[0:r, 1, t:t + 1],
                       pj[PJ[("G", t)][3]][0:r, 256:512]).then_inc(pj_act, 1)
            for t in range(TILES):
                pj_out(("R", t), zR[0:ROWS[t], t, :], rs[0:ROWS[t], 1, t:t + 1]).then_inc(pj_act, 1)
            tr_out(("R", 0), gaT[:, 0:512], tr[1][0:16, :])
            tr_out(("R", 1), gaT[:, 512:TOK], tr[1][0:16, 0:DEC])
            for r, ts in ((P, slice(0, 4)), (DEC, slice(4, 5))):
                act.activation(zR[0:r, ts, 0:256], zR[0:r, ts, 0:256], ACT.Silu).then_inc(silu_ready, 1)

            def rows_block(b, t, n):
                rowbuf_free(n)
                r, w = ROWS[t], WIDTH[b]
                pj_out((b, t), rowbuf[0:r, n % 2, 0:w], rs[0:r, 1, t:t + 1]).then_inc(pj_act, 1)
                act.wait_ge(pj_act, PJ[(b, t)][2] + 1)
                if b == "K":
                    out = O[2][0, 0, P * t:P * t + P] if t < 4 else O[8][0, 0]
                    act.dma_start(out.rearrange("m h d -> m (h d)"), rowbuf[0:r, n % 2, :]).then_inc(row_out[n % 2], 16)
                if b == "U" and t >= 3:
                    out = O[7] if t == 3 else O[11]
                    act.dma_start(out[0, 0], rowbuf[r - HIST:r, n % 2, 0:256]).then_inc(row_out[n % 2], 16)

            def u_out(t):
                c0 = 16 + P * t if t < 4 else S0
                tr_out(("U", t), ext[:, :, c0:c0 + ROWS[t]], heads_view(tr[1], 2, ROWS[t]))

            for t in range(TILES):
                rows_block("U", t, ROW_AT[("U", t)])
                if t:
                    u_out(t - 1)
            u_out(TILES - 1)
            tr_out(("hist",), ext[:, :, S0 - HIST:S0], heads_view(tr[1], 2, HIST))

            act.wait_ge(gate_arg, 1)
            link(act.activation(t2[:, :], t2[:, :], ACT.Exp))
            act.activation(t3[:, :], t2[:, :], ACT.Ln, bias=1.0).then_inc(gate_log, 1)

            def kq_out(b, t):
                tr_out((b, t), (kT if b == "K" else qT)[:, :, cols(t)], heads_view(tr[1], HEADS, ROWS[t]))

            for t in range(TILES):
                rows_block("K", t, ROW_AT[("K", t)])
                if t:
                    kq_out("K", t - 1)
            kq_out("K", TILES - 1)
            act.wait_ge(cum_ready, 1)
            act.activation(dec_end[:, :], cum[:, :].rearrange("p (c n) -> p c n", n=CH)[:, :, CH - 1], ACT.Exp)\
                .then_inc(decay_exp, 1)
            act.activation(t3[:, :], cum[:, :], ACT.Exp).then_inc(decay_exp, 1)
            for i, buf in enumerate((t1, t2, t4)):
                act.wait_ge(decay_arg, i + 1)
                act.activation(buf[:, :], buf[:, :], ACT.Exp).then_inc(decay_exp, 1)
            act.wait_ge(lam_sum, 1)
            act.activation(lams[:, 2:4], lams[:, 0:2], ACT.Exp).then_inc(lam_exp, 1)

            for t in range(TILES):
                pj_out(("V", t), vrow[0:ROWS[t], t, :], rs[0:ROWS[t], 1, t:t + 1]).then_inc(pj_act, 1)
                act.wait_ge(pj_act, PJ[("V", t)][2] + 1)
                out = O[3][0, 0, P * t:P * t + P] if t < 4 else O[9][0, 0]
                act.dma_start(out.rearrange("m h d -> m (h d)"), vrow[0:ROWS[t], t, :]).then_inc(stored, 16)
            for t in range(2):
                rows_block("Q", t, ROW_AT[("Q", t)])
            kq_out("Q", 0)

            def mixg_out(t):
                tr_out(("mix_g", t), mixT[:, 0:2, cols(t)], heads_view(tr[1], 2, ROWS[t]))

            act.wait_ge(states_ready, 1)
            for i, src in ((6, S[:, 8, :]), (10, Ss[:, 1, :])):
                for h in range(GH):
                    act.dma_start(O[i][0, 0, h], src[GK * h:GK * h + GK, GV * h:GV * h + GV]).then_inc(state_out, 16)
            for t in range(TILES):
                j, r = PJ[("gla_o", t)][3], ROWS[t]
                act.wait_ge(pj_full, PJ[("gla_o", t)][0] + 1)
                if t:
                    act.wait_ge(ms_dve, t)
                act.activation(gla_sq[0:r, :], pj[j][0:r, 0:256], ACT.Square, scale=0.125).then_inc(sq_act, 1)
                if t + 2 < TILES:
                    rows_block("Q", t + 2, ROW_AT[("Q", t + 2)])
                if t + 2 == TILES - 1:
                    act.dma_start(kprow, A["cache_diff_k"][0, 0].rearrange("(b p) h d -> p b (h d)", p=P)).then_inc(kp_in, 16)
                    act.dma_start(vp, A["cache_diff_v"][0, 0].rearrange("(b p) h d -> p b (h d)", p=P)).then_inc(vp_in, 16)
                if t + 1 < TILES:
                    kq_out("Q", t + 1)
                if t:
                    mixg_out(t - 1)
            mixg_out(TILES - 1)

            act.wait_ge(state_out, 16 * 8)
            act.dma_start(xw[:, 0:4, :], A["x_prompt"][0].rearrange("(t p) n -> p t n", p=P)).then_inc(x_again, 16)
            act.dma_start(xw[0:DEC, 4, :], A["x_sample"][0]).then_inc(x_again, 16)

            def exps(s):
                t, h = STEPS[s]
                r, nk = ROWS[t], keys_of(t)
                act.wait_ge(max_ready, s + 1)
                if s >= 2:
                    act.wait_ge(tr_full, TR[("pd", *STEPS[s - 2], 1 if STEPS[s - 2][0] == 4 else 0)][0] + 1)
                for m in (0, 1) if t < 4 else (1, 0):
                    done = (m == 1) if t < 4 else True
                    ins = act.activation(prob[0:r, s % 2, m, 0:nk], maps(t, h, nk)[:, m, :], ACT.Exp,
                                         bias=nmax[0:r, s % 2, m:m + 1], scale=DH ** -0.5,
                                         accum_out=psum_[0:r, s % 2, m:m + 1])
                    ins.then_inc(sc_act, 1) if done else ins.then_inc(act_step, 1)
                    steps[0] += not done

            def mixd_out(t):
                tr_out(("mix_d", t), mixT[:, 4:8, cols(t)], heads_view(tr[1], 4, ROWS[t]))

            def x1_square(t):
                pj_read(act, ("w_out", 1, t))
                mean_square(("x1", t), xw_tile(t), sq_scr)

            exps(0)
            for s, (t, h) in enumerate(STEPS):
                r, nb = ROWS[t], min(key_blocks(t), 4)
                tr_out(("pd", t, h, 0), pdT[:, s % 2, 0:nb, 0:r], heads_view(tr[1], nb, r))
                if t == 4:
                    tr_out(("pd", t, h, 1), pdT[0:CH, s % 2, 4, 0:r], tr[1][0:CH, 0:r])
                if h == 1 and t:
                    mixd_out(t - 1)
                if s + 1 < len(STEPS):
                    exps(s + 1)
                if t == 0:
                    tr_out(("kp", h), kpT[:, :, P * h:P * h + P], heads_view(tr[1], HEADS))
                    (name, b), (c0, c1) = POOL_USES[h], ((0, SEQ), (SEQ, TOK))[h % 2]
                    pj_out((name, b), mixT[:, 2 + b, c0:c1], pscale[:, b:b + 1]).then_inc(pj_act, 1)
                if h == 1 and t >= 2:
                    x1_square(t - 2)
                if h == HEADS - 1:
                    act.wait_ge(pj_full, PJ[("diff_o", t)][0] + 1)
                    act.wait_ge(ms_dve, TILES + t)
                    act.activation(diff_sq[0:r, :], pj[PJ[("diff_o", t)][3]][0:r, :], ACT.Square, scale=P ** -0.5)\
                        .then_inc(sq_act, 1)
            act.wait_ge(pj_full, PJ[("diff_o", 4)][0] + 1)
            act.wait_ge(row_out[0], 16 * ROW_TOTAL[0])
            act.wait_ge(row_out[1], 16 * ROW_TOTAL[1])
            act.wait_ge(stored, 16 * (2 + TILES))
            act.dma_start(cmkrow, A["cache_mem_k"][0, 0].rearrange("(b p) h d -> p b (h d)", p=P)).then_inc(cmk_in, 16)
            act.dma_start(cmv, A["cache_mem_v"][0, 0].rearrange("(b p) h d -> p b (h d)", p=P)).then_inc(cmv_in, 16)
            mixd_out(TILES - 1)
            act.dma_start(gffn[:, :], A["norm_ffn_g"].to_broadcast([P, D])).then_inc(gffn_in, 16)
            for t in range(TILES - 2, TILES):
                x1_square(t)

            def mq_out(t):
                if t >= 2:
                    act.wait_ge(tr_full, TR[("mq", t - 2)][0] + 1)
                act.wait_ge(rs_ready, RS[("x1", t)] + 1)
                pj_out(("mem_q", t), rowbuf[0:ROWS[t], t % 2, :], rs[0:ROWS[t], 2, t:t + 1]).then_inc(pj_act, 1)

            def exps_m(t):
                act.wait_ge(maxm_ready, t + 1)
                r = ROWS[t]
                for h in range(MH):
                    ins = act.activation(probm[0:r, t % 2, h, :], half(("mem", t))[0:r, MEM * h:MEM * h + MEM], ACT.Exp,
                                         bias=nmaxm[0:r, t % 2, h:h + 1], scale=P ** -0.5,
                                         accum_out=psumm[0:r, t % 2, h:h + 1])
                    if h == MH - 1:
                        ins.then_inc(sc_act, 1)
                    else:
                        steps[0] += 1
                        ins.then_inc(act_step, 1)

            def x2_square(t):
                pj_read(act, ("w_mem_o", 1, t))
                mean_square(("x2", t), x_tile(t), sq_scr)

            def h3_out_of(t):
                act.wait_ge(h3_ready, t + 1)
                act.dma_start(h3_rows[P * t:P * t + ROWS[t], :], h3[0:ROWS[t], t % 2, :]).then_inc(h3_out[t % 2], 16)
                tr_out(("x2", t, 0), hT[:, 0:4, cols(t)], heads_view(tr[1], 4, ROWS[t]))

            mq_out(0)
            exps_m(0)
            for t in range(TILES):
                if t + 1 < TILES:
                    mq_out(t + 1)
                tr_out(("pm", t, 0), pmT[:, t % 2, 0:4, 0:ROWS[t]], heads_view(tr[1], 4, ROWS[t]))
                act.wait_ge(pj_full, PJ[("mem_o", t)][0] + 1)
                act.activation(omT[:, :, cols(t)], heads_view(pj[PJ[("mem_o", t)][3]], 4, ROWS[t]), ACT.Copy)\
                    .then_inc(pj_act, 1)
                if t == 3:
                    for b in range(2):
                        tr_out(("cmk", b), cmkT[:, :, P * b:P * b + P], heads_view(tr[1], MH))
                if t + 1 < TILES:
                    exps_m(t + 1)
                if t >= 2:
                    h3_out_of(t - 2)
                if t:
                    x2_square(t - 1)
            split_hi(0, 0, -2)
            split_hi(0, 0, -1)
            x2_square(TILES - 1)
            h3_out_of(TILES - 2)
            split_hi(0, 0, 0)
            h3_out_of(TILES - 1)
            split_hi(0, 0, 1)
            for i, v in enumerate((r20[1], r5[3])):
                act.wait_ge(route_arg, i + 1)
                act.activation(v, v, ACT.Exp).then_inc(route_exp, 1)
            def x_hi(e, b):
                for g in range(2):
                    act.wait_ge(xt_done, 2 * e + (g + 1))
                    if not fixed(e, 2):
                        act.wait_ge(pe_unit, 6 * e - 8)
                    act.activation(xgh[:, b, 4 * g:4 * g + 4, :], px[g].rearrange("p (k q) -> p k q", k=4),
                                   ACT.Copy).then_inc(xh_done, 1)

            def silu(e, bank, units):
                act.wait_ge(pe_unit, units)
                if not fixed(e, 1):
                    act.wait_ge(h_done, e)
                act.activation(act_g[:, :], bank[:, :], ACT.Silu).then_inc(sg_done, 1)

            def hid_hi(e, b, units=None):
                act.wait_ge(ht_done, e + 1)
                if not fixed(e, 2):
                    act.wait_ge(pe_unit, 6 * e - 4)
                act.activation(hTh[:, b, :, :], ph[:, :].rearrange("p (k q) -> p k q", k=4), ACT.Copy)\
                    .then_inc(hh_done, 1)

            def y_evac(b, c, units, stores):
                act.wait_ge(pe_unit, units)
                if c == 0 and not fixed(stores, 1):
                    act.wait_ge(y_out[b], stores)
                act.activation(y[:, b, 512 * c:512 * c + 512], py[c], ACT.Copy).then_inc(y_done, 1)

            def step(e, b, last=False):
                first = fixed(e, 1)
                silu(e, pg[b], 2 if first else 6 * e)
                if not last:
                    x_hi(e + 1, 1 - b)
                if not first:
                    y_evac(1 - b, 1, 6 * e + 2, None)
                if last:
                    split_hi(e, b, 3)
                    hid_hi(e, b)
                    y_evac(b, 0, 6 * e + 5, 8 * e - 8 * b)
                    y_evac(b, 1, 6 * e + 6, None)
                    return
                for j in range(3, 9):
                    if j == 6:
                        hid_hi(e, b)
                    split_hi(e, b, j)
                y_evac(b, 0, 6 * e + 7, 8 * e - 8 * b)

            x_hi(0, 0)
            split_hi(0, 0, 2)
            for e in range(2):
                step(e, e)
            with act.Fori(1, E // 2 - 1) as i:
                for b in range(2):
                    step(2 * i + b, b)
            step(E - 2, 0)
            step(E - 1, 1, last=True)
            act.wait_ge(list_ready, 1)
            rounds = act.value_load(extra_i[0:1, MAX_EXTRA:MAX_EXTRA + 1], min_val=0, max_val=MAX_EXTRA)
            with act.If(rounds > 0):
                with act.Fori(0, rounds) as i:
                    r, units = i + E, 6 * i + NMOE
                    act.wait_ge(pe_unit, units)
                    x_hi(r, 0)
                    for k in range(6):
                        if k == 4:
                            silu(r, pg[0], units + 2)
                        act.wait_ge(unit_in[k], 16 * i + 16 * ((NDENSE + NMOE) // RING + 1))
                        if k >= WR:
                            act.wait_ge(pe_unit, units + (k - 3))
                        act.activation(wh[:, k % WR, :], raw[:, k, :], ACT.Copy).then_inc(hi_done, 1)
                    hid_hi(r, 0)
                    y_evac(0, 0, units + 5, 16 * i + 8 * E)
                    y_evac(0, 1, units + 6, None)
            def store_end(t):
                act.wait_ge(out_ready, t + 1)
                out = O[0][0, P * t:P * t + P, :] if t < 4 else O[1][0]
                act.dma_start(out, outb[0:ROWS[t], t % 2, :]).then_inc(out_stored[t % 2], 16)

            for t in range(TILES):
                act.wait_ge(sum_done, t + 1)
                mean_square(("end", t), x_tile(t), junk_end)
                if t:
                    store_end(t - 1)
            store_end(TILES - 1)
            act.wait_ge(stored, 16 * (2 + TILES))
            act.wait_ge(out_stored[0], 16 * 3)
            act.wait_ge(out_stored[1], 16 * 2)

        @block.vector
        def _(dve):
            steps = [0]

            def link(ins):
                steps[0] += 1
                ins.then_inc(dve_step, 1)
                dve.wait_ge(dve_step, steps[0])

            def tt(out, a, b, op):
                return dve.tensor_tensor(out, a, b, op)

            def tr_wait(key):
                dve.wait_ge(tr_full, TR[key][0] + 1)

            def split_lo(e, b, j):
                s4, s6 = (2 + 6 * b + j) % WR, (2 + j) % RING
                dve.wait_ge(hi_done, 6 * e + (3 + j))
                tt(wl[:, s4, :], raw[:, s6, :], wh[:, s4, :].bitcast(F32), ALU.subtract).then_inc(lo_done, 1)

            def gained(key, dst, gain):
                tr_wait(key)
                src = tr[0][:, :].rearrange("p (k q) -> p k q", k=4)[:, :, 0:dst.shape[2]]
                tt(dst, src, gain.unsqueeze(2).to_broadcast([P, 4, dst.shape[2]]), ALU.mult).then_inc(tr_dve, 1)

            tr_wait(("params",))
            dve.tensor_copy(gcol[:, :], tr[0][:, 0:27]).then_inc(tr_dve, 1)
            tr_read(dve, ("params",))
            for i in range(2):
                for g in range(2):
                    gained(("mem", i, g), memT[:, 4 * g:4 * g + 4, P * i:P * i + P], gains[:, 1, 4 * g:4 * g + 4])
            for t in range(TILES):
                for g in range(2):
                    gained(("x", t, g), hT[:, 4 * g:4 * g + 4, cols(t)], gains[:, 0, 4 * g:4 * g + 4])

            dve.wait_ge(params_in, 16 * NPARAMS)
            link(tt(lamv[:, 0, :], lamv[:, 0, :], lamv[:, 1, :], ALU.mult))
            link(tt(lamv[:, 2, :], lamv[:, 2, :], lamv[:, 3, :], ALU.mult))
            link(dve.tensor_reduce(lams[:, 0:1], lamv[:, 0, :], AX.X, ALU.add))
            dve.tensor_reduce(lams[:, 1:2], lamv[:, 2, :], AX.X, ALU.add).then_inc(lam_sum, 1)
            link(dve.tensor_scalar(gdiff[:, :], gdiff[:, :], 1.0 - LAM_INIT, None, ALU.mult))
            dve.wait_ge(consts, 14)
            for g in range(4):
                rows, b, w = slice(64 * (g % 2), 64 * (g % 2) + 64), g // 2, float(POOL_WINDOWS[g])
                link(dve.tensor_scalar(ramp[rows, b, :], eidx[rows, :], 1.0, w, ALU.add, ALU.min))
                link(dve.reciprocal(ramp[rows, b, :], ramp[rows, b, :]))
                ins = dve.tensor_scalar(ramp[rows, b, :], ramp[rows, b, :], w, None, ALU.mult)
                if g < 3:
                    link(ins)
                else:
                    ins.then_inc(ramp_ready, 1)

            for t in range(TILES):
                tr_wait(("G", t))
                link(dve.tensor_scalar(gq[:, cols(t)], tr[0][:, 0:ROWS[t]], GK ** -0.5, None, ALU.mult))
                dve.tensor_copy(gk[:, cols(t)], tr[0][:, P:P + ROWS[t]]).then_inc(tr_dve, 1)

            dve.wait_ge(sc_full, SC[("gate",)][0] + 1)
            ins = dve.tensor_scalar(t1[:, :], half(("gate",))[:, 0:TOK], ba[:, 0:1], None, ALU.add)
            ins.then_inc(sc_dve, 1)
            dve.wait_ge(sc_dve, 1)
            dve.scalar_tensor_tensor(out=t2[:, :], in0=t1[:, :], scalar=-1.0, in1=t1[:, :], op0=ALU.mult,
                                     op1=ALU.min).then_inc(gate_arg, 1)
            dve.wait_ge(gate_arg, 1)
            link(dve.tensor_scalar(t1[:, :], t1[:, :], 0.0, None, ALU.min))
            dve.wait_ge(gate_log, 1)
            link(tt(t1[:, :], t1[:, :], t3[:, :], ALU.subtract))
            link(dve.tensor_scalar(t1[:, :], t1[:, :], 1.0 / 16, None, ALU.mult))
            dve.tensor_tensor_scan(cum[:, :], keep, t1[:, :], 0.0, ALU.mult, ALU.add).then_inc(cum_ready, 1)
            dve.wait_ge(cum_ready, 1)
            c3 = cum[:, :].rearrange("p (c n) -> p c n", n=CH)

            def chunks(ap):
                return ap.rearrange("p (c n) -> p c n", n=CH)

            mid = c3[:, :, CH // 2 - 1:CH // 2].to_broadcast([P, NCH, CH])
            last = c3[:, :, CH - 1:CH].to_broadcast([P, NCH, CH])
            link(tt(chunks(t1[:, :]), c3, mid, ALU.subtract))
            link(dve.tensor_scalar(t2[:, :], t1[:, :], -1.0, EXP_CLAMP, ALU.mult, ALU.min))
            dve.tensor_scalar(t1[:, :], t1[:, :], EXP_CLAMP, None, ALU.min).then_inc(decay_arg, 1)
            tt(chunks(t4[:, :]), last, c3, ALU.subtract).then_inc(decay_arg, 2)
            for i, (buf, by, n) in enumerate(((t3, gq, 2), (t1, gq, 3), (t2, gk, 4), (t4, gk, 5))):
                dve.wait_ge(decay_exp, n)
                tt(buf[:, :], buf[:, :], by[:, :], ALU.mult).then_inc(gla_in, 1)
            dve.wait_ge(lam_exp, 1)
            link(tt(lams[:, 4:5], lams[:, 3:4], lams[:, 2:3], ALU.subtract))
            link(dve.tensor_scalar(lams[:, 5:6], lams[:, 4:5], LAM_INIT, None, ALU.subtract))

            for g, ts in enumerate((slice(0, 4), slice(4, 5))):
                r = P if g == 0 else DEC
                tr_wait(("kend", g))
                dve.tensor_copy(kend[0:r, ts, :], tr[0][0:r, 0:P * (ts.stop - ts.start)].rearrange(
                    "p (t n) -> p t n", n=P)).then_inc(tr_dve, 1)
            dve.wait_ge(state_in, 16 * 8)
            for g in range(3):
                dve.wait_ge(sc_full, SC[("kv", g)][0] + 1)
                cs = range(4 * g, min(4 * g + 4, NCH))
                if g < 2:
                    src = half(("kv", g))[:, :].rearrange("p (o c n) -> p c o n", o=2, n=256)
                    dst = S[:, 1 + cs[0]:1 + cs[-1] + 1, :].rearrange("p (c o) n -> p c o n", o=2)
                    mask = own[:, :].unsqueeze(1).unsqueeze(1).to_broadcast([P, 2, 2, 256])
                else:
                    src, dst, mask = half(("kv", g))[:, 0:256], Ss[:, 1, :], own[:, :]
                tt(dst, src, mask, ALU.mult).then_inc(sc_dve, 1)
                dve.wait_ge(sc_dve, SC[("kv", g)][2] + 1)
            for c in range(NCH):
                old, new = (S[:, c, :], S[:, c + 1, :]) if c < NCH - 1 else (Ss[:, 0, :], Ss[:, 1, :])
                ins = dve.scalar_tensor_tensor(out=new, in0=old, scalar=dec_end[:, c:c + 1], in1=new, op0=ALU.mult,
                                               op1=ALU.add)
                if c < NCH - 1:
                    link(ins)
                else:
                    ins.then_inc(states_ready, 1)

            def mask_scores(t):
                r = ROWS[t]
                dve.wait_ge(sc_full, SC[("att", t)][0] + 1)
                if t >= 2:
                    dve.wait_ge(pj_full, PJ[("gla_o", t - 2)][0] + 1)
                src = half(("att", t))[0:r, 0:GH * r].rearrange("p (h q) -> p h q", h=GH)
                dst = attm[0:r, t % 2, :].rearrange("p (h q) -> p h q", h=GH)[:, :, 0:r]
                tt(dst, src, causal[0:r, 0:r].unsqueeze(1).to_broadcast([r, GH, r]), ALU.mult).then_inc(sc_dve, 1)

            def hv(ap):
                return ap.rearrange("p (h v) -> p h v", h=4)

            def head_squares(key, n, sq, width):
                rows, i, cs = stat_of(key)
                dve.wait_ge(sq_act, n + 1)
                dve.tensor_reduce(stat[rows, i, cs], hv(sq[0:ROWS[key[1]], 0:width]), AX.X, ALU.add).then_inc(ms_dve, 1)

            def head_norm(key, width, dst, gain_bc, ready, free_key):
                t, r, j = key[1], ROWS[key[1]], PJ[free_key][3]
                rows, i, cs = stat_of(key)
                dve.wait_ge(rs_ready, RS[key] + 1)
                if t >= 2:
                    dve.wait_ge(tr_full, TR[({"gla": "mix_g", "diff": "mix_d"}[key[0]], t - 2)][0] + 1)
                w = width // 4
                tt(hv(dst), hv(pj[j][0:r, 0:width]), rs[rows, i, cs].unsqueeze(2).to_broadcast([r, 4, w]),
                   ALU.mult).then_inc(pj_dve, 1)
                dve.wait_ge(pj_dve, PJ[free_key][2] + 1)
                tt(hv(dst), hv(dst), gain_bc, ALU.mult).then_inc(ready, 1)

            def q_by_head(t):
                r = ROWS[t]
                if t >= 2:
                    dve.wait_ge(sc_full, SC[("att", t - 2)][0] + 1)
                tt(q_heads[t % 2][:, 0:GH * r].rearrange("p (h q) -> p h q", h=GH),
                   t1[:, cols(t)].unsqueeze(1).to_broadcast([P, GH, r]),
                   own[:, :].rearrange("p (h v) -> p h v", h=GH)[:, :, 0:1].to_broadcast([P, GH, r]), ALU.mult)\
                    .then_inc(qb_ready, 1)

            dve.wait_ge(gla_in, 4)
            q_by_head(0)
            q_by_head(1)
            mask_scores(0)
            dve.wait_ge(glu_ready, TILES)
            for t in range(TILES):
                if t + 2 < TILES:
                    q_by_head(t + 2)
                if t + 1 < TILES:
                    mask_scores(t + 1)
                r = ROWS[t]
                head_squares(("gla", t), t, gla_sq, 256)
                head_norm(("gla", t), 256, mixg[0:r, t % 2, :],
                          zR[0:r, t, 0:256].rearrange("p (h v) -> p h v", h=GH), mixg_ready, ("gla_o", t))

            def row_max(s):
                t, h = STEPS[s]
                r = ROWS[t]
                dve.wait_ge(sc_full, SC[last_score(t, h)][0] + 1)
                link(dve.tensor_reduce(nmax[0:r, s % 2, :], maps(t, h, keys_of(t)), AX.X, ALU.max))
                dve.tensor_scalar(nmax[0:r, s % 2, :], nmax[0:r, s % 2, :], -DH ** -0.5, None, ALU.mult)\
                    .then_inc(max_ready, 1)

            def diff_norm(t):
                r = ROWS[t]
                head_norm(("diff", t), 512, mixd[0:r, t % 2, :],
                          gdiff[0:r, :].unsqueeze(1).to_broadcast([r, 4, P]), mixd_ready, ("diff_o", t))

            def add_rows(name, c, t, dst, src):
                j, r, h = PJ[(name, c, t)][3], ROWS[t], slice(512 * c, 512 * c + 512)
                dve.wait_ge(pj_full, PJ[(name, c, t)][0] + 1)
                tt(dst[0:r, t, h], pj[j][0:r, :], src[0:r, t, h], ALU.add).then_inc(pj_dve, 1)

            row_max(0)
            for s, (t, h) in enumerate(STEPS):
                r, nk, b = ROWS[t], keys_of(t), s % 2
                sc_read(dve, last_score(t, h))
                link(dve.reciprocal(recip[0:r, b, :], psum_[0:r, b, :]))
                link(tt(recip[0:r, b, 1:2], recip[0:r, b, 1:2], lams[0:r, 5:6], ALU.mult))
                link(dve.tensor_scalar(prob[0:r, b, 1, 0:nk], prob[0:r, b, 1, 0:nk], recip[0:r, b, 1:2], None, ALU.mult))
                dve.scalar_tensor_tensor(out=prob[0:r, b, 0, 0:nk], in0=prob[0:r, b, 0, 0:nk], scalar=recip[0:r, b, 0:1],
                                         in1=prob[0:r, b, 1, 0:nk], op0=ALU.mult, op1=ALU.add).then_inc(pd_ready, 1)
                if s + 1 < len(STEPS):
                    row_max(s + 1)
                if t and h == 2:
                    if t == 1:
                        dve.wait_ge(x_again, 32)
                    add_rows("w_out", 0, t - 1, xw, xw)
                if h == 0 and t:
                    diff_norm(t - 1)
                if h == HEADS - 1:
                    head_squares(("diff", t), TILES + t, diff_sq, 512)
                    if t:
                        add_rows("w_out", 1, t - 1, xw, xw)
            diff_norm(TILES - 1)
            for c in range(2):
                add_rows("w_out", c, TILES - 1, xw, xw)

            def x1_T(t):
                for g in range(2):
                    gained(("x1", t, g), hT[:, 4 * g:4 * g + 4, cols(t)], gains[:, 2, 4 * g:4 * g + 4])

            def q_T(t):
                tr_wait(("mq", t))
                dve.tensor_copy(qmT[:, t % 2, :, 0:ROWS[t]], tr[0][:, :].rearrange("p (h q) -> p h q", h=MH)[:, :, 0:ROWS[t]])\
                    .then_inc(tr_dve, 1)

            def max_m(t):
                r = ROWS[t]
                dve.wait_ge(sc_full, SC[("mem", t)][0] + 1)
                link(dve.tensor_reduce(nmaxm[0:r, t % 2, :], half(("mem", t))[0:r, :].rearrange("p (h k) -> p h k", h=MH),
                                       AX.X, ALU.max))
                dve.tensor_scalar(nmaxm[0:r, t % 2, :], nmaxm[0:r, t % 2, :], -P ** -0.5, None, ALU.mult)\
                    .then_inc(maxm_ready, 1)

            def moe_input(t):
                r = ROWS[t]
                if t >= 2:
                    dve.wait_ge(h3_out[t % 2], 16 * (t // 2))
                    dve.wait_ge(tr_full, TR[("x2", t - 2, 1)][0] + 1)
                dve.wait_ge(rs_ready, RS[("x2", t)] + 1)
                dve.scalar_tensor_tensor(out=h3[0:r, t % 2, :], in0=x_tile(t), scalar=rs[0:r, 3, t:t + 1],
                                         in1=gffn[0:r, :], op0=ALU.mult, op1=ALU.mult).then_inc(h3_ready, 1)

            def x2_T(t):
                tr_wait(("x2", t, 1))
                dve.tensor_copy(hT[:, 4:8, cols(t)], tr[0][:, :].rearrange("p (k q) -> p k q", k=4)[:, :, 0:ROWS[t]])\
                    .then_inc(tr_dve, 1)

            x1_T(0)
            x1_T(1)
            q_T(0)
            max_m(0)
            for t in range(TILES):
                r = ROWS[t]
                sc_read(dve, ("mem", t))
                link(dve.reciprocal(nrec[0:r, t % 2, :], psumm[0:r, t % 2, :]))
                tt(probm[0:r, t % 2, :, :], probm[0:r, t % 2, :, :],
                   nrec[0:r, t % 2, :].unsqueeze(2).to_broadcast([r, MH, MEM]), ALU.mult).then_inc(pm_ready, 1)
                tr_wait(("pm", t, 1))
                dve.tensor_copy(pmT[:, t % 2, 4:8, 0:r], tr[0][:, :].rearrange("p (h q) -> p h q", h=4)[:, :, 0:r])\
                    .then_inc(tr_dve, 1)
                if t + 1 < TILES:
                    q_T(t + 1)
                if t + 2 < TILES:
                    x1_T(t + 2)
                if t + 1 < TILES:
                    max_m(t + 1)
                if t == 2:
                    dve.wait_ge(gffn_in, 16)
                if t >= 2:
                    moe_input(t - 2)
                if t:
                    for c in range(2):
                        add_rows("w_mem_o", c, t - 1, X, xw)
                if t >= 2:
                    x2_T(t - 2)
            moe_input(TILES - 2)
            for c in range(2):
                split_lo(0, 0, c - 2)
                add_rows("w_mem_o", c, TILES - 1, X, xw)
            x2_T(TILES - 2)
            split_lo(0, 0, 0)
            moe_input(TILES - 1)
            x2_T(TILES - 1)

            dve.wait_ge(pj_full, PJ[("router",)][0] + 1)
            link(dve.memset(lg, 0.0))
            jb = pj[PJ[("router",)][3]]
            link(tt(lg[:, 0:4, :], jb[:, 0:80].rearrange("p (t n) -> p t n", t=4),
                    br[:, :].unsqueeze(1).to_broadcast([P, 4, 20]), ALU.add))
            tt(lg[0:DEC, 4, :], jb[0:DEC, 80:100], br[0:DEC, :], ALU.add).then_inc(pj_dve, 1)
            dve.wait_ge(pj_dve, PJ[("router",)][2] + 1)

            def bc(ap, n):
                return ap.unsqueeze(len(ap.shape)).to_broadcast(list(ap.shape) + [n])

            first = eidx[:, 0:4]

            def first_max(v, m, hot):
                link(dve.tensor_reduce(m, v, AX.X, ALU.max))
                link(tt(hot, v, bc(m, 4), ALU.is_equal))
                link(tt(hot, hot, rank4[:, :].unsqueeze(1).to_broadcast([P, TILES, 4]), ALU.mult))
                link(dve.tensor_reduce(r5[4], hot, AX.X, ALU.max))
                link(tt(hot, hot, bc(r5[4], 4), ALU.is_equal))

            link(dve.tensor_scalar(rank4, first, -1.0, 4.0, ALU.mult, ALU.add))
            first_max(lg[:, :, 0:4], r5[0], r20[0])
            tt(r20[1], lg[:, :, 0:4], bc(r5[0], 4), ALU.subtract).then_inc(route_arg, 1)
            link(tt(r80[0].rearrange("p t (g i) -> p t g i", g=4), lg[:, :, 4:20].rearrange("p t (g i) -> p t g i", g=4),
                    bc(r20[0], 4), ALU.mult))
            link(dve.tensor_reduce(r20[2], r80[0].rearrange("p t (g i) -> p t i g", g=4), AX.X, ALU.add))
            first_max(r20[2], r5[1], r20[3])
            link(dve.scalar_tensor_tensor(out=r20[4], in0=r20[3], scalar=-1e30, in1=r20[2], op0=ALU.mult, op1=ALU.add))
            first_max(r20[4], r5[2], r20[5])
            tt(r5[3], r5[2], r5[1], ALU.subtract).then_inc(route_arg, 1)
            for i, hot in ((1, r20[3]), (2, r20[5])):
                for g in range(4):
                    ins = tt(r80[i][:, :, 4 * g:4 * g + 4], hot, bc(r20[0][:, :, g], 4), ALU.mult)
                link(ins)
            link(tt(chosen[:, :, :], r80[1], r80[2], ALU.add))
            dve.memset(chosen[DEC:P, 4, :], 0.0).then_inc(chosen_ready, 1)
            for i in range(2):
                link(tt(held[:, i], r80[i + 1].unsqueeze(2).to_broadcast([P, TILES, 2, E]),
                        bc(entry[:, i], E), ALU.mult))
            dve.wait_ge(pj_full, PJ[("pos",)][0] + 1)
            dve.tensor_copy(posc, pj[PJ[("pos",)][3]][:, 0:96]).then_inc(pj_dve, 1)
            dve.wait_ge(pj_dve, PJ[("pos",)][2] + 1)
            pos, cnt = posc[:, 0:80].rearrange("p (t e) -> p t e", e=E), posc[:, 80:96]
            for i in range(2):
                link(tt(r80[3], r80[i + 1], pos, ALU.mult))
                link(dve.tensor_reduce(posi[i], r80[3], AX.X, ALU.add))
                for t in range(TILES):
                    ins = dve.tensor_scalar(placed[:, i, t, :], lane[:, :], posi[i][:, t:t + 1], None, ALU.is_equal)
                ins.then_inc(place_ready, 1)
            dve.wait_ge(route_exp, 1)
            link(dve.tensor_reduce(r5[4], r20[1], AX.X, ALU.add))
            link(dve.reciprocal(r5[4], r5[4]))
            dve.wait_ge(route_exp, 2)
            link(dve.tensor_scalar(r5[5], r5[3], 1.0, None, ALU.add))
            link(dve.reciprocal(r5[5], r5[5]))
            link(tt(gate[:, 0, :], r5[4], r5[5], ALU.mult))
            link(tt(gate[:, 1, :], gate[:, 0, :], r5[3], ALU.mult))
            dve.wait_ge(pj_full, PJ[("entries",)][0] + 1)
            dve.tensor_scalar(idx_sb[:, :, :].rearrange("p e v -> p v e"),
                              pj[PJ[("entries",)][3]][:, 0:2 * E].rearrange("p (v e) -> p v e", v=2), float(EMPTY), None,
                              ALU.add).then_inc(pj_dve, 1)
            link(dve.tensor_scalar(more, cnt, float(P), None, ALU.is_gt))
            for q in range(2, 5):
                link(dve.scalar_tensor_tensor(out=more, in0=cnt, scalar=float(P * q), in1=more, op0=ALU.is_gt, op1=ALU.add))
            link(dve.memset(ones16, 1.0))
            link(dve.tensor_tensor_scan(upto, ones16, more, 0.0, ALU.mult, ALU.add))
            link(tt(base, upto, more, ALU.subtract))
            link(dve.tensor_scalar(base, base, float(P), -float(P + EMPTY), ALU.mult, ALU.add))
            link(tt(r80[3], pos, base.unsqueeze(1).to_broadcast([P, TILES, E]), ALU.add))
            link(dve.scalar_tensor_tensor(out=r80[0], in0=pos, scalar=P - 0.5, in1=r80[3], op0=ALU.is_gt, op1=ALU.mult))
            for i in (1, 2):
                link(tt(r80[i], r80[i], r80[0], ALU.mult))
                link(dve.tensor_reduce(r5[6], r80[i], AX.X, ALU.add))
                ins = dve.tensor_scalar(slot_i[:, i - 1, :], r5[6], float(EMPTY), None, ALU.add)
                if i == 1:
                    link(ins)
            ins.then_inc(slots_ready, 1)
            link(tt(r8x16, upto[0:1, :].unsqueeze(1).to_broadcast([1, MAX_EXTRA, E]),
                    eidx[0:1, 0:MAX_EXTRA].unsqueeze(2).to_broadcast([1, MAX_EXTRA, E]), ALU.is_le))
            link(dve.tensor_reduce(extra_f, r8x16, AX.X, ALU.add))
            link(dve.tensor_copy(extra_i[:, 0:MAX_EXTRA], extra_f))
            dve.tensor_copy(extra_i[:, MAX_EXTRA:MAX_EXTRA + 1], upto[0:1, E - 1:E]).then_inc(list_ready, 1)
            def x_lo(e, b):
                for g in range(2):
                    dve.wait_ge(xh_done, 2 * e + (g + 1))
                    tt(xgl[:, b, 4 * g:4 * g + 4, :], px[g].rearrange("p (k q) -> p k q", k=4),
                       xgh[:, b, 4 * g:4 * g + 4, :].bitcast(F32), ALU.subtract).then_inc(xl_done, 1)

            def hidden(e, units):
                dve.wait_ge(sg_done, e + 1)
                dve.wait_ge(pe_unit, units)
                if not fixed(e, 1):
                    dve.wait_ge(ht_done, e)
                tt(hid[:, :], act_g[:, :], pu[:, :], ALU.mult).then_inc(h_done, 1)

            def hid_lo(e, b):
                dve.wait_ge(hh_done, e + 1)
                tt(hTl[:, b, :, :], ph[:, :].rearrange("p (k q) -> p k q", k=4),
                   hTh[:, b, :, :].bitcast(F32), ALU.subtract).then_inc(hl_done, 1)

            def step(e, b, last=False):
                if not last:
                    x_lo(e + 1, 1 - b)
                if last:
                    split_lo(e, b, 3)
                    hidden(e, 6 * e + 4)
                    hid_lo(e, b)
                    return
                for j in range(3, 9):
                    if j == 5:
                        hidden(e, 6 * e + 4)
                    if j == 6:
                        hid_lo(e, b)
                    split_lo(e, b, j)

            split_lo(0, 0, 1)
            x_lo(0, 0)
            split_lo(0, 0, 2)
            for e in range(2):
                step(e, e)
            with dve.Fori(1, E // 2 - 1) as i:
                for b in range(2):
                    step(2 * i + b, b)
            step(E - 2, 0)
            step(E - 1, 1, last=True)
            dve.wait_ge(list_ready, 1)
            rounds = dve.value_load(extra_i[0:1, MAX_EXTRA:MAX_EXTRA + 1], min_val=0, max_val=MAX_EXTRA)
            with dve.If(rounds > 0):
                with dve.Fori(0, rounds) as i:
                    r, units = i + E, 6 * i + NMOE
                    x_lo(r, 0)
                    for k in range(6):
                        if k == 4:
                            hidden(r, units + 4)
                        dve.wait_ge(hi_done, units + (k + 1))
                        tt(wl[:, k % WR, :], raw[:, k, :], wh[:, k % WR, :].bitcast(F32), ALU.subtract).then_inc(lo_done, 1)
                    hid_lo(r, 0)
            for t in range(TILES + 1):
                if t < TILES:
                    r = ROWS[t]
                    dve.wait_ge(yg_in[t], 16)
                    link(dve.scalar_tensor_tensor(out=x_tile(t), in0=yg[0:r, t, 0, :], scalar=gate[0:r, 0, t:t + 1],
                                                  in1=x_tile(t), op0=ALU.mult, op1=ALU.add))
                    dve.scalar_tensor_tensor(out=x_tile(t), in0=yg[0:r, t, 1, :], scalar=gate[0:r, 1, t:t + 1],
                                             in1=x_tile(t), op0=ALU.mult, op1=ALU.add).then_inc(sum_done, 1)
                if t:
                    u, r = t - 1, ROWS[t - 1]
                    dve.wait_ge(rs_ready, RS[("end", u)] + 1)
                    dve.wait_ge(gfin_in, 16)
                    if u >= 2:
                        dve.wait_ge(out_stored[u % 2], 16 * (u // 2))
                    dve.scalar_tensor_tensor(out=outb[0:r, u % 2, :], in0=x_tile(u), scalar=rs[0:r, 4, u:u + 1],
                                             in1=gfin[0:r, :], op0=ALU.mult, op1=ALU.mult).then_inc(out_ready, 1)

        @block.tensor
        def _(pe):
            def claim(kind, numbers, keys, key, act_sem, dve_sem):
                n = numbers[key][0]
                place = 1 if kind == "tr" else 3
                for k in [k for k in keys[:n] if numbers[k][place] == numbers[key][place]][-1:]:
                    read_out(pe, numbers, act_sem, dve_sem, k)
                return numbers[key][3]

            def mm(out, lhsT, rhs, start, stop):
                return pe.matmul(out, lhsT, rhs, start=start, stop=stop, skip_group_check=True)

            def transposes(key, blocks):
                claim("tr", TR, TR_KEYS, key, tr_act, tr_dve)
                bank = tr[0] if TR[key][1] == "V" else tr[1]
                for c0, src in blocks:
                    r, n = src.shape
                    ins = pe.transpose(bank[0:n, c0:c0 + r], src, ident[0:r, 0:r])
                ins.then_inc(tr_full, 1)

            def unit_ready(n):
                pe.wait_ge(unit_in[n % RING], 16 * (n // RING + 1))

            def unit(n, w):
                return raw[:, n % RING, 0:4 * w].rearrange("p (k w) -> p k w", k=4)

            def project(key, lhs, units, w, r, part=None):
                nk, j = 4 * len(units), PJ[key][3]
                if part != 1:
                    claim("pj", PJ, PJ_KEYS, key, pj_act, pj_dve)
                    for n in units:
                        unit_ready(n)
                for k in range(nk) if part is None else range(part * nk // 2, (part + 1) * nk // 2):
                    ins = mm(pj[j][0:r, 0:w], lhs(k), unit(units[k // 4], w)[:, k % 4, :], k == 0, k == nk - 1)
                if part != 0:
                    ins.then_inc(pj_full, 1)

            def h_block(t):
                return lambda k: hT[:, k, cols(t)]

            pe.wait_ge(consts, 1)
            pe.wait_ge(gains_in, 16 * 5)
            transposes(("params",), [(0, grow[:, :])])
            pe.wait_ge(mem_in, 16)
            for i in range(2):
                for g in range(2):
                    transposes(("mem", i, g), [(P * k, memsrc[:, i, P * (4 * g + k):P * (4 * g + k) + P]) for k in range(4)])
            for n, b in enumerate(("memk", "memv")):
                for i in range(2):
                    tr_read(pe, ("mem", i, 1))
                    project((b, i), lambda k: memT[:, k, P * i:P * i + P], (2 * n, 2 * n + 1), 512, P)
            for i in range(2):
                pj_read(pe, ("memk", i))
                transposes(("mk", i), [(P * h, rowbuf[:, i, P * h:P * h + P]) for h in range(MH)])
            for t in range(TILES):
                pe.wait_ge(x_in[t], 16)
                for g in range(2):
                    transposes(("x", t, g), [(P * k, x_tile(t)[:, P * (4 * g + k):P * (4 * g + k) + P]) for k in range(4)])

            def rows_T(b, t, nb):
                pj_read(pe, (b, t))
                n = ROW_AT[(b, t)]
                transposes((b, t), [(P * k, rowbuf[0:ROWS[t], n % 2, P * k:P * k + P]) for k in range(nb)])

            def in_block(b, nb):
                for t in range(TILES):
                    tr_read(pe, ("x", t, 1))
                    project((b, t), h_block(t), BLOCK_UNITS[b], WIDTH[b], ROWS[t])
                    if t and nb:
                        rows_T(b, t - 1, nb)
                if nb:
                    rows_T(b, TILES - 1, nb)

            in_block("G", 2)
            in_block("R", 0)
            pj_read(pe, ("R", 4))
            transposes(("R", 0), [(P * t, zR[:, t, 256:272]) for t in range(4)])
            transposes(("R", 1), [(0, zR[0:DEC, 4, 256:272])])
            tr_read(pe, ("R", 1))
            claim("sc", SC, SC_KEYS, ("gate",), sc_act, sc_dve)
            mm(half(("gate",))[:, 0:512], wa2[:, :], gaT[:, 0:512], True, True)
            mm(half(("gate",))[:, 512:TOK], wa2[:, :], gaT[:, 512:TOK], True, True).then_inc(sc_full, 1)
            in_block("U", 2)
            pe.wait_ge(hist_in, 16)
            transposes(("hist",), [(P * b, hist[:, P * b:P * b + P]) for b in range(2)])
            in_block("K", 4)
            in_block("V", 0)
            pe.wait_ge(gla_in, 4)
            for g, ts in enumerate((range(4), range(4, 5))):
                transposes(("kend", g), [(P * (t - ts[0]), t4[:, cols(t)]) for t in ts])
            for g in range(3):
                claim("sc", SC, SC_KEYS, ("kv", g), sc_act, sc_dve)
                if g == 0:
                    tr_read(pe, ("kend", 1))
                for c in range(4 * g, min(4 * g + 4, NCH)):
                    rows = slice(CH * (c % 2), CH * (c % 2) + CH)
                    place = 512 * (c % 2) + 256 * (c % 4 // 2)
                    ins = mm(half(("kv", g))[:, place:place + 256], kend[rows, c // 2, :],
                             gv[rows, c // 2, :], True, True)
                ins.then_inc(sc_full, 1)

            def query(t):
                tr_read(pe, ("x", t, 1))
                project(("Q", t), h_block(t), BLOCK_UNITS["Q"], WIDTH["Q"], ROWS[t])

            def gla_scores(t):
                r = ROWS[t]
                claim("sc", SC, SC_KEYS, ("att", t), sc_act, sc_dve)
                pe.wait_ge(qb_ready, t + 1)
                mm(half(("att", t))[0:r, 0:GH * r], t2[:, cols(t)], q_heads[t % 2][:, 0:GH * r], True, True)\
                    .then_inc(sc_full, 1)

            def gla_out(t):
                r, j = ROWS[t], claim("pj", PJ, PJ_KEYS, ("gla_o", t), pj_act, pj_dve)
                for u in range(r // CH):
                    c = 2 * t + u
                    state = S[:, c, :] if t < 4 else Ss[:, 0, :]
                    mm(pj[j][CH * u:CH * u + CH, 0:256], t3[:, CH * c:CH * c + CH], state, True, False)
                read_out(pe, SC, sc_act, sc_dve, ("att", t))
                for h in range(GH):
                    ins = mm(pj[j][0:r, GV * h:GV * h + GV], attm[0:r, t % 2, P * h:P * h + r],
                             gv[0:r, t, GV * h:GV * h + GV], False, h == GH - 1)
                ins.then_inc(pj_full, 1)

            def mixg_T(t):
                pe.wait_ge(mixg_ready, t + 1)
                transposes(("mix_g", t), [(P * b, mixg[0:ROWS[t], t % 2, P * b:P * b + P]) for b in range(2)])

            query(0)
            query(1)
            rows_T("Q", 0, 4)
            gla_scores(0)
            pe.wait_ge(states_ready, 1)
            for t in range(TILES):
                if t + 1 < TILES:
                    gla_scores(t + 1)
                gla_out(t)
                if t + 2 < TILES:
                    query(t + 2)
                if t + 1 < TILES:
                    rows_T("Q", t + 1, 4)
                if t:
                    mixg_T(t - 1)
            mixg_T(TILES - 1)
            tr_read(pe, ("K", 4))
            tr_read(pe, ("Q", 4))
            pj_read(pe, ("V", 4))

            def diff_scores(s):
                t, h = STEPS[s]
                r, nk = ROWS[t], keys_of(t)
                for m in (0, 1) if t < 4 else (1, 0):
                    ms, q = slice(DH * m, DH * m + DH), qT[DH * m:DH * m + DH, h, cols(t)]
                    if t < 4:
                        key = ("diff", t, h)
                        if m == 0:
                            claim("sc", SC, SC_KEYS, key, sc_act, sc_dve)
                        out = half(key)[:, 512 * m:512 * m + 512]
                        mm(out[:, 0:nk], q, kT[ms, h, 0:nk], True, False)
                        ins = mm(out[:, nk - CH:nk], hide_q[DH * m:DH * m + 1, :], hide_k[DH * m:DH * m + 1, :], False, True)
                        if m == 1:
                            ins.then_inc(sc_full, 1)
                    else:
                        tr_read(pe, ("kp", 3))
                        claim("sc", SC, SC_KEYS, ("diff", t, h, m), sc_act, sc_dve)
                        mm(sc[0:r, 1024 * m:1024 * m + PAST], q, kpT[ms, h, :], True, True)
                        mm(sc[0:r, 1024 * m + PAST:1024 * m + nk], q, kT[ms, h, SEQ:TOK], True, True).then_inc(sc_full, 1)

            def mixd_T(t):
                pe.wait_ge(mixd_ready, t + 1)
                transposes(("mix_d", t), [(P * b, mixd[0:ROWS[t], t % 2, P * b:P * b + P]) for b in range(4)])

            def w_out(c, t, part=None):
                tr_read(pe, ("mix_d", t))
                if t == 0 and c == 0 and part != 1:
                    tr_read(pe, ("mix_g", 4))
                    pj_read(pe, ("pool_s", 1))
                project(("w_out", c, t), lambda k: mixT[:, k, cols(t)], (WO_UNIT + 2 * c, WO_UNIT + 2 * c + 1), 512,
                        ROWS[t], part)

            pe.wait_ge(consts, 11)
            diff_scores(0)
            for s, (t, h) in enumerate(STEPS):
                r, nb, b = ROWS[t], key_blocks(t), s % 2
                if s + 1 < len(STEPS):
                    diff_scores(s + 1)
                pe.wait_ge(pd_ready, s + 1)
                transposes(("pd", t, h, 0), [(P * k, prob[0:r, b, 0, P * k:P * k + P]) for k in range(min(nb, 4))])
                if t == 4:
                    transposes(("pd", t, h, 1), [(0, prob[0:r, b, 0, PAST:PAST + DEC])])
                if h == 1 and t:
                    mixd_T(t - 1)
                if h == 0:
                    j = claim("pj", PJ, PJ_KEYS, ("diff_o", t), pj_act, pj_dve)
                tr_read(pe, ("pd", t, h, 0))
                if t == 4:
                    tr_read(pe, ("pd", t, h, 1))
                    pe.wait_ge(vp_in, 16)
                hs = slice(DV * h, DV * h + DV)
                for k in range(nb):
                    if t < 4:
                        ins = mm(pj[j][0:r, hs], pdT[:, b, k, 0:r], vrow[:, k, hs], k == 0, k == nb - 1)
                    elif k < 4:
                        ins = mm(pj[j][0:r, hs], pdT[:, b, k, 0:r], vp[:, k, hs], k == 0, False)
                    else:
                        ins = mm(pj[j][0:r, hs], pdT[0:DEC, b, 4, 0:r], vrow[0:DEC, 4, hs], False, True)
                if h == HEADS - 1:
                    ins.then_inc(pj_full, 1)
                if t == 0:
                    if h == 0:
                        pe.wait_ge(kp_in, 16)
                        pe.wait_ge(pool_ready, 4)
                        pe.wait_ge(state_in, 16 * 8)
                    transposes(("kp", h), [(P * k, kprow[:, h, P * k:P * k + P]) for k in range(HEADS)])
                    (_, b), (c0, w) = POOL_USES[h], ((16, SEQ), (S0, DEC))[h % 2]
                    i = claim("pj", PJ, PJ_KEYS, POOL_USES[h], pj_act, pj_dve)
                    mm(pj[i][:, 0:w], poolw[:, b, :], ext[:, b, c0:c0 + w], True, True).then_inc(pj_full, 1)
                if h == 1 and t:
                    w_out(0, t - 1)
                if h >= 2 and t:
                    w_out(1, t - 1, h - 2)
            mixd_T(TILES - 1)
            for c in range(2):
                w_out(c, TILES - 1)

            def x1_T(t):
                pj_read(pe, ("w_out", 1, t))
                for g in range(2):
                    transposes(("x1", t, g), [(P * k, xw_tile(t)[:, P * (4 * g + k):P * (4 * g + k) + P]) for k in range(4)])

            def mem_q(t):
                tr_read(pe, ("x1", t, 1))
                project(("mem_q", t), h_block(t), (MQ_UNIT, MQ_UNIT + 1), 512, ROWS[t])

            def mem_q_T(t):
                pj_read(pe, ("mem_q", t))
                transposes(("mq", t), [(P * h, rowbuf[0:ROWS[t], t % 2, P * h:P * h + P]) for h in range(MH)])

            def mem_scores(t):
                tr_read(pe, ("mq", t))
                claim("sc", SC, SC_KEYS, ("mem", t), sc_act, sc_dve)
                for h in range(MH):
                    ins = mm(half(("mem", t))[0:ROWS[t], MEM * h:MEM * h + MEM], qmT[:, t % 2, h, 0:ROWS[t]],
                             (mkT if t < 4 else cmkT)[:, h, :], True, True)
                ins.then_inc(sc_full, 1)

            def w_mem_o(t):
                for c in range(2):
                    pj_read(pe, ("mem_o", t))
                    project(("w_mem_o", c, t), lambda k: omT[:, k, cols(t)], (MO_UNIT + c,), 512, ROWS[t])

            def x2_T(t):
                pe.wait_ge(h3_ready, t + 1)
                for g in range(2):
                    transposes(("x2", t, g), [(P * k, h3[0:ROWS[t], t % 2, P * (4 * g + k):P * (4 * g + k) + P]) for k in range(4)])

            x1_T(0)
            x1_T(1)
            mem_q(0)
            mem_q_T(0)
            mem_scores(0)
            for t in range(TILES):
                r = ROWS[t]
                if t + 1 < TILES:
                    mem_q(t + 1)
                pe.wait_ge(pm_ready, t + 1)
                for g in range(2):
                    transposes(("pm", t, g), [(P * (2 * hh + k), probm[0:r, t % 2, 2 * g + hh, P * k:P * k + P])
                                              for hh in range(2) for k in range(2)])
                if t + 1 < TILES:
                    mem_q_T(t + 1)
                j = claim("pj", PJ, PJ_KEYS, ("mem_o", t), pj_act, pj_dve)
                for g in range(2):
                    tr_read(pe, ("pm", t, g))
                if t == 4:
                    pe.wait_ge(cmv_in, 16)
                for h in range(MH):
                    for k in range(2):
                        ins = mm(pj[j][:, P * h:P * h + r], (mv if t < 4 else cmv)[:, k, P * h:P * h + P],
                                 pmT[:, t % 2, 2 * h + k, 0:r], k == 0, k == 1)
                ins.then_inc(pj_full, 1)
                if t + 2 < TILES:
                    x1_T(t + 2)
                if t == 3:
                    pe.wait_ge(cmk_in, 16)
                    for b in range(2):
                        transposes(("cmk", b), [(P * h, cmkrow[:, b, P * h:P * h + P]) for h in range(MH)])
                    tr_read(pe, ("cmk", 1))
                if t + 1 < TILES:
                    mem_scores(t + 1)
                if t:
                    w_mem_o(t - 1)
                if t >= 2:
                    x2_T(t - 2)
            w_mem_o(TILES - 1)
            x2_T(TILES - 2)
            j = claim("pj", PJ, PJ_KEYS, ("router",), pj_act, pj_dve)
            for t in range(TILES):
                if t == TILES - 1:
                    x2_T(t)
                for g in range(2):
                    tr_read(pe, ("x2", t, g))
                for k in range(KB):
                    ins = mm(pj[j][0:ROWS[t], 20 * t:20 * t + 20], hT[:, k, cols(t)], wr[:, k, :], k == 0, k == KB - 1)
            ins.then_inc(pj_full, 1)
            pe.wait_ge(chosen_ready, 1)
            j = claim("pj", PJ, PJ_KEYS, ("pos",), pj_act, pj_dve)
            for t in range(TILES + 1):
                for i in range(min(t + 1, TILES)):
                    ins = mm(pj[j][:, E * t:E * t + E], (before if i == t else onesb)[:, :], chosen[:, i, :],
                             i == 0, i == min(t, TILES - 1))
            ins.then_inc(pj_full, 1)
            j = claim("pj", PJ, PJ_KEYS, ("entries",), pj_act, pj_dve)
            for i in range(2):
                pe.wait_ge(place_ready, i + 1)
                for t in range(TILES):
                    r = ROWS[t]
                    ins = mm(pj[j][:, 0:2 * E], placed[0:r, i, t, :], held[0:r, i, t].rearrange("p v e -> p (v e)"),
                             i == 0 and t == 0, i == 1 and t == TILES - 1)
            ins.then_inc(pj_full, 1)
            def x_turn(e, buf, landed):
                pe.wait_ge(xg_in[buf], landed)
                for g in range(2):
                    if not fixed(e, 1):
                        pe.wait_ge(xl_done, 2 * e + (g - 1))
                    for k in range(4):
                        ins = pe.transpose(px[g][:, P * k:P * k + P], xg[:, buf, P * (4 * g + k):P * (4 * g + k) + P],
                                           ident[:, :])
                    ins.then_inc(xt_done, 1)

            def split_mm(out, hi, lo, slot, start, stop):
                for k in range(4):
                    w = slice(512 * k, 512 * k + 512)
                    mm(out, hi[:, k, :], wh[:, slot, w], start and k == 0, False)
                    mm(out, hi[:, k, :], wl[:, slot, w], False, False)
                    ins = mm(out, lo[:, k, :], wh[:, slot, w], False, stop and k == 3)
                ins.then_inc(pe_unit, 1)

            def gate_or_up(bank, buf, part, slot, split):
                pe.wait_ge(lo_done, split)
                split_mm(bank[:, :], xgh[:, buf, 4 * part:4 * part + 4, :], xgl[:, buf, 4 * part:4 * part + 4, :], slot,
                         part == 0, part == 1)

            def hid_turn(e):
                pe.wait_ge(h_done, e + 1)
                if not fixed(e, 1):
                    pe.wait_ge(hl_done, e)
                for k in range(4):
                    ins = pe.transpose(ph[:, P * k:P * k + P], hid[:, P * k:P * k + P], ident[:, :])
                ins.then_inc(ht_done, 1)

            def down(e, c, buf, slot, split):
                if c == 0:
                    pe.wait_ge(hl_done, e + 1)
                if not fixed(e, 1):
                    pe.wait_ge(y_done, 2 * e + (c - 1))
                pe.wait_ge(lo_done, split)
                split_mm(py[c], hTh[:, buf, :, :], hTl[:, buf, :, :], slot, True, True)

            def step(e, b, last=False):
                s4 = lambda j: (2 + 6 * b + j) % WR
                first = fixed(e, 1)
                if not last:
                    x_turn(e + 1, 1 - b, 8 * e + (16 if b == 0 else 24))
                if not first:
                    pe.wait_ge(h_done, e)
                for part in range(2):
                    gate_or_up(pu, b, part, s4(part), 6 * e + (3 + part))
                if not last:
                    pe.wait_ge(xl_done, 2 * e + 4)
                    if not first:
                        pe.wait_ge(sg_done, e)
                    for part in range(2):
                        gate_or_up(pg[1 - b], 1 - b, part, s4(2 + part), 6 * e + (5 + part))
                        if part == 0:
                            hid_turn(e)
                else:
                    hid_turn(e)
                for c in range(2):
                    j = (2 if last else 4) + c
                    down(e, c, b, s4(j), 6 * e + (3 + j))

            x_turn(0, 0, 16)
            pe.wait_ge(xl_done, 2)
            pj_read(pe, ("entries",))
            for part in range(2):
                gate_or_up(pg[0], 0, part, part, part + 1)
            for e in range(2):
                step(e, e)
            with pe.Fori(1, E // 2 - 1) as i:
                for b in range(2):
                    step(2 * i + b, b)
            step(E - 2, 0)
            step(E - 1, 1, last=True)
            pe.wait_ge(list_ready, 1)
            rounds = pe.value_load(extra_i[0:1, MAX_EXTRA:MAX_EXTRA + 1], min_val=0, max_val=MAX_EXTRA)
            with pe.If(rounds > 0):
                with pe.Fori(0, rounds) as i:
                    r, u = i + E, 6 * i + NMOE
                    x_turn(r, 0, 16 * i + (8 * E + 16))
                    pe.wait_ge(xl_done, 2 * i + (2 * E + 2))
                    for j, bank in ((0, pg[0]), (2, pu)):
                        for part in range(2):
                            gate_or_up(bank, 0, part, (j + part) % WR, u + (j + part + 1))
                    hid_turn(r)
                    for c in range(2):
                        down(r, c, 0, (4 + c) % WR, u + (5 + c))


_INS = ['x_prompt', 'x_sample', 'mem_prompt', 'cache_diff_k', 'cache_diff_v', 'cache_mem_k', 'cache_mem_v',
        'state_gla', 'state_pool', 'norm_mix_g', 'w_in', 'w_gla_a2', 'b_gla_a', 'gla_norm_g', 'pool_w', 'pool_scale',
        'lambda_q1', 'lambda_k1', 'lambda_q2', 'lambda_k2', 'diff_norm_g', 'w_out', 'norm_mem_g', 'mem_norm_g',
        'w_mem_q', 'w_mem_kv', 'w_mem_o', 'norm_ffn_g', 'w_router_group', 'b_router_group',
        'w_router_expert', 'b_router_expert', 'w_exp_gate', 'w_exp_up', 'w_exp_down', 'final_norm_g']
_OUTS = [(1, SEQ, D), (1, DEC, D), (1, 1, SEQ, HEADS, 2 * DH), (1, 1, SEQ, HEADS, DV), (1, 1, MEM, MH, P),
         (1, 1, MEM, MH, P), (1, 1, GH, GK, GV), (1, 1, HIST, 256), (1, 1, DEC, HEADS, 2 * DH),
         (1, 1, DEC, HEADS, DV), (1, 1, GH, GK, GV), (1, 1, HIST, 256)]


def kernel(**inputs):
    import numpy as _np
    import concourse.bacc as _bacc
    from concourse.bass_utils import run_bass_kernel_spmd as _run

    nc = _bacc.Bacc("TRN2", target_bir_lowering=False, num_devices=1)
    arrays, ins = {}, {}
    for name in _INS:
        a = _np.ascontiguousarray(inputs[name])
        arrays[f"in_{name}"] = a
        ins[name] = nc.dram_tensor(f"in_{name}", a.shape, mybir.dt.from_np(a.dtype), kind="ExternalInput").ap()
    outs = [nc.dram_tensor(f"out_{i}", shape, F32, kind="ExternalOutput").ap() for i, shape in enumerate(_OUTS)]
    layer_program(nc, ins, outs)
    r = _run(nc, [arrays], core_ids=[0])
    return tuple(r.results[0][f"out_{i}"] for i in range(len(_OUTS)))
```
